# Optimizing a Trainium2 kernel written in Bass

```python
import math
import jax, jax.numpy as jnp
from jax import lax
import numpy as np

D_MODEL = 1024
BATCH = 1
SEQ = 1024
DEPTH = 1

HEAD_DIM = 128
ATTN_GROUPS = ((128, 1), (512, 4), (2048, 16))
N_GROUPS = 3
HEADS_PER_GROUP = 4
ATTN_QKV_W = N_GROUPS * HEADS_PER_GROUP * HEAD_DIM
ATTN_OUT = HEADS_PER_GROUP * HEAD_DIM
CONV_CH = 512
CONV_WIDTH = 31
N_MEM = 256
N_XHEADS = 4
XATTN_W = N_XHEADS * HEAD_DIM
N_BRANCH = 3
D_FF = 2816
FFN_CONV_WIDTH = 3
N_BUCKETS = 32
MAX_DISTANCE = 2048
N_REL_HEADS = N_GROUPS * HEADS_PER_GROUP
RMS_EPS = 1e-6
LN_EPS = 1e-5
N_IN = 3 * ATTN_QKV_W + 2 * CONV_CH + XATTN_W + N_BRANCH * D_MODEL
IN_SPLITS = (ATTN_QKV_W, 2 * ATTN_QKV_W, 3 * ATTN_QKV_W,
             3 * ATTN_QKV_W + CONV_CH, 3 * ATTN_QKV_W + 2 * CONV_CH,
             3 * ATTN_QKV_W + 2 * CONV_CH + XATTN_W)

kernel_name = "hybrid_gated_dilated_conformer_block"

def rms_norm(x, w, eps=RMS_EPS):
    xf = x.astype(jnp.float32)
    y = xf * lax.rsqrt(jnp.mean(xf * xf, axis=-1, keepdims=True) + eps)
    return (y * w.astype(jnp.float32)).astype(x.dtype)

def layer_norm(x, w, b, eps=LN_EPS):
    xf = x.astype(jnp.float32)
    mu = jnp.mean(xf, axis=-1, keepdims=True)
    xc = xf - mu
    y = xc * lax.rsqrt(jnp.mean(xc * xc, axis=-1, keepdims=True) + eps)
    return (y * w.astype(jnp.float32) + b.astype(jnp.float32)).astype(x.dtype)

def causal_depthwise_conv(x, w, b):
    K, C = w.shape
    y = lax.conv_general_dilated(
        x, w[:, None, :].astype(x.dtype), window_strides=(1,), padding=[(K - 1, 0)],
        dimension_numbers=("NWC", "WIO", "NWC"), feature_group_count=C)
    return y + b.astype(x.dtype)

def t5_bucket(dist):
    max_exact = N_BUCKETS // 2
    d = jnp.maximum(dist.astype(jnp.float32), 1.0)
    large = max_exact + (jnp.log(d / max_exact) / math.log(MAX_DISTANCE / max_exact)
                         * (N_BUCKETS - max_exact)).astype(jnp.int32)
    large = jnp.minimum(large, N_BUCKETS - 1)
    return jnp.where(dist < max_exact, dist, large)

def dilated_window_attention(q, k, v, bias_cols, window, dilation):
    B, S, H, Dh = q.shape
    n = window // dilation
    span = n * dilation
    s_pad = -(-S // span) * span
    nb = s_pad // span

    def to_blocks(a):
        a = jnp.pad(a, ((0, 0), (0, s_pad - S), (0, 0), (0, 0)))
        a = a.reshape(B, nb * n, dilation, H, Dh).transpose(0, 2, 1, 3, 4)
        return a.reshape(B, dilation, nb, n, H, Dh)

    def with_prev(a):
        prev = jnp.pad(a, ((0, 0), (0, 0), (1, 0), (0, 0), (0, 0), (0, 0)))[:, :, :-1]
        return jnp.concatenate([prev, a], axis=3)

    qb = to_blocks(q)
    kk = with_prev(to_blocks(k))
    vv = with_prev(to_blocks(v))

    qi = jnp.arange(n)[:, None]
    kj = jnp.arange(2 * n)[None, :]
    step = qi + n - kj
    band = (step >= 0) & (step <= n)
    not_before_start = (jnp.arange(nb)[:, None, None] > 0) | (kj[None] >= n)
    mask = band[None] & not_before_start
    bucket = t5_bucket(jnp.clip(step, 0, None) * dilation)
    bias = jnp.transpose(bias_cols[bucket].astype(jnp.float32), (2, 0, 1))

    scores = jnp.einsum("brnqhd,brnkhd->brnhqk", qb, kk).astype(jnp.float32) * (Dh ** -0.5) + bias
    scores = jnp.where(mask[:, None], scores, -jnp.inf)
    m = jnp.max(scores, axis=-1, keepdims=True)
    p = jnp.exp(scores - m)
    l = jnp.sum(p, axis=-1, keepdims=True)
    o = jnp.einsum("brnhqk,brnkhd->brnqhd", p.astype(v.dtype), vv).astype(jnp.float32)
    l_t = jnp.swapaxes(l[..., 0], 3, 4)
    lse_t = jnp.swapaxes((m + jnp.log(l))[..., 0], 3, 4)
    o = o / l_t[..., None]

    def from_blocks(a):
        a = a.reshape(B, dilation, nb * n, H, -1).transpose(0, 2, 1, 3, 4)
        return a.reshape(B, s_pad, H, -1)[:, :S]

    return from_blocks(o), from_blocks(lse_t[..., None])[..., 0]

def memory_cross_attention(zq, mem, mem_norm_w, w_mem_kv, xq_norm_w, xk_norm_w):
    B, S, _ = zq.shape
    mem_n = rms_norm(mem, mem_norm_w)
    kv = mem_n @ w_mem_kv
    mk, mv = jnp.split(kv, 2, axis=-1)
    mk = rms_norm(mk.reshape(B, -1, N_XHEADS, HEAD_DIM), xk_norm_w)
    mv = mv.reshape(B, -1, N_XHEADS, HEAD_DIM)
    q = rms_norm(zq.reshape(B, S, N_XHEADS, HEAD_DIM), xq_norm_w)
    s = jnp.einsum("bshd,bmhd->bhsm", q, mk).astype(jnp.float32) * (HEAD_DIM ** -0.5)
    p = jax.nn.softmax(s, axis=-1).astype(mv.dtype)
    o = jnp.einsum("bhsm,bmhd->bshd", p, mv)
    return o.reshape(B, S, XATTN_W)

def setup_inputs(seed: int = 0) -> dict:
    key = jax.random.key(seed)
    ks = iter(jax.random.split(key, 32))
    nrm = lambda shape, scale: scale * jax.random.normal(next(ks), shape, jnp.float32)
    L = DEPTH
    return {
        "x": nrm((BATCH, SEQ, D_MODEL), 1.0),
        "mem": nrm((BATCH, N_MEM, D_MODEL), 1.0),
        "rel_bias_table": nrm((N_BUCKETS, N_REL_HEADS), 0.2),
        "attn_norm_w": 1.0 + nrm((L, D_MODEL), 0.02),
        "w_in": nrm((L, D_MODEL, N_IN), D_MODEL ** -0.5),
        "b_gate": nrm((L, N_BRANCH * D_MODEL), 0.02),
        "q_norm_w": 1.0 + nrm((L, N_GROUPS, HEAD_DIM), 0.02),
        "k_norm_w": 1.0 + nrm((L, N_GROUPS, HEAD_DIM), 0.02),
        "w_attn_o": nrm((L, ATTN_OUT, D_MODEL), ATTN_OUT ** -0.5),
        "conv_dw_w": nrm((L, CONV_WIDTH, CONV_CH), CONV_WIDTH ** -0.5),
        "conv_dw_b": nrm((L, CONV_CH), 0.02),
        "conv_ln_w": 1.0 + nrm((L, CONV_CH), 0.02),
        "conv_ln_b": nrm((L, CONV_CH), 0.02),
        "w_conv_o": nrm((L, CONV_CH, D_MODEL), CONV_CH ** -0.5),
        "mem_norm_w": 1.0 + nrm((L, D_MODEL), 0.02),
        "w_mem_kv": nrm((L, D_MODEL, 2 * XATTN_W), D_MODEL ** -0.5),
        "xq_norm_w": 1.0 + nrm((L, HEAD_DIM), 0.02),
        "xk_norm_w": 1.0 + nrm((L, HEAD_DIM), 0.02),
        "w_cross_o": nrm((L, XATTN_W, D_MODEL), XATTN_W ** -0.5),
        "w_out": nrm((L, D_MODEL, D_MODEL), D_MODEL ** -0.5),
        "ffn_norm_w": 1.0 + nrm((L, D_MODEL), 0.02),
        "w_up": nrm((L, D_MODEL, 2 * D_FF), D_MODEL ** -0.5),
        "ffn_conv_w": nrm((L, FFN_CONV_WIDTH, 2 * D_FF), FFN_CONV_WIDTH ** -0.5),
        "ffn_conv_b": nrm((L, 2 * D_FF), 0.02),
        "w_down": nrm((L, D_FF, D_MODEL), D_FF ** -0.5),
    }

def reference(x, mem, rel_bias_table, attn_norm_w, w_in, b_gate, q_norm_w, k_norm_w, w_attn_o,
              conv_dw_w, conv_dw_b, conv_ln_w, conv_ln_b, w_conv_o, mem_norm_w, w_mem_kv,
              xq_norm_w, xk_norm_w, w_cross_o, w_out, ffn_norm_w, w_up, ffn_conv_w, ffn_conv_b,
              w_down):
    B, S, _ = x.shape
    h = x
    for l in range(DEPTH):
        xn = rms_norm(h, attn_norm_w[l])
        z = xn @ w_in[l]
        zq, zk, zv, zc_val, zc_gate, zx_q, zg = jnp.split(z, IN_SPLITS, axis=-1)

        q = rms_norm(zq.reshape(B, S, N_GROUPS, HEADS_PER_GROUP, HEAD_DIM), q_norm_w[l][:, None, :])
        k = rms_norm(zk.reshape(B, S, N_GROUPS, HEADS_PER_GROUP, HEAD_DIM), k_norm_w[l][:, None, :])
        v = zv.reshape(B, S, N_GROUPS, HEADS_PER_GROUP, HEAD_DIM)
        outs, lses = [], []
        for g, (win, dil) in enumerate(ATTN_GROUPS):
            cols = rel_bias_table[:, g * HEADS_PER_GROUP:(g + 1) * HEADS_PER_GROUP]
            o_g, lse_g = dilated_window_attention(q[:, :, g], k[:, :, g], v[:, :, g], cols, win, dil)
            outs.append(o_g)
            lses.append(lse_g)
        wts = jax.nn.softmax(jnp.stack(lses), axis=0)
        attn = jnp.sum(wts[..., None] * jnp.stack(outs), axis=0).astype(x.dtype)
        y_attn = attn.reshape(B, S, ATTN_OUT) @ w_attn_o[l]

        u = zc_val * jax.nn.sigmoid(zc_gate)
        u = causal_depthwise_conv(u, conv_dw_w[l], conv_dw_b[l])
        u = jax.nn.silu(layer_norm(u, conv_ln_w[l], conv_ln_b[l]))
        y_conv = u @ w_conv_o[l]

        y_cross = memory_cross_attention(zx_q, mem, mem_norm_w[l], w_mem_kv[l],
                                         xq_norm_w[l], xk_norm_w[l]) @ w_cross_o[l]

        gates = jax.nn.sigmoid((zg + b_gate[l]).astype(jnp.float32)).astype(x.dtype)
        gates = gates.reshape(B, S, N_BRANCH, D_MODEL)
        merged = gates[:, :, 0] * y_attn + gates[:, :, 1] * y_conv + gates[:, :, 2] * y_cross
        h = h + merged @ w_out[l]

        hn = rms_norm(h, ffn_norm_w[l])
        up = causal_depthwise_conv(hn @ w_up[l], ffn_conv_w[l], ffn_conv_b[l])
        a, gt = jnp.split(up, 2, axis=-1)
        h = h + (jax.nn.silu(gt) * a) @ w_down[l]
    return h


_drawn_inputs = setup_inputs


def setup_inputs(seed=0):
    import zlib

    import numpy as np

    out = dict(_drawn_inputs(seed))
    spreads = {}
    factors = {'rel_bias_table': 4.21,
     'attn_norm_w': 6.904,
     'b_gate': 8.0,
     'q_norm_w': 8.0,
     'k_norm_w': 8.0,
     'conv_dw_b': 22.068,
     'conv_ln_w': 33.485,
     'conv_ln_b': 35.491,
     'mem_norm_w': 8.0,
     'xq_norm_w': 8.0,
     'xk_norm_w': 8.0,
     'ffn_norm_w': 15.25,
     'ffn_conv_b': 15.006}
    for name, (base, spread) in spreads.items():
        noise = np.random.default_rng([zlib.crc32(name.encode()), seed]).standard_normal(out[name].shape)
        drawn = base * np.exp(spread * noise) if base else spread * noise
        out[name] = __import__('jax').numpy.asarray(drawn.astype(out[name].dtype))
    for name, factor in factors.items():
        out[name] = (out[name] * factor).astype(out[name].dtype)
    return out
```

```python
import math
from contextlib import ExitStack

import numpy as np

import concourse.bass as bass
from concourse import mybir

F32 = mybir.dt.float32
F32R = mybir.dt.float32r
ALU = mybir.AluOpType
ACT = mybir.ActivationFunctionType
AX = mybir.AxisListType

P = 128
S = 1024
D = 1024
NT = S // P
KT = D // P
CW = 512
HD = 128
NH = 4
NG = 3
DIL = (1, 4, 16)
STEPS = 128
SPACING = (1, 4, 8)
CONV_W = 31
CONV_CH = 512
FT = CONV_CH // P
N_MEM = 256
MT = N_MEM // P
D_FF = 2816
NU = D_FF // P
N_BUCKETS = 32
MAX_DISTANCE = 2048
RMS_EPS = 1e-6
LN_EPS = 1e-5
MASKED = -1e30
RING = 8
LINE = 384

V_ATTN_NORM = 0
V_MEM_NORM = V_ATTN_NORM + KT
V_FFN_NORM = V_MEM_NORM + KT
V_GATE_B = V_FFN_NORM + KT
V_QNORM = V_GATE_B + 3 * KT
V_KNORM = V_QNORM + NG
V_XQ = V_KNORM + NG
V_XK = V_XQ + 1
V_DW_B = V_XK + 1
V_LN_W = V_DW_B + FT
V_LN_B = V_LN_W + FT
ROWS_A = V_LN_B + FT
V_FB = ROWS_A
V_FW = V_FB + 2 * NU
V_DW = V_FW + 3 * 2 * NU
NV = V_DW + FT * CONV_W
assert ROWS_A + 2 * NU <= P and NV <= CW
V_QS = NV
NVECS = NV + NG + 1

SLOTS_GROUP = 3 * RING
BASE_ATT = 0
BASE_MEM = BASE_ATT + NG * SLOTS_GROUP
BASE_CROSS = BASE_MEM + 2 * RING
BASE_GLU = BASE_CROSS + RING
SLOTS_BRANCH = 3 * RING
BASE_BRANCH = BASE_GLU + 2 * RING
BASE_WOUT = BASE_BRANCH + 3 * SLOTS_BRANCH
BASE_UP = BASE_WOUT + 2 * RING
N_UP = NU // 2
BASE_DOWN = BASE_UP + N_UP * RING

COL_Q, COL_K, COL_V = 0, NG * CW, 2 * NG * CW
COL_VAL = 3 * NG * CW
COL_GLU = COL_VAL + CONV_CH
COL_XQ = COL_GLU + CONV_CH
COL_GATE = COL_XQ + CW


def bias_constants():
    onehot = np.zeros((N_BUCKETS + 1, NG * LINE), np.float32)
    exact = N_BUCKETS // 2
    for g in range(NG):
        for i in range(LINE):
            apart = 2 * STEPS - 1 - i
            d = apart * SPACING[g]
            if d < 0 or d > STEPS * DIL[g] or d % DIL[g]:
                row = N_BUCKETS
            else:
                large = exact + int(np.float32(math.log(max(d, 1) / exact) / math.log(MAX_DISTANCE / exact)
                                               * (N_BUCKETS - exact)))
                row = d if d < exact else min(large, N_BUCKETS - 1)
            onehot[row, g * LINE + i] = 1.0
    return onehot


def build(nc, x, mem, rel_bias_table, attn_norm_w, w_in, b_gate, q_norm_w, k_norm_w, w_attn_o, conv_dw_w,
          conv_dw_b, conv_ln_w, conv_ln_b, w_conv_o, mem_norm_w, w_mem_kv, xq_norm_w, xk_norm_w,
          w_cross_o, w_out, ffn_norm_w, w_up, ffn_conv_w, ffn_conv_b, w_down, identity, mirror,
          bias_onehot, out):
    x, out, mem = x[0], out[0], mem[0]
    w_in, w_mem_kv, w_out, w_up, w_down = w_in[0], w_mem_kv[0], w_out[0], w_up[0], w_down[0]
    w_branch_o = [w_cross_o[0], w_conv_o[0], w_attn_o[0]]

    ctx = ExitStack()
    with ctx:
        bottom = (nc.sbuf_base + 63) // 64 * 64

        def at(name, offset, shape, dt=F32):
            return nc.alloc_sbuf_tensor_at(name, [P] + shape, dt, offset=bottom + offset)

        slot_bytes = CW * 4
        stage = at("stage", 0, [RING, CW])
        whi = at("whi", RING * slot_bytes, [RING, CW], F32R)
        wlo = at("wlo", 2 * RING * slot_bytes, [RING, CW], F32R)
        ACTS = 3 * RING * slot_bytes
        act_hi = at("act_hi", ACTS, [KT, S], F32R)
        act_lo = at("act_lo", ACTS + KT * S * 4, [KT, S], F32R)
        SMALL = ACTS + 2 * KT * S * 4
        ident = at("ident", SMALL, [P])
        mirror_sb = at("mirror_sb", SMALL + 512, [P])
        vecs = at("vecs", SMALL + 1024, [NVECS])
        STATS = SMALL + 1024 + (NVECS * 4 + 63) // 64 * 64
        sumsq = at("sumsq", STATS, [NT])
        meansq = at("meansq", STATS + 32, [NT])
        rstd = at("rstd", STATS + 64, [2, NT])
        minus_half = at("minus_half", STATS + 128, [NT])
        softstat = at("softstat", STATS + 160, [4, 2, NH])
        recip_l = at("recip_l", STATS + 288, [2, NH])
        moments = at("moments", STATS + 320, [2, 8])
        combine_s = at("combine_s", STATS + 384, [6, NG, NH])
        FREE = STATS + 384 + 288 + 32

        psum = ctx.enter_context(nc.psum_tensor("psum", [P, 8, CW], F32))

        def banks(b, n=2):
            return psum[:, b:b + n, :].rearrange("p b c -> p (b c)")

        bias_lines = nc.dram_tensor("bias_lines", (NG, NH, LINE), F32).ap()
        group_out = [nc.dram_tensor(f"group_out{g}", (S, NH * HD + 2 * NH), F32).ap() for g in range(NG)]
        h_dram = nc.dram_tensor("h_scratch", (S, D), F32).ap()

        def sem(name):
            return ctx.enter_context(nc.semaphore(name))

        w_loaded = [sem(f"w_loaded{p}") for p in range(RING)]
        w_hi = sem("w_hi")
        w_lo = [sem("w_lo_even"), sem("w_lo_odd")]
        w_freed = sem("w_freed")

        def load_slot(sp, turn, pos, src, cols=None):
            if not (isinstance(turn, int) and turn == 0):
                sp.wait_ge(w_lo[pos % 2], 4 * (turn - 1) + pos // 2 + 1)
            dst = stage[:, pos, :]
            if cols:
                dst = dst.rearrange("p (h c) -> p h c", h=cols)
            sp.dma_start(dst, src).then_inc(w_loaded[pos], 16)

        def split_hi(act, turn, pos):
            act.wait_ge(w_loaded[pos], 16 * (turn + 1))
            if not (isinstance(turn, int) and turn == 0):
                act.wait_ge(w_freed, RING * (turn - 1) + pos + 1)
            nc.scalar.copy(whi[:, pos, :], stage[:, pos, :]).then_inc(w_hi, 1)

        def split_lo(eng, ops, turn, pos):
            eng.wait_ge(w_hi, RING * turn + pos + 1)
            ops.tensor_tensor(wlo[:, pos, :], stage[:, pos, :], whi[:, pos, :].bitcast(F32),
                              ALU.subtract).then_inc(w_lo[pos % 2], 1)

        def wait_slot(pe, turn, pos):
            pe.wait_ge(w_lo[pos % 2], 4 * turn + pos // 2 + 1)

        def splits_act(act, turn, n=RING):
            for pos in range(n):
                split_hi(act, turn, pos)

        def splits_dve(dve, turn, n=RING):
            for pos in range(1, n, 2):
                split_lo(dve, nc.vector, turn, pos)

        def splits_pool(pool, turn, n=RING):
            for pos in range(0, n, 2):
                split_lo(pool, nc.gpsimd, turn, pos)

        def piece(w, k, col):
            return w[k * P:(k + 1) * P, col:col + CW]

        sources = []
        for g in range(NG):
            for col in (COL_K, COL_V, COL_Q):
                sources.append([piece(w_in, k, col + g * CW) for k in range(KT)])
        for col in (0, CW):
            sources.append([piece(w_mem_kv, k, col) for k in range(KT)])
        for col in (COL_XQ, COL_GLU, COL_VAL):
            sources.append([piece(w_in, k, col) for k in range(KT)])
        for b, gate in enumerate((2, 1, 0)):
            pieces = []
            for j in range(2):
                pieces += [piece(w_in, k, COL_GATE + gate * D + j * CW) for k in range(KT)]
                pieces += [piece(w_branch_o[b], k, j * CW) for k in range(FT)]
            sources += [pieces[i * RING:(i + 1) * RING] for i in range(3)]
        for j in range(2):
            sources.append([piece(w_out, k, j * CW) for k in range(KT)])
        up_halves = w_up.rearrange("k (h c) -> k h c", h=2)
        sources.append([up_halves[k * P:(k + 1) * P, :, 0:CW // 2] for k in range(KT)])

        def load_turns(sp, first, last):
            for turn in range(first, last):
                for pos in range(RING):
                    load_slot(sp, turn, pos, sources[turn][pos], 2 if turn == BASE_UP // RING else None)

        def three(pe, dst, lhs, rhs, first, last, lead=0):
            nc.tensor.matmul(dst, lhs[1], rhs[0], start=first, stop=False, skip_group_check=True)
            nc.tensor.matmul(dst, lhs[0], rhs[1], start=False, stop=False, skip_group_check=True)
            return nc.tensor.matmul(dst, lhs[0], rhs[0], start=False, stop=last, skip_group_check=True)

        gemm_done = sem("gemm_done")
        gemm_freed = sem("gemm_freed")

        def token_gemm(pe, index, turn, lhs, first, last):
            if index >= 2:
                pe.wait_ge(gemm_freed, index - 1)
            for k in range(KT):
                if first:
                    wait_slot(pe, turn, k)
                mm = three(pe, psum[:, index % 2, :], lhs(k), (whi[:, k, :], wlo[:, k, :]), k == 0, k == KT - 1)
                if last:
                    mm.then_inc(w_freed, 1)
            if last:
                pe.wait_ge(w_freed, RING * (turn + 1))
                pe.sem_inc(gemm_done, 1)
            else:
                mm.then_inc(gemm_done, 1)

        def act_tile(tokens):
            return lambda k: (act_hi[:, k, tokens], act_lo[:, k, tokens])

        def group_tile(g, t):
            def pick(a, k):
                if g == 0:
                    return a[:, k, t * P:(t + 1) * P]
                if g == 1:
                    r, b = t // 2, t % 2
                    return a[:, k, r + b * 4 * P:r + (b + 1) * 4 * P - 3:4]
                return a[:, k, t:t + 8 * P - 7:8]
            return lambda k: (pick(act_hi, k), pick(act_lo, k))

        row_loaded = sem("row_loaded")
        row_ss = sem("row_ss")
        row_ms = sem("row_ms")
        row_rstd = sem("row_rstd")
        row_scaled = sem("row_scaled")
        row_tr = sem("row_tr")
        row_hi = sem("row_hi")
        row_lo = sem("row_lo")

        class Rows:
            def __init__(self, before, rows, junk, tiles, batch, wcol, hi, lo):
                self.rows, self.junk, self.tiles, self.batch, self.wcol = rows, junk, tiles, batch, wcol
                self.hi, self.lo = hi, lo
                self.tile0 = before.tile0 + before.tiles if before else 0
                self.batch0 = before.batch0 + before.tiles // before.batch if before else 0
                self.bank0 = before.bank0 + before.tiles // before.batch * KT if before else 0
                self.batches = range(tiles // batch)

        def rows_act_squares(act, r, ready):
            for t in range(r.tiles):
                ready(act, t)
                if t >= 1:
                    act.wait_ge(row_ss, r.tile0 + t)
                nc.scalar.activation(r.junk[:], r.rows[:, t, :], ACT.Square,
                                     accum_out=sumsq[:, t:t + 1]).then_inc(row_ss, 1)

        def rows_pool(pool, r):
            for b in r.batches:
                s = slice(b * r.batch, (b + 1) * r.batch)
                pool.wait_ge(row_ss, r.tile0 + (b + 1) * r.batch)
                nc.gpsimd.tensor_scalar(meansq[:, s], sumsq[:, s], 1.0 / D, RMS_EPS, ALU.mult,
                                        ALU.add).then_inc(row_ms, 1)
                pool.wait_ge(row_ms, r.batch0 + b + 1)
                nc.gpsimd.tensor_tensor(rstd[:, 0, s], meansq[:, s], minus_half[:, s], ALU.pow).then_inc(row_rstd, 1)

        def rows_dve_scale(dve, r):
            for t in range(r.tiles):
                if t % r.batch == 0:
                    dve.wait_ge(row_rstd, r.batch0 + t // r.batch + 1)
                nc.vector.tensor_scalar(r.rows[:, t, :], r.rows[:, t, :], rstd[:, 0, t:t + 1], None,
                                        ALU.mult).then_inc(row_scaled, 1)

        def rows_pe(pe, r):
            for b in r.batches:
                pe.wait_ge(row_scaled, r.tile0 + (b + 1) * r.batch)
                for k in range(KT):
                    n = r.bank0 + b * KT + k
                    if n >= 4:
                        pe.wait_ge(row_lo, n - 3)
                    for i in range(r.batch):
                        mm = nc.tensor.transpose(psum[:, 4 + n % 4, i * P:(i + 1) * P],
                                                 r.rows[:, b * r.batch + i, k * P:(k + 1) * P], ident[:])
                    mm.then_inc(row_tr, 1)

        def rows_evacuate(r):
            for b in r.batches:
                for k in range(KT):
                    n = r.bank0 + b * KT + k
                    w = vecs[:, r.wcol + k:r.wcol + k + 1]
                    cols = slice(b * r.batch * P, (b + 1) * r.batch * P)
                    yield n, w, psum[:, 4 + n % 4, 0:r.batch * P], r.hi[:, k, cols], r.lo[:, k, cols]

        def rows_act_hi(act, r):
            for n, w, src, hi, _ in rows_evacuate(r):
                act.wait_ge(row_tr, n + 1)
                nc.scalar.activation(hi, src, ACT.Copy, scale=w).then_inc(row_hi, 1)

        def rows_dve_lo(dve, r):
            for n, w, src, hi, lo in rows_evacuate(r):
                dve.wait_ge(row_hi, n + 1)
                nc.vector.scalar_tensor_tensor(lo, src, w, hi.bitcast(F32), ALU.mult,
                                               ALU.subtract).then_inc(row_lo, 1)

        x_rows = at("x_rows", FREE, [NT, D])
        x_junk = at("x_junk", FREE + 32768, [D])
        rows_a = at("rows_a", FREE + 36864, [P])
        rows_b = at("rows_b", FREE + 37376, [P])
        rows_c = at("rows_c", FREE + 37888, [P])
        dw_rows = at("dw_rows", FREE + 38400, [CONV_CH])
        table_aug = at("table_aug", FREE + 40448, [NG * NH])
        onehot_sb = at("onehot_sb", FREE + 40512, [NG * LINE])
        lines_sb = at("lines_sb", FREE + 40512 + NG * LINE * 4, [NG, LINE])

        xr = Rows(None, x_rows, x_junk, NT, NT // 2, V_ATTN_NORM, act_hi, act_lo)
        x_loaded = [sem(f"x_loaded{b}") for b in range(2)]
        params_loaded = sem("params_loaded")
        ident_loaded = sem("ident_loaded")
        masked_set = sem("masked_set")
        half_set = sem("half_set")
        params_tr = sem("params_tr")
        vecs_ready = sem("vecs_ready")
        lines_mm = sem("lines_mm")
        lines_copied = sem("lines_copied")
        lines_stored = sem("lines_stored")
        fw = ffn_conv_w[0].rearrange("w (f p) -> (w f) p", p=P)
        param_loads = [(identity, ident[:]), (mirror, mirror_sb[:])]
        row = 0
        for v, n in ((attn_norm_w, KT), (mem_norm_w, KT), (ffn_norm_w, KT), (b_gate, 3 * KT)):
            param_loads.append((v[0].rearrange("(r p) -> r p", p=P), rows_a[row:row + n, :]))
            row += n
        param_loads.append((q_norm_w[0], rows_a[row:row + NG, :]))
        param_loads.append((k_norm_w[0], rows_a[row + NG:row + 2 * NG, :]))
        row += 2 * NG
        param_loads.append((xq_norm_w, rows_a[row:row + 1, :]))
        param_loads.append((xk_norm_w, rows_a[row + 1:row + 2, :]))
        row += 2
        for v, n in ((conv_dw_b, FT), (conv_ln_w, FT), (conv_ln_b, FT), (ffn_conv_b, 2 * NU)):
            param_loads.append((v[0].rearrange("(r p) -> r p", p=P), rows_a[row:row + n, :]))
            row += n
        assert row == V_FW
        param_loads.append((fw[0:4 * NU, :], rows_b[0:4 * NU, :]))
        param_loads.append((fw[4 * NU:6 * NU, :], rows_c[0:2 * NU, :]))
        param_loads.append((conv_dw_w[0], dw_rows[0:CONV_W, :]))
        param_loads.append((rel_bias_table, table_aug[0:N_BUCKETS, :]))
        param_loads.append((bias_onehot, onehot_sb[0:N_BUCKETS + 1, :]))

        with nc.Block() as block:
            @block.sync
            def _(sp):
                for t in range(NT // 2):
                    sp.dma_start(x_rows[:, t, :], x[t * P:(t + 1) * P, :]).then_inc(x_loaded[0], 16)
                for t in range(NT // 2, NT):
                    sp.dma_start(x_rows[:, t, :], x[t * P:(t + 1) * P, :]).then_inc(x_loaded[1], 16)
                load_turns(sp, 0, 1)
                sp.wait_ge(lines_copied, NG)
                sp.dma_start(bias_lines.rearrange("g h i -> h g i"), lines_sb[0:NH, :, :]).then_inc(lines_stored, 16)
                sp.wait_ge(lines_stored, 16)

            @block.scalar
            def _(act):
                for src, dst in param_loads[:2]:
                    act.dma_start(dst, src).then_inc(ident_loaded, 16)
                for src, dst in param_loads[2:]:
                    act.dma_start(dst, src).then_inc(params_loaded, 16)
                rows_act_squares(act, xr, lambda e, t: e.wait_ge(x_loaded[t // 4], 16 * 4))
                act.wait_ge(vecs_ready, 1)
                rows_act_hi(act, xr)
                splits_act(act, 0)

            @block.gpsimd
            def _(pool):
                pool.wait_ge(half_set, 1)
                rows_pool(pool, xr)
                splits_pool(pool, 0)

            @block.vector
            def _(dve):
                nc.vector.memset(minus_half[:], -0.5).then_inc(half_set, 1)
                nc.vector.memset(table_aug[N_BUCKETS:N_BUCKETS + 1, :], MASKED).then_inc(masked_set, 1)
                dve.wait_ge(params_tr, 1)
                nc.vector.tensor_copy(vecs[:, 0:NV], psum[:, 0, 0:NV]).then_inc(vecs_ready, 1)
                dve.wait_ge(vecs_ready, 1)
                nc.vector.tensor_scalar(vecs[:, V_QS:V_QS + NG], vecs[:, V_QNORM:V_QNORM + NG], HD ** -0.5, None,
                                        ALU.mult).then_inc(vecs_ready, 1)
                nc.vector.tensor_scalar(vecs[:, V_QS + NG:V_QS + NG + 1], vecs[:, V_XQ:V_XQ + 1], HD ** -0.5, None,
                                        ALU.mult).then_inc(vecs_ready, 1)
                for g in range(NG):
                    dve.wait_ge(lines_mm, g + 1)
                    nc.vector.tensor_copy(lines_sb[0:NH, g, :], psum[0:NH, 1 + g, 0:LINE]).then_inc(lines_copied, 1)
                rows_dve_scale(dve, xr)
                rows_dve_lo(dve, xr)
                splits_dve(dve, 0)

            @block.tensor
            def _(pe):
                pe.wait_ge(ident_loaded, 32)
                pe.wait_ge(params_loaded, 16 * (len(param_loads) - 2))
                nc.tensor.transpose(psum[:, 0, 0:V_FW], rows_a[0:V_FW, :], ident[0:V_FW, 0:V_FW])
                nc.tensor.transpose(psum[:, 0, V_FW:V_FW + 4 * NU], rows_b[0:4 * NU, :], ident[0:4 * NU, 0:4 * NU])
                nc.tensor.transpose(psum[:, 0, V_FW + 4 * NU:V_DW], rows_c[0:2 * NU, :], ident[0:2 * NU, 0:2 * NU])
                for f in range(FT):
                    tr = nc.tensor.transpose(psum[:, 0, V_DW + f * CONV_W:V_DW + (f + 1) * CONV_W],
                                             dw_rows[0:CONV_W, f * P:(f + 1) * P], ident[0:CONV_W, 0:CONV_W])
                tr.then_inc(params_tr, 1)
                pe.wait_ge(masked_set, 1)
                for g in range(NG):
                    nc.tensor.matmul(psum[0:NH, 1 + g, 0:LINE], table_aug[0:N_BUCKETS + 1, g * NH:(g + 1) * NH],
                                     onehot_sb[0:N_BUCKETS + 1, g * LINE:(g + 1) * LINE],
                                     start=True, stop=True).then_inc(lines_mm, 1)
                rows_pe(pe, xr)

        hn_sq = sem("hn_sq")
        hn_ss = sem("hn_ss")
        hn_ms = sem("hn_ms")
        hn_rstd = sem("hn_rstd")
        hn_tr = sem("hn_tr")
        hn_hi = sem("hn_hi")
        hn_lo = sem("hn_lo")
        s_done = sem("s_done")
        s_read = sem("s_read")
        m_done = sem("m_done")
        p_done = sem("p_done")
        p_scaled = sem("p_scaled")
        l_recip = sem("l_recip")
        tp_done = sem("tp_done")
        pt_hi_done = sem("pt_hi_done")
        pt_lo_done = sem("pt_lo_done")
        o_done = sem("o_done")
        o_read = sem("o_read")
        o_stored = [sem("o_stored_even"), sem("o_stored_odd")]
        bias_loaded = sem("bias_loaded")
        bias_flipped = sem("bias_flipped")
        bias_ready = sem("bias_ready")
        v_hi_done = sem("v_hi_done")

        def norm_act_square(act, n, index, sq):
            act.wait_ge(gemm_done, index + 1)
            if n >= 1:
                act.wait_ge(hn_ss, n)
            nc.scalar.activation(sq[:], psum[:, index % 2, :], ACT.Square).then_inc(hn_sq, 1)

        def norm_dve_sum(dve, n, sq):
            dve.wait_ge(hn_sq, n + 1)
            nc.vector.tensor_reduce(sumsq[:, 0:NH], sq[:].rearrange("p (h d) -> p h d", h=NH), AX.X,
                                    ALU.add).then_inc(hn_ss, 1)

        def norm_pool(pool, n):
            pool.wait_ge(hn_ss, n + 1)
            nc.gpsimd.tensor_scalar(meansq[:, 0:NH], sumsq[:, 0:NH], 1.0 / HD, RMS_EPS, ALU.mult,
                                    ALU.add).then_inc(hn_ms, 1)
            pool.wait_ge(hn_ms, n + 1)
            nc.gpsimd.tensor_tensor(rstd[:, n % 2, 0:NH], meansq[:, 0:NH], minus_half[:, 0:NH],
                                    ALU.pow).then_inc(hn_rstd, 1)

        def norm_dve_scale(dve, n, index, qn):
            dve.wait_ge(hn_rstd, n + 1)
            if n >= 1:
                dve.wait_ge(hn_tr, n)
            nc.vector.tensor_tensor(qn[:].rearrange("p (h d) -> p h d", h=NH),
                                    psum[:, index % 2, :].rearrange("p (h d) -> p h d", h=NH),
                                    rstd[:, n % 2, 0:NH].unsqueeze(2).to_broadcast([P, NH, HD]),
                                    ALU.mult).then_inc(gemm_freed, 1)

        def norm_pe(pe, n, index, qn):
            pe.wait_ge(gemm_freed, index + 1)
            if n >= 1:
                pe.wait_ge(hn_lo, n)
            for h in range(NH):
                tr = nc.tensor.transpose(psum[:, 2, h * HD:(h + 1) * HD], qn[:, h * HD:(h + 1) * HD], ident[:])
            tr.then_inc(hn_tr, 1)

        def heads_of(a, tokens):
            return a[:, :, tokens]

        bank2_heads = psum[:, 2, :].rearrange("p (h t) -> p h t", h=NH)

        def norm_act_hi(act, n, wcol, hi, free=None):
            act.wait_ge(hn_tr, n + 1)
            if free:
                act.wait_ge(*free)
            nc.scalar.activation(hi, bank2_heads, ACT.Copy, scale=vecs[:, wcol:wcol + 1]).then_inc(hn_hi, 1)

        def norm_dve_lo(dve, n, wcol, hi, lo):
            dve.wait_ge(hn_hi, n + 1)
            nc.vector.scalar_tensor_tensor(lo, bank2_heads, vecs[:, wcol:wcol + 1], hi.bitcast(F32), ALU.mult,
                                           ALU.subtract).then_inc(hn_lo, 1)

        def transposed_p(pe, a, sc, nkt, ready, count):
            pe.wait_ge(ready, count)
            if a >= 1:
                pe.wait_ge(pt_lo_done, a)
            for h in range(NH):
                for kt in range(nkt):
                    i = h * nkt + kt
                    tr = nc.tensor.transpose(banks(5)[:, i * P:(i + 1) * P], sc[:, h, kt * P:(kt + 1) * P], ident[:])
            tr.then_inc(tp_done, 1)

        def p_act_hi(act, a, pt, n):
            act.wait_ge(tp_done, a + 1)
            if a >= 1:
                act.wait_ge(o_done, a)
            nc.scalar.copy(pt[0][:, 0:n], banks(5)[:, 0:n]).then_inc(pt_hi_done, 1)

        def p_dve_lo(dve, a, pt, n):
            dve.wait_ge(pt_hi_done, a + 1)
            nc.vector.tensor_tensor(pt[1][:, 0:n], banks(5)[:, 0:n], pt[0][:, 0:n].bitcast(F32),
                                    ALU.subtract).then_inc(pt_lo_done, 1)

        off = FREE
        kT = [at("k_hi", off, [NH, S], F32R), at("k_lo", off + 16384, [NH, S], F32R)]
        vT = [at("v_hi", off + 32768, [NT, CW], F32R), at("v_lo", off + 49152, [NT, CW], F32R)]
        off += 65536
        sq = at("sq", off, [CW])
        qn = at("qn", off + 2048, [CW])
        qT = [at("q_hi", off + 4096, [NH, P], F32R), at("q_lo", off + 6144, [NH, P], F32R)]
        sc = at("sc", off + 8192, [NH, 2 * P])
        hankel = at("hankel", off + 8192, [NH, 2 * P])
        pt = [at("pt_hi", off + 12288, [2 * NH * P], F32R), at("pt_lo", off + 16384, [2 * NH * P], F32R)]
        bias = at("bias", off + 20480, [NH, 2 * P])
        ob = at("ob", off + 24576, [2, CW])

        LAST = NT + 4
        for g in range(NG):
            turn_k = g * 3
            turn_v, turn_q, turn_next = turn_k + 1, turn_k + 2, turn_k + 3
            ik, iv, iq = g * 24, g * 24 + 8, g * 24 + 16
            nk0, nq0 = g * 16, g * 16 + 8
            a0 = g * 8

            def has_prev(t):
                return t > 0 if g == 0 else t % 2 == 1 if g == 1 else False

            with nc.Block() as block:
                @block.sync
                def _(sp):
                    sp.wait_ge(lines_stored, 16)
                    lines = bass.AP(bias_lines.tensor, g * NH * LINE, [[1, P], [LINE, NH], [1, 2 * P]])
                    sp.dma_start(hankel[:], lines).then_inc(bias_loaded, 16)
                    load_turns(sp, turn_v, turn_next + 1)

                @block.tensor
                def _(pe):
                    pe.wait_ge(bias_loaded, 16 * (g + 1))
                    for j in range(2):
                        mm = nc.tensor.matmul(psum[:, 3 + j, :], mirror_sb[:],
                                              hankel[:, 2 * j:2 * j + 2, :].rearrange("p h c -> p (h c)"),
                                              start=True, stop=True)
                    mm.then_inc(bias_flipped, 1)
                    for i in range(2 * NT):
                        t = i % NT
                        token_gemm(pe, ik + i, turn_k if i < NT else turn_v, group_tile(g, t), t == 0, t == NT - 1)
                        if 0 <= i - 1 < NT:
                            norm_pe(pe, nk0 + i - 1, ik + i - 1, qn)
                    for i in range(LAST):
                        if i < NT:
                            token_gemm(pe, iq + i, turn_q, group_tile(g, i), i == 0, i == NT - 1)
                        if 0 <= i - 1 < NT:
                            norm_pe(pe, nq0 + i - 1, iq + i - 1, qn)
                        if 0 <= i - 2 < NT:
                            t = i - 2
                            pe.wait_ge(hn_lo, nq0 + t + 1)
                            if a0 + t >= 1:
                                pe.wait_ge(s_read, a0 + t)
                            if t == 0:
                                pe.wait_ge(bias_ready, g + 1)
                            c0, n = ((t - 1) * P, 2 * P) if has_prev(t) else (t * P, P)
                            for h in range(NH):
                                mm = three(pe, banks(3)[:, h * 256:h * 256 + n],
                                           (qT[0][:, h, :], qT[1][:, h, :]),
                                           (kT[0][:, h, c0:c0 + n], kT[1][:, h, c0:c0 + n]), True, True)
                            mm.then_inc(s_done, 1)
                        if 0 <= i - 3 < NT:
                            t = i - 3
                            transposed_p(pe, a0 + t, sc, 1 + has_prev(t), p_done, a0 + t + 1)
                        if 0 <= i - 4 < NT:
                            t = i - 4
                            pe.wait_ge(pt_lo_done, a0 + t + 1)
                            if a0 + t >= 1:
                                pe.wait_ge(o_read, a0 + t)
                            tiles = [t - 1, t] if has_prev(t) else [t]
                            for h in range(NH):
                                for j, kt in enumerate(tiles):
                                    n = (h * len(tiles) + j) * P
                                    mm = three(pe, psum[:, 7, h * HD:(h + 1) * HD],
                                               (pt[0][:, n:n + P], pt[1][:, n:n + P]),
                                               (vT[0][:, kt, h * HD:(h + 1) * HD], vT[1][:, kt, h * HD:(h + 1) * HD]),
                                               j == 0, j == len(tiles) - 1)
                            mm.then_inc(o_done, 1)

                def rows_of(t):
                    if g == 0:
                        return group_out[g][t * P:(t + 1) * P, :]
                    if g == 1:
                        return group_out[g].rearrange("(b p r) c -> r b p c", r=4, p=P)[t // 2, t % 2]
                    return group_out[g].rearrange("(p r) c -> r p c", r=8)[t]

                per_tile = 2 * 16
                stored0 = NT // 2 * per_tile * g

                @block.scalar
                def _(act):
                    for t in range(NT + 1):
                        if t == NT - 1:
                            splits_act(act, turn_v)
                        if t < NT:
                            norm_act_square(act, nk0 + t, ik + t, sq)
                        if t >= 1:
                            n = nk0 + t - 1
                            norm_act_hi(act, n, V_KNORM + g, kT[0][:, :, (t - 1) * P:t * P])
                    for t in range(NT):
                        if t == NT - 1:
                            splits_act(act, turn_q)
                        act.wait_ge(gemm_done, iv + t + 1)
                        nc.scalar.copy(vT[0][:, t, :], psum[:, (iv + t) % 2, :]).then_inc(v_hi_done, 1)
                    for i in range(LAST + 1):
                        if i == NT - 1:
                            splits_act(act, turn_next)
                        if i < NT:
                            norm_act_square(act, nq0 + i, iq + i, sq)
                        if 0 <= i - 1 < NT:
                            t = i - 1
                            free = (s_done, a0 + t) if a0 + t >= 1 else None
                            norm_act_hi(act, nq0 + t, V_QS + g, qT[0][:], free)
                        if 0 <= i - 2 < NT:
                            t = i - 2
                            r = (a0 + t) % 4
                            n = P * (1 + has_prev(t))
                            act.wait_ge(m_done, a0 + t + 1)
                            for h in range(NH):
                                e = nc.scalar.activation(sc[:, h, 0:n], sc[:, h, 0:n], ACT.Exp,
                                                         bias=softstat[:, r, 1, h:h + 1],
                                                         accum_out=softstat[:, r, 0, h:h + 1])
                            e.then_inc(p_done, 1)
                        if 0 <= i - 3 < NT:
                            t = i - 3
                            p_act_hi(act, a0 + t, pt, NH * P * (1 + has_prev(t)))
                        if 0 <= i - 5 < NT:
                            t = i - 5
                            act.wait_ge(o_read, a0 + t + 1)
                            dst = rows_of(t)
                            act.dma_start(dst[:, 0:CW], ob[:, t % 2, :]).then_inc(o_stored[t % 2], 16)
                            act.dma_start(dst[:, CW:], softstat[:, (a0 + t) % 4, :, :].rearrange(
                                "p a h -> p (a h)")).then_inc(o_stored[t % 2], 16)
                        if 0 <= i - 4 < NT:
                            t = i - 4
                            act.wait_ge(o_done, a0 + t + 1)
                            if t >= 2:
                                act.wait_ge(o_stored[t % 2], stored0 + per_tile * (t // 2))
                            nc.scalar.copy(ob[:, t % 2, :], psum[:, 7, :]).then_inc(o_read, 1)
                    for j in range(2):
                        act.wait_ge(o_stored[j], stored0 + per_tile * 4)

                @block.gpsimd
                def _(pool):
                    for t in range(NT):
                        if t == NT - 1:
                            splits_pool(pool, turn_v)
                        norm_pool(pool, nk0 + t)
                    splits_pool(pool, turn_q)
                    for t in range(NT):
                        if t == NT - 1:
                            splits_pool(pool, turn_next)
                        norm_pool(pool, nq0 + t)

                @block.vector
                def _(dve):
                    dve.wait_ge(bias_flipped, g + 1)
                    nc.vector.tensor_copy(bias[:].rearrange("p h c -> p (h c)"), banks(3)).then_inc(bias_ready, 1)
                    for t in range(NT + 1):
                        if t == NT - 1:
                            splits_dve(dve, turn_v)
                        if t < NT:
                            norm_dve_sum(dve, nk0 + t, sq)
                        if t >= 1:
                            cols = slice((t - 1) * P, t * P)
                            norm_dve_lo(dve, nk0 + t - 1, V_KNORM + g, kT[0][:, :, cols], kT[1][:, :, cols])
                        if t < NT:
                            norm_dve_scale(dve, nk0 + t, ik + t, qn)
                    for t in range(NT):
                        if t == NT - 1:
                            splits_dve(dve, turn_q)
                        dve.wait_ge(v_hi_done, a0 + t + 1)
                        nc.vector.tensor_tensor(vT[1][:, t, :], psum[:, (iv + t) % 2, :], vT[0][:, t, :].bitcast(F32),
                                                ALU.subtract).then_inc(gemm_freed, 1)
                    for i in range(NT + 4):
                        if i == NT - 1:
                            splits_dve(dve, turn_next)
                        if i < NT:
                            norm_dve_sum(dve, nq0 + i, sq)
                        if 0 <= i - 1 < NT:
                            norm_dve_lo(dve, nq0 + i - 1, V_QS + g, qT[0][:], qT[1][:])
                        if 0 <= i - 2 < NT:
                            t = i - 2
                            a = a0 + t
                            n = P * (1 + has_prev(t))
                            dve.wait_ge(s_done, a + 1)
                            if a >= 1:
                                dve.wait_ge(tp_done, a)
                            if t == 0:
                                dve.wait_ge(bias_ready, g + 1)
                            nc.vector.tensor_tensor(sc[:, :, 0:n],
                                                    banks(3).rearrange("p (h c) -> p h c", h=NH)[:, :, 0:n],
                                                    bias[:, :, 2 * P - n:], ALU.add).then_inc(s_read, 1)
                            dve.wait_ge(s_read, a + 1)
                            if t >= 4:
                                dve.wait_ge(o_stored[t % 2], stored0 + per_tile * ((t - 4) // 2 + 1))
                            nc.vector.tensor_reduce(softstat[:, a % 4, 1, :], sc[:, :, 0:n], AX.X, ALU.max,
                                                    negate=True).then_inc(m_done, 1)
                        if i < NT:
                            norm_dve_scale(dve, nq0 + i, iq + i, qn)
                        if 0 <= i - 3 < NT:
                            t = i - 3
                            p_dve_lo(dve, a0 + t, pt, NH * P * (1 + has_prev(t)))

        bact = [at("bact_hi", FREE, [FT, S], F32R), at("bact_lo", FREE + 16384, [FT, S], F32R)]
        off = FREE + 32768
        mkT = [at("mk_hi", off, [NH, N_MEM], F32R), at("mk_lo", off + 4096, [NH, N_MEM], F32R)]
        mv = [at("mv_hi", off + 8192, [MT, CW], F32R), at("mv_lo", off + 12288, [MT, CW], F32R)]
        off += 16384
        xsq = at("xsq", off, [CW])
        xqn = at("xqn", off + 2048, [CW])
        xqT = [at("xq_hi", off + 4096, [NH, P], F32R), at("xq_lo", off + 6144, [NH, P], F32R)]
        xsc = at("xsc", off + 8192, [NH, N_MEM])
        xpt = [at("xpt_hi", off + 12288, [2 * NH * P], F32R), at("xpt_lo", off + 16384, [2 * NH * P], F32R)]
        mem_hi = at("mem_hi", off + 20480, [KT, N_MEM], F32R)
        mem_lo = at("mem_lo", off + 28672, [KT, N_MEM], F32R)
        mem_rows = at("mem_rows", off + 36864, [MT, D])
        mem_junk = at("mem_junk", off + 8192, [D])

        mr = Rows(xr, mem_rows, mem_junk, MT, MT, V_MEM_NORM, mem_hi, mem_lo)
        turn_mk = BASE_MEM // RING
        im, nm = NG * 24, NG * 16

        with nc.Block() as block:
            @block.sync
            def _(sp):
                for t in range(MT):
                    sp.dma_start(mem_rows[:, t, :], mem[t * P:(t + 1) * P, :]).then_inc(row_loaded, 16)
                load_turns(sp, turn_mk + 1, turn_mk + 3)

            @block.tensor
            def _(pe):
                rows_pe(pe, mr)
                pe.wait_ge(row_lo, mr.bank0 + KT)
                lhs = [lambda k, t=t: (mem_hi[:, k, t * P:(t + 1) * P], mem_lo[:, k, t * P:(t + 1) * P])
                       for t in range(MT)]
                for t in range(MT):
                    token_gemm(pe, im + t, turn_mk, lhs[t], t == 0, t == MT - 1)
                for t in range(MT):
                    norm_pe(pe, nm + t, im + t, xqn)
                for t in range(MT):
                    token_gemm(pe, im + MT + t, turn_mk + 1, lhs[t], t == 0, t == MT - 1)

            def key_cols(a, t):
                return a[:, :, t * P:(t + 1) * P]

            @block.scalar
            def _(act):
                rows_act_squares(act, mr, lambda e, t: e.wait_ge(row_loaded, 16 * MT))
                rows_act_hi(act, mr)
                norm_act_square(act, nm, im, xsq)
                splits_act(act, turn_mk + 1)
                norm_act_square(act, nm + 1, im + 1, xsq)
                for t in range(MT):
                    norm_act_hi(act, nm + t, V_XK, key_cols(mkT[0], t))
                for t in range(MT):
                    if t == MT - 1:
                        splits_act(act, turn_mk + 2)
                    act.wait_ge(gemm_done, im + MT + t + 1)
                    nc.scalar.copy(mv[0][:, t, :], psum[:, (im + t) % 2, :]).then_inc(v_hi_done, 1)

            @block.gpsimd
            def _(pool):
                rows_pool(pool, mr)
                norm_pool(pool, nm)
                splits_pool(pool, turn_mk + 1)
                norm_pool(pool, nm + 1)
                splits_pool(pool, turn_mk + 2)

            @block.vector
            def _(dve):
                rows_dve_scale(dve, mr)
                rows_dve_lo(dve, mr)
                norm_dve_sum(dve, nm, xsq)
                norm_dve_scale(dve, nm, im, xqn)
                splits_dve(dve, turn_mk + 1)
                norm_dve_sum(dve, nm + 1, xsq)
                norm_dve_lo(dve, nm, V_XK, key_cols(mkT[0], 0), key_cols(mkT[1], 0))
                norm_dve_scale(dve, nm + 1, im + 1, xqn)
                norm_dve_lo(dve, nm + 1, V_XK, key_cols(mkT[0], 1), key_cols(mkT[1], 1))
                for t in range(MT):
                    if t == MT - 1:
                        splits_dve(dve, turn_mk + 2)
                    dve.wait_ge(v_hi_done, NG * NT + t + 1)
                    nc.vector.tensor_tensor(mv[1][:, t, :], psum[:, (im + t) % 2, :], mv[0][:, t, :].bitcast(F32),
                                            ALU.subtract).then_inc(gemm_freed, 1)

        b_hi = sem("b_hi")
        b_lo = sem("b_lo")
        turn_x = BASE_CROSS // RING
        ix, nx, ax = im + 2 * MT, nm + MT, NG * NT

        def bact_tile(part, t):
            return bact[part][:, :, t * P:(t + 1) * P]

        def bank_channels(b):
            return psum[:, b, :].rearrange("p (f t) -> p f t", f=FT)

        with nc.Block() as block:
            @block.sync
            def _(sp):
                load_turns(sp, turn_x + 1, turn_x + 2)

            @block.tensor
            def _(pe):
                for i in range(LAST):
                    if i < NT:
                        token_gemm(pe, ix + i, turn_x, act_tile(slice(i * P, (i + 1) * P)), i == 0, i == NT - 1)
                    if 0 <= i - 1 < NT:
                        norm_pe(pe, nx + i - 1, ix + i - 1, xqn)
                    if 0 <= i - 2 < NT:
                        t = i - 2
                        pe.wait_ge(hn_lo, nx + t + 1)
                        if t >= 1:
                            pe.wait_ge(p_done, ax + t)
                        for h in range(NH):
                            mm = three(pe, banks(3)[:, h * N_MEM:(h + 1) * N_MEM],
                                       (xqT[0][:, h, :], xqT[1][:, h, :]), (mkT[0][:, h, :], mkT[1][:, h, :]),
                                       True, True)
                        mm.then_inc(s_done, 1)
                    if 0 <= i - 3 < NT:
                        t = i - 3
                        transposed_p(pe, ax + t, xsc, MT, p_scaled, t + 1)
                    if 0 <= i - 4 < NT:
                        t = i - 4
                        pe.wait_ge(pt_lo_done, ax + t + 1)
                        if t >= 1:
                            pe.wait_ge(b_lo, t)
                        for h in range(NH):
                            for kt in range(MT):
                                n = (h * MT + kt) * P
                                mm = three(pe, psum[:, 7, h * P:(h + 1) * P],
                                           (mv[0][:, kt, h * HD:(h + 1) * HD], mv[1][:, kt, h * HD:(h + 1) * HD]),
                                           (xpt[0][:, n:n + P], xpt[1][:, n:n + P]), kt == 0, kt == MT - 1)
                        mm.then_inc(o_done, 1)

            @block.scalar
            def _(act):
                for i in range(LAST):
                    if i == NT - 1:
                        splits_act(act, turn_x + 1)
                    if i < NT:
                        norm_act_square(act, nx + i, ix + i, xsq)
                    if 0 <= i - 1 < NT:
                        norm_act_hi(act, nx + i - 1, V_QS + NG, xqT[0][:], (s_done, ax + i - 1))
                    if 0 <= i - 2 < NT:
                        a = ax + i - 2
                        act.wait_ge(m_done, a + 1)
                        act.wait_ge(tp_done, a)
                        for h in range(NH):
                            e = nc.scalar.activation(xsc[:, h, :], banks(3)[:, h * N_MEM:(h + 1) * N_MEM], ACT.Exp,
                                                     bias=softstat[:, a % 4, 1, h:h + 1],
                                                     accum_out=softstat[:, a % 4, 0, h:h + 1])
                        e.then_inc(p_done, 1)
                    if 0 <= i - 3 < NT:
                        p_act_hi(act, ax + i - 3, xpt, MT * NH * P)
                    if 0 <= i - 4 < NT:
                        t = i - 4
                        act.wait_ge(o_done, ax + t + 1)
                        nc.scalar.copy(bact_tile(0, t), bank_channels(7)).then_inc(b_hi, 1)

            @block.gpsimd
            def _(pool):
                for t in range(NT):
                    if t == NT - 1:
                        splits_pool(pool, turn_x + 1)
                    norm_pool(pool, nx + t)

            @block.vector
            def _(dve):
                for i in range(LAST):
                    if i == NT - 1:
                        splits_dve(dve, turn_x + 1)
                    if i < NT:
                        norm_dve_sum(dve, nx + i, xsq)
                    if 0 <= i - 1 < NT:
                        norm_dve_lo(dve, nx + i - 1, V_QS + NG, xqT[0][:], xqT[1][:])
                    if 0 <= i - 2 < NT:
                        a = ax + i - 2
                        dve.wait_ge(s_done, a + 1)
                        nc.vector.tensor_reduce(softstat[:, a % 4, 1, :],
                                                banks(3).rearrange("p (h c) -> p h c", h=NH), AX.X, ALU.max,
                                                negate=True).then_inc(m_done, 1)
                    if i < NT:
                        norm_dve_scale(dve, nx + i, ix + i, xqn)
                    if 0 <= i - 3 < NT:
                        p_dve_lo(dve, ax + i - 3, xpt, MT * NH * P)
                    if 0 <= i - 2 < NT:
                        a = ax + i - 2
                        dve.wait_ge(p_done, a + 1)
                        nc.vector.reciprocal(recip_l[:, a % 2, :], softstat[:, a % 4, 0, :]).then_inc(l_recip, 1)
                        dve.wait_ge(l_recip, i - 1)
                        nc.vector.tensor_tensor(xsc[:], xsc[:],
                                                recip_l[:, a % 2, :].unsqueeze(2).to_broadcast([P, NH, N_MEM]),
                                                ALU.mult).then_inc(p_scaled, 1)
                    if 0 <= i - 4 < NT:
                        t = i - 4
                        dve.wait_ge(b_hi, t + 1)
                        nc.vector.tensor_tensor(bact_tile(1, t), bank_channels(7), bact_tile(0, t).bitcast(F32),
                                                ALU.subtract).then_inc(b_lo, 1)

        gate_done = sem("gate_done")
        sig_done = sem("sig_done")
        val_done = sem("val_done")
        prod_done = sem("prod_done")
        sum_done = sem("sum_done")

        def feature_half(pe, bank, slots, acts, f, half, first, last, done):
            for k, s in enumerate(slots):
                turn, pos = s // RING, s % RING
                if first:
                    wait_slot(pe, turn, pos)
                mm = three(pe, psum[:, bank + half, :],
                           (whi[:, pos, f * P:(f + 1) * P], wlo[:, pos, f * P:(f + 1) * P]),
                           (acts[0][:, k, half * CW:(half + 1) * CW], acts[1][:, k, half * CW:(half + 1) * CW]),
                           k == 0, k == len(slots) - 1)
                if last:
                    mm.then_inc(w_freed, 1)
            if last:
                pe.wait_ge(w_freed, slots[-1] + 1)
                pe.sem_inc(done, 1)
            elif half == 1:
                mm.then_inc(done, 1)

        act_pair = (act_hi, act_lo)

        def gate_features(pe, before, slots, after_half=None):
            for f in range(4):
                n = before + f
                if n >= 2:
                    pe.wait_ge(sig_done, n - 1)
                for half in range(2):
                    feature_half(pe, n % 2 * 2, slots, act_pair, f, half, f == 0 and half == 0,
                                 f == 3 and half == 1, gate_done)
                    if after_half:
                        after_half(2 * f + half)

        def value_features(pe, before, slots, acts):
            for f in range(4):
                n = before + f
                if n >= 2:
                    pe.wait_ge(prod_done, n - 1)
                for half in range(2):
                    feature_half(pe, 4 + n % 2 * 2, slots, acts, f, half, f == 0 and half == 0,
                                 f == 3 and half == 1, val_done)

        PAD = CONV_W - 1
        merged = at("merged", FREE + 32768, [KT, S])
        u = at("u", FREE + 65536, [FT, S + 32])
        acc = at("acc", FREE + 65536 + FT * (S + 32) * 4, [S])
        pad_set = sem("pad_set")
        conv_done = sem("conv_done")
        turn_glu = BASE_GLU // RING

        def conv_step(dve, n):
            f, tap = n // CONV_W, CONV_W - 1 - n % CONV_W
            w = vecs[:, V_DW + f * CONV_W + tap:V_DW + f * CONV_W + tap + 1]
            if n >= 1:
                dve.wait_ge(conv_done, n)
            src = u[:, f, tap:tap + S]
            if tap == CONV_W - 1:
                dve.wait_ge(pad_set, 1)
                dve.wait_ge(prod_done, f + 1)
                step = nc.vector.tensor_scalar(acc[:], src, w, vecs[:, V_DW_B + f:V_DW_B + f + 1], ALU.mult, ALU.add)
            else:
                step = nc.vector.scalar_tensor_tensor(u[:, f, 0:S] if tap == 0 else acc[:], src, w, acc[:],
                                                      ALU.mult, ALU.add)
            step.then_inc(conv_done, 1)

        conv_steps = iter(range(FT * CONV_W))

        def conv(dve, count):
            for _, n in zip(range(count), conv_steps):
                conv_step(dve, n)

        with nc.Block() as block:
            @block.sync
            def _(sp):
                load_turns(sp, turn_glu + 1, turn_glu + 3)

            @block.tensor
            def _(pe):
                gate_features(pe, 0, range(BASE_GLU, BASE_GLU + RING))
                value_features(pe, 0, range(BASE_GLU + RING, BASE_GLU + 2 * RING), act_pair)

            @block.scalar
            def _(act):
                for f in range(4):
                    if f == 3:
                        splits_act(act, turn_glu + 1)
                    act.wait_ge(gate_done, f + 1)
                    nc.scalar.activation(merged[:, f, :], banks(f % 2 * 2), ACT.Sigmoid).then_inc(sig_done, 1)
                splits_act(act, turn_glu + 2)

            @block.gpsimd
            def _(pool):
                splits_pool(pool, turn_glu + 1)
                splits_pool(pool, turn_glu + 2)

            @block.vector
            def _(dve):
                nc.vector.memset(u[:, :, 0:PAD], 0.0).then_inc(pad_set, 1)
                splits_dve(dve, turn_glu + 1)
                for f in range(4):
                    if f == 3:
                        splits_dve(dve, turn_glu + 2)
                    dve.wait_ge(sig_done, f + 1)
                    dve.wait_ge(val_done, f + 1)
                    nc.vector.tensor_tensor(u[:, f, PAD:PAD + S], banks(4 + f % 2 * 2), merged[:, f, :],
                                            ALU.mult).then_inc(prod_done, 1)
                    if f < 3:
                        conv(dve, 6)

        gbuf = at("gbuf", FREE + 65536, [4, S])
        off = FREE + 65536 + FT * (S + 32) * 4
        nrm = at("nrm", off, [CW])
        swz = at("swz", off + 2048, [FT, P])
        sws = at("sws", off + 4096, [FT, P])
        off = FREE + 65536 + 16384
        CMB = NH * HD + 2 * NH
        grp = at("grp", off, [NG, CMB])
        prod = at("prod", off + NG * CMB * 4, [CW])
        mean = at("mean", off + NG * CMB * 4 + 2048, [CW])

        ln_tr = sem("ln_tr")
        ln_stats = sem("ln_stats")
        ln_aggr = sem("ln_aggr")
        ln_eps = sem("ln_eps")
        ln_rstd = sem("ln_rstd")
        ln_normed = sem("ln_normed")
        ln_back = sem("ln_back")
        sw_z = sem("sw_z")
        sw_sig = sem("sw_sig")
        sw_done = sem("sw_done")
        grp_loaded = sem("grp_loaded")
        cmb_min = sem("cmb_min")
        cmb_exp = sem("cmb_exp")
        cmb_step = sem("cmb_step")
        cmb_done = sem("cmb_done")
        cmb_tr = sem("cmb_tr")

        def channels_norm_pe(pe, q):
            if q < NT:
                if q >= 2:
                    pe.wait_ge(ln_normed, q - 1)
                for f in range(FT):
                    tr = nc.tensor.transpose(psum[:, 4 + q % 2, f * P:(f + 1) * P], u[:, f, q * P:(q + 1) * P], ident[:])
                tr.then_inc(ln_tr, 1)
            if q >= 1:
                t = q - 1
                pe.wait_ge(ln_normed, t + 1)
                if t >= 2:
                    pe.wait_ge(sw_sig, t - 1)
                for f in range(FT):
                    tr = nc.tensor.transpose(psum[:, 6 + t % 2, f * P:(f + 1) * P], nrm[:, f * P:(f + 1) * P], ident[:])
                tr.then_inc(ln_back, 1)

        def channels_norm_dve(dve, q):
            if q < NT:
                m = moments[:, q % 2, :]
                dve.wait_ge(ln_tr, q + 1)
                nc.vector.bn_stats(combine_s[:, 0:1, :, 0:2], psum[:, 4 + q % 2, :]).then_inc(ln_stats, 1)
                dve.wait_ge(ln_stats, q + 1)
                nc.vector.bn_aggr(m[:, 0:2], combine_s[:, 0:1, :, 0:2]).then_inc(ln_aggr, 1)
            if q >= 1:
                t = q - 1
                dve.wait_ge(sw_sig, t + 1)
                nc.vector.tensor_tensor(swz[:], swz[:], sws[:], ALU.mult).then_inc(sw_done, 1)
                dve.wait_ge(b_hi, NT + t + 1)
                nc.vector.tensor_tensor(bact_tile(1, t), swz[:], bact_tile(0, t).bitcast(F32),
                                        ALU.subtract).then_inc(b_lo, 1)
            if q < NT:
                dve.wait_ge(ln_rstd, q + 1)
                if q >= 1:
                    dve.wait_ge(ln_back, q)
                nc.vector.tensor_scalar(nrm[:], psum[:, 4 + q % 2, :], m[:, 0:1], m[:, 3:4], ALU.subtract,
                                        ALU.mult).then_inc(ln_normed, 1)

        def channels_norm_pool(pool, q):
            if q < NT:
                m = moments[:, q % 2, :]
                pool.wait_ge(ln_aggr, q + 1)
                nc.gpsimd.tensor_scalar(m[:, 2:3], m[:, 1:2], 1.0, LN_EPS, ALU.mult, ALU.add).then_inc(ln_eps, 1)
                pool.wait_ge(ln_eps, q + 1)
                nc.gpsimd.tensor_tensor(m[:, 3:4], m[:, 2:3], minus_half[:, 0:1], ALU.pow).then_inc(ln_rstd, 1)

        def channels_norm_act(act, q):
            if q >= 1:
                t = q - 1
                act.wait_ge(ln_back, t + 1)
                if t >= 1:
                    act.wait_ge(b_lo, NT + t)
                for f in range(FT):
                    w, b = (vecs[:, v + f:v + f + 1] for v in (V_LN_W, V_LN_B))
                    src = psum[:, 6 + t % 2, f * P:(f + 1) * P]
                    z = nc.scalar.activation(swz[:, f, :], src, ACT.Identity, bias=b, scale=w)
                    s = nc.scalar.activation(sws[:, f, :], src, ACT.Sigmoid, bias=b, scale=w)
                s.then_inc(sw_sig, 1)
                act.wait_ge(sw_done, t + 1)
                nc.scalar.copy(bact_tile(0, t), swz[:]).then_inc(b_hi, 1)

        def groups_mean_sync(sp):
            for t in range(NT):
                if t >= 1:
                    sp.wait_ge(cmb_done, t)
                for g in range(NG):
                    sp.dma_start(grp[:, g, :], group_out[g][t * P:(t + 1) * P, :]).then_inc(grp_loaded, 16)

        def groups_mean_dve(dve, q):
            base = 7 * q

            def chained(ins, n):
                ins.then_inc(cmb_step, 1)
                dve.wait_ge(cmb_step, base + n)
            if q < NT:
                low, shift, e, le, total, f = (combine_s[:, i] for i in range(6))
                dve.wait_ge(grp_loaded, 16 * NG * (q + 1))
                neg = grp[:, :, CW + NH:CW + 2 * NH]
                chained(nc.vector.tensor_tensor(low[:, 0], neg[:, 0], neg[:, 1], ALU.min), 1)
                chained(nc.vector.tensor_tensor(low[:, 0], low[:, 0], neg[:, 2], ALU.min), 2)
                nc.vector.tensor_tensor(shift, low[:, 0].unsqueeze(1).to_broadcast([P, NG, NH]), neg,
                                        ALU.subtract).then_inc(cmb_min, 1)
                dve.wait_ge(cmb_exp, q + 1)
                chained(nc.vector.tensor_tensor(le, e, grp[:, :, CW:CW + NH], ALU.mult), 3)
                chained(nc.vector.tensor_tensor(total[:, 0], le[:, 0], le[:, 1], ALU.add), 4)
                chained(nc.vector.tensor_tensor(total[:, 0], total[:, 0], le[:, 2], ALU.add), 5)
                chained(nc.vector.reciprocal(total[:, 1], total[:, 0]), 6)
                chained(nc.vector.tensor_tensor(f, e, total[:, 1].unsqueeze(1).to_broadcast([P, NG, NH]),
                                                ALU.mult), 7)
                if q >= 1:
                    dve.wait_ge(cmb_tr, q)
                for g in range(NG):
                    dst = mean if g == 0 else prod
                    nc.vector.tensor_tensor(dst[:].rearrange("p (h d) -> p h d", h=NH),
                                            grp[:, g, 0:CW].rearrange("p (h d) -> p h d", h=NH),
                                            f[:, g].unsqueeze(2).to_broadcast([P, NH, HD]),
                                            ALU.mult).then_inc(cmb_part, 1)
                    dve.wait_ge(cmb_part, 4 * q + (1, 2, 4)[g])
                    if g:
                        nc.vector.tensor_tensor(mean[:], mean[:], prod[:], ALU.add).then_inc(
                            cmb_part if g == 1 else cmb_done, 1)
                    if g == 1:
                        dve.wait_ge(cmb_part, 4 * q + 3)
            if q >= 1:
                t = q - 1
                dve.wait_ge(b_hi, 2 * NT + t + 1)
                nc.vector.tensor_tensor(bact_tile(1, t), bank_channels(4 + t % 2), bact_tile(0, t).bitcast(F32),
                                        ALU.subtract).then_inc(b_lo, 1)

        def groups_mean_act(act, q):
            if q < NT:
                act.wait_ge(cmb_min, q + 1)
                nc.scalar.activation(combine_s[:, 2], combine_s[:, 1], ACT.Exp).then_inc(cmb_exp, 1)
            if q >= 1:
                t = q - 1
                act.wait_ge(cmb_tr, t + 1)
                nc.scalar.copy(bact_tile(0, t), bank_channels(4 + t % 2)).then_inc(b_hi, 1)

        def groups_mean_pe(pe, q):
            if q >= 1:
                t = q - 1
                pe.wait_ge(cmb_done, t + 1)
                if t >= 2:
                    pe.wait_ge(b_lo, 2 * NT + t - 1)
                for h in range(NH):
                    tr = nc.tensor.transpose(psum[:, 4 + t % 2, h * P:(h + 1) * P], mean[:, h * P:(h + 1) * P], ident[:])
                tr.then_inc(cmb_tr, 1)

        cmb_part = sem("cmb_part")
        NOTHING = (lambda e, q: None,) * 4
        prepare = [NOTHING, (channels_norm_pe, channels_norm_act, channels_norm_dve, channels_norm_pool),
                   (groups_mean_pe, groups_mean_act, groups_mean_dve, lambda e, q: None)]

        for b, gate in enumerate((2, 1, 0)):
            first = BASE_BRANCH + b * SLOTS_BRANCH
            turn = first // RING
            gates = [range(first, first + 8), range(first + 12, first + 20)]
            outs = [range(first + 8, first + 12), range(first + 20, first + 24)]
            before = 4 + b * KT

            def quarters(a):
                return a.rearrange("p (a c) -> p a c", c=S // 4)

            def sig_at(f):
                if b == 0:
                    return quarters(merged[:, f, :])
                if b == 1:
                    return u[:, :, f % 4 * 2 * P:(f % 4 * 2 + 2) * P]
                return quarters(gbuf[:, f % 4, :])
            prep_pe, prep_act, prep_dve, prep_pool = prepare[b]

            def pair(n, base=0):
                return banks(base + n % 2 * 2)

            def split_range(eng, ops, s0, s1):
                for s in range(s0, s1):
                    t, pos = (first + s) // RING, (first + s) % RING
                    if ops is None:
                        split_hi(eng, t, pos)
                    elif (pos % 2 == 0) == (ops is nc.gpsimd):
                        split_lo(eng, ops, t, pos)

            with nc.Block() as block:
                @block.sync
                def _(sp):
                    if b == 2:
                        groups_mean_sync(sp)
                    load_turns(sp, turn + 1, turn + 4)

                @block.tensor
                def _(pe):
                    gate_features(pe, before, gates[0], lambda q: prep_pe(pe, q))
                    prep_pe(pe, NT)
                    pe.wait_ge(b_lo, NT * (b + 1))
                    value_features(pe, before, outs[0], bact)
                    gate_features(pe, before + 4, gates[1])
                    value_features(pe, before + 4, outs[1], bact)

                def gate_sigmoid(act, f):
                    n = before + f
                    act.wait_ge(gate_done, n + 1)
                    if b >= 1 and f >= 4:
                        act.wait_ge(prod_done, n - 3)
                        act.wait_ge(sum_done, (b - 1) * KT + f - 3)
                    if b == 1 and f < 4:
                        act.wait_ge(ln_tr, 2 * f + 2)
                    col = V_GATE_B + gate * KT + f
                    nc.scalar.activation(sig_at(f), quarters(pair(n)), ACT.Sigmoid, bias=vecs[:, col:col + 1]).then_inc(sig_done, 1)

                @block.scalar
                def _(act):
                    for q in range(NT):
                        if q == NT - 1:
                            split_range(act, None, 8, 16)
                        prep_act(act, q)
                        if q % 2 == 1:
                            gate_sigmoid(act, q // 2)
                    prep_act(act, NT)
                    split_range(act, None, 16, 20)
                    for f in range(4, KT):
                        if f == KT - 1:
                            split_range(act, None, 20, 28)
                        gate_sigmoid(act, f)
                    split_range(act, None, 28, 32)

                @block.gpsimd
                def _(pool):
                    for q in range(NT):
                        if q == NT - 1:
                            split_range(pool, nc.gpsimd, 8, 16)
                        prep_pool(pool, q)
                    split_range(pool, nc.gpsimd, 16, 32)

                def branch_product(dve, f):
                    n = before + f
                    dve.wait_ge(sig_done, n + 1)
                    dve.wait_ge(val_done, n + 1)
                    nc.vector.tensor_tensor(sig_at(f), quarters(pair(n, 4)), sig_at(f), ALU.mult).then_inc(prod_done, 1)
                    if b >= 1:
                        dve.wait_ge(prod_done, n + 1)
                        nc.vector.tensor_tensor(quarters(merged[:, f, :]), quarters(merged[:, f, :]), sig_at(f),
                                                ALU.add).then_inc(sum_done, 1)

                @block.vector
                def _(dve):
                    for q in range(NT):
                        if q == NT - 1:
                            split_range(dve, nc.vector, 8, 16)
                        prep_dve(dve, q)
                        if b == 0:
                            conv(dve, 4)
                    prep_dve(dve, NT)
                    for f in range(0, 4):
                        if f == 3:
                            split_range(dve, nc.vector, 16, 20)
                        branch_product(dve, f)
                        if b == 0:
                            conv(dve, 3)
                    if b == 0:
                        conv(dve, 30)
                    split_range(dve, nc.vector, 20, 28)
                    for f in range(4, KT):
                        if f == KT - 1:
                            split_range(dve, nc.vector, 28, 32)
                        branch_product(dve, f)
                        if b == 0:
                            conv(dve, 4 if f < KT - 1 else FT * CONV_W)

        h_rows = at("h_rows", FREE, [NT, D])
        h_junk = at("h_junk", FREE + 65536, [D])
        h_hi = act_hi
        m_hi = sem("m_hi")
        m_lo = sem("m_lo")
        res_loaded = sem("res_loaded")
        h_stored = [sem("h_stored0"), sem("h_stored1")]
        turn_o = BASE_WOUT // RING
        io = ix + NT
        hr = Rows(mr, h_rows, h_junk, NT, NT // 2, V_FFN_NORM, act_hi, act_lo)
        T_UP = BASE_UP // RING
        T_DOWN = BASE_DOWN // RING

        with nc.Block() as block:
            @block.sync
            def _(sp):
                for t in range(NT):
                    sp.dma_start(h_rows[:, t, :], x[t * P:(t + 1) * P, :]).then_inc(res_loaded, 16)
                load_turns(sp, turn_o + 1, turn_o + 3)

            @block.tensor
            def _(pe):
                for j in range(2):
                    for t in range(NT):
                        if j == 0 and t == 0:
                            tile = act_tile(slice(0, P))

                            def tile_when_cut(k):
                                pe.wait_ge(m_lo, k + 1)
                                return tile(k)
                            token_gemm(pe, io, turn_o, tile_when_cut, True, False)
                        else:
                            token_gemm(pe, io + j * NT + t, turn_o + j, act_tile(slice(t * P, (t + 1) * P)), t == 0,
                                       t == NT - 1)
                rows_pe(pe, hr)

            @block.scalar
            def _(act):
                for k in range(KT):
                    nc.scalar.copy(act_hi[:, k, :], merged[:, k, :]).then_inc(m_hi, 1)
                splits_act(act, turn_o + 1)

                def row_ready(e, t):
                    if t == NT - 1:
                        splits_act(e, turn_o + 2)
                    e.wait_ge(gemm_freed, io + NT + t + 1)
                    e.dma_start(h_dram[t * P:(t + 1) * P, :], h_rows[:, t, :]).then_inc(h_stored[t // 4], 16)
                rows_act_squares(act, hr, row_ready)
                rows_act_hi(act, hr)

            @block.gpsimd
            def _(pool):
                splits_pool(pool, turn_o + 1)
                splits_pool(pool, turn_o + 2)
                rows_pool(pool, hr)

            @block.vector
            def _(dve):
                for k in range(KT):
                    dve.wait_ge(m_hi, k + 1)
                    nc.vector.tensor_tensor(act_lo[:, k, :], merged[:, k, :], act_hi[:, k, :].bitcast(F32),
                                            ALU.subtract).then_inc(m_lo, 1)
                dve.wait_ge(res_loaded, 16 * NT)
                for j in range(2):
                    for t in range(NT):
                        if t == NT - 1:
                            splits_dve(dve, turn_o + 1 + j)
                        n = io + j * NT + t
                        cols = slice(j * CW, (j + 1) * CW)
                        dve.wait_ge(gemm_done, n + 1)
                        nc.vector.tensor_tensor(h_rows[:, t, cols], psum[:, n % 2, :], h_rows[:, t, cols],
                                                ALU.add).then_inc(gemm_freed, 1)
                for b in range(2):
                    dve.wait_ge(h_stored[b], 16 * 4)
                rows_dve_scale(dve, hr)
                rows_dve_lo(dve, hr)

        gated = at("gated", FREE, [NU, S])
        value = at("value", FREE + NU * S * 4, [S])
        wait_met = sem("wait_met")
        up_done = sem("up_done")
        pairs_free = sem("pairs_free")
        base_done = sem("base_done")
        tap_done = sem("tap_done")
        silu_done = sem("silu_done")
        value_free = sem("value_free")

        def up_param(base, kind, U):
            col = base + kind * NU + U
            return vecs[:, bass.ds(col, 1)]

        def up_dst(kind, U):
            return gated[:, U, :] if kind else value[:]

        def met(act):
            act.sem_inc(wait_met, 1)

        def up_base(act, kind, U, i):
            act.wait_ge(up_done, 2 * U + (1 if kind else 2))
            if not kind:
                act.wait_ge(value_free, U + 1)
            met(act)
            nc.scalar.activation(up_dst(kind, U), banks((0 if kind else 4) + 2 * i), ACT.Identity,
                                 bias=up_param(V_FB, kind, U), scale=up_param(V_FW + 4 * NU, kind, U)
                                 ).then_inc(base_done, 1)

        def up_silu(act, U):
            act.wait_ge(pairs_free, 4 + 2 * U + 1)
            met(act)
            nc.scalar.activation(gated[:, U, :], gated[:, U, :], ACT.Silu).then_inc(silu_done, 1)

        def up_taps(dve, kind, U, i):
            src, dst = banks((0 if kind else 4) + 2 * i), up_dst(kind, U)
            dve.wait_ge(base_done, 2 * U + (1 if kind else 2))
            nc.vector.scalar_tensor_tensor(dst[:, 1:], src[:, 0:S - 1], up_param(V_FW + 2 * NU, kind, U), dst[:, 1:],
                                           ALU.mult, ALU.add).then_inc(tap_done, 1)
            dve.wait_ge(tap_done, 2 * U + (1 if kind else 2))
            nc.vector.scalar_tensor_tensor(dst[:, 2:], src[:, 0:S - 2], up_param(V_FW, kind, U), dst[:, 2:],
                                           ALU.mult, ALU.add).then_inc(pairs_free, 1)

        def up_product(dve, U):
            dve.wait_ge(silu_done, U + 1)
            dve.wait_ge(pairs_free, 4 + 2 * U + 2)
            nc.vector.tensor_tensor(gated[:, U, :], gated[:, U, :], value[:], ALU.mult).then_inc(value_free, 1)

        def up_chunk_act(act, c, splits):
            for i in range(2):
                U = 2 * c + i
                up_base(act, 1, U, i)
                if i == 1:
                    splits(act)
                up_base(act, 0, U, i)
                up_silu(act, U)

        def up_chunk_dve(dve, c, splits):
            for i in range(2):
                U = 2 * c + i
                up_taps(dve, 1, U, i)
                if i == 1:
                    splits(dve)
                up_taps(dve, 0, U, i)
                up_product(dve, U)

        def down_piece(k, n):
            return w_down[bass.ds(k * P, P), n * CW:(n + 1) * CW]

        with nc.Block() as block:
            @block.sync
            def _(sp):
                with sp.Fori(0, N_UP - 1) as c:
                    for pos in range(RING):
                        load_slot(sp, c + (T_UP + 1), pos,
                                  up_halves[pos * P:(pos + 1) * P, :, bass.ds((c + 1) * (CW // 2), CW // 2)], 2)
                for pos in range(2):
                    load_slot(sp, T_DOWN, pos, w_down[pos * P:(pos + 1) * P, 0:CW])

            @block.tensor
            def _(pe):
                with pe.Fori(0, N_UP) as c:
                    for i in range(2):
                        for kind in (1, 0):
                            pe.wait_ge(pairs_free, 4 * c + (2 * i + 2 - kind))
                            last_tile = i == 1 and kind == 0
                            for half in range(2):
                                for k in range(KT):
                                    if i == 0 and kind == 1 and half == 0:
                                        wait_slot(pe, c + T_UP, k)
                                    cols = slice((2 * kind + i) * P, (2 * kind + i + 1) * P)
                                    mm = three(pe, psum[:, (0 if kind else 4) + 2 * i + half, :],
                                               (whi[:, k, cols], wlo[:, k, cols]),
                                               (act_hi[:, k, half * CW:(half + 1) * CW],
                                                act_lo[:, k, half * CW:(half + 1) * CW]), k == 0, k == KT - 1)
                                    if last_tile and half == 1:
                                        mm.then_inc(w_freed, 1)
                            if last_tile:
                                pe.wait_ge(w_freed, RING * c + (BASE_UP + RING))
                                pe.sem_inc(up_done, 1)
                            else:
                                mm.then_inc(up_done, 1)

            @block.scalar
            def _(act):
                with act.Fori(0, N_UP - 1) as c:
                    up_chunk_act(act, c, lambda e: splits_act(e, c + (T_UP + 1)))
                up_chunk_act(act, N_UP - 1, lambda e: splits_act(e, T_DOWN, 2))

            @block.gpsimd
            def _(pool):
                with pool.Fori(0, N_UP - 1) as c:
                    splits_pool(pool, c + (T_UP + 1))
                splits_pool(pool, T_DOWN, 2)

            @block.vector
            def _(dve):
                dve.sem_inc(pairs_free, 4)
                dve.sem_inc(value_free, 1)
                with dve.Fori(0, N_UP - 1) as c:
                    up_chunk_dve(dve, c, lambda e: splits_dve(e, c + (T_UP + 1)))
                up_chunk_dve(dve, N_UP - 1, lambda e: splits_dve(e, T_DOWN, 2))

        gs = [at("gs_hi", ACTS, [2, S], F32R), at("gs_lo", ACTS + 2 * S * 4, [2, S], F32R)]
        h_res = at("h_res", ACTS + 4 * S * 4, [NT, CW])
        gs_hi_done = sem("gs_hi_done")
        gs_lo_done = sem("gs_lo_done")
        hres_loaded = sem("hres_loaded")
        down_done = sem("down_done")
        out_ready = sem("out_ready")
        out_stored = sem("out_stored")
        LO0, FREED0 = 4 * T_DOWN, BASE_DOWN

        def down_split_hi(act, half_m, pos, k, with_weight):
            if with_weight:
                act.wait_ge(w_freed, 2 * half_m + (pos - 1 + FREED0))
                met(act)
            nc.scalar.copy(gs[0][:, pos, :], gated[:, k, :]).then_inc(gs_hi_done, 1)
            if with_weight:
                act.wait_ge(w_loaded[pos], 16 * half_m + 16 * (T_DOWN + 1))
                nc.scalar.copy(whi[:, pos, :], stage[:, pos, :]).then_inc(w_hi, 1)

        def down_lo_gated(dve, half_m, pos, k):
            dve.wait_ge(gs_hi_done, 2 * half_m + (pos + 1))
            nc.vector.tensor_tensor(gs[1][:, pos, :], gated[:, k, :], gs[0][:, pos, :].bitcast(F32),
                                    ALU.subtract).then_inc(gs_lo_done, 1)

        def down_lo_weight(eng, ops, half_m, pos):
            eng.wait_ge(w_hi, 2 * half_m + (FREED0 + pos + 1))
            ops.tensor_tensor(wlo[:, pos, :], stage[:, pos, :], whi[:, pos, :].bitcast(F32),
                              ALU.subtract).then_inc(w_lo[pos], 1)

        with nc.Block() as block:
            @block.sync
            def _(sp):
                def load_residual(n):
                    for t in range(NT):
                        sp.dma_start(h_res[:, t, :], h_dram[t * P:(t + 1) * P, n * CW:(n + 1) * CW]
                                     ).then_inc(hres_loaded, 16)

                def load_pieces(first, n):
                    with sp.Fori(first, NU // 2) as kk:
                        for pos in range(2):
                            sp.wait_ge(w_lo[pos], kk + (LO0 + NU // 2 * n))
                            sp.dma_start(stage[:, pos, :], down_piece(2 * kk + pos, n)).then_inc(w_loaded[pos], 16)

                def store_columns(n):
                    for t in range(NT):
                        sp.wait_ge(out_ready, NT * n + t + 1)
                        sp.dma_start(out[t * P:(t + 1) * P, n * CW:(n + 1) * CW], h_res[:, t, :]
                                     ).then_inc(out_stored, 16)

                load_residual(0)
                load_pieces(1, 0)
                for pos in range(2):
                    sp.wait_ge(w_lo[pos], LO0 + NU // 2)
                    sp.dma_start(stage[:, pos, :], w_down[pos * P:(pos + 1) * P, CW:2 * CW]).then_inc(w_loaded[pos], 16)
                store_columns(0)
                sp.wait_ge(out_stored, 16 * NT)
                load_residual(1)
                load_pieces(1, 1)
                store_columns(1)
                sp.wait_ge(out_stored, 2 * 16 * NT)

            @block.tensor
            def _(pe):
                def piece_products(half_m, pos, start, stop, n):
                    wait_count = half_m + (LO0 + 1)
                    pe.wait_ge(w_lo[pos], wait_count)
                    pe.wait_ge(gs_lo_done, 2 * half_m + (pos + 1))
                    for t in range(NT):
                        if start and n == 1:
                            pe.wait_ge(out_ready, t + 1)
                        tok = slice(t * P, (t + 1) * P)
                        mm = three(pe, psum[:, t, :], (gs[0][:, pos, tok], gs[1][:, pos, tok]),
                                   (whi[:, pos, :], wlo[:, pos, :]), start, stop)
                        if stop:
                            mm.then_inc(down_done, 1)
                    if stop:
                        pe.wait_ge(down_done, NT * (n + 1))
                        pe.sem_inc(w_freed, 1)
                    else:
                        mm.then_inc(w_freed, 1)

                for n in range(2):
                    half0 = n * NU // 2
                    piece_products(half0, 0, True, False, n)
                    piece_products(half0, 1, False, False, n)
                    with pe.Fori(1, NU // 2 - 1) as kk:
                        for pos in range(2):
                            piece_products(kk + half0, pos, False, False, n)
                    piece_products(half0 + NU // 2 - 1, 0, False, False, n)
                    piece_products(half0 + NU // 2 - 1, 1, False, True, n)

            @block.scalar
            def _(act):
                for pos in range(2):
                    down_split_hi(act, 0, pos, pos, False)
                with act.Fori(1, NU // 2) as kk:
                    for pos in range(2):
                        down_split_hi(act, kk, pos, 2 * kk + pos, True)
                with act.Fori(0, NU // 2) as kk:
                    for pos in range(2):
                        down_split_hi(act, kk + NU // 2, pos, 2 * kk + pos, True)

            @block.gpsimd
            def _(pool):
                with pool.Fori(1, NU) as half_m:
                    down_lo_weight(pool, nc.gpsimd, half_m, 0)

            @block.vector
            def _(dve):
                def finish_columns(n):
                    dve.wait_ge(hres_loaded, 16 * NT * (n + 1))
                    for t in range(NT):
                        dve.wait_ge(down_done, NT * n + t + 1)
                        nc.vector.tensor_tensor(h_res[:, t, :], psum[:, t, :], h_res[:, t, :],
                                                ALU.add).then_inc(out_ready, 1)

                for pos in range(2):
                    down_lo_gated(dve, 0, pos, pos)
                with dve.Fori(1, NU // 2) as kk:
                    down_lo_gated(dve, kk, 0, 2 * kk)
                    down_lo_gated(dve, kk, 1, 2 * kk + 1)
                    down_lo_weight(dve, nc.vector, kk, 1)
                half0 = NU // 2
                down_lo_gated(dve, half0, 0, 0)
                finish_columns(0)
                down_lo_gated(dve, half0, 1, 1)
                down_lo_weight(dve, nc.vector, half0, 1)
                with dve.Fori(1, NU // 2) as kk:
                    down_lo_gated(dve, kk + half0, 0, 2 * kk)
                    down_lo_gated(dve, kk + half0, 1, 2 * kk + 1)
                    down_lo_weight(dve, nc.vector, kk + half0, 1)
                finish_columns(1)


_INS = ["x", "mem", "rel_bias_table", "attn_norm_w", "w_in", "b_gate", "q_norm_w", "k_norm_w", "w_attn_o",
        "conv_dw_w", "conv_dw_b", "conv_ln_w", "conv_ln_b", "w_conv_o", "mem_norm_w", "w_mem_kv", "xq_norm_w",
        "xk_norm_w", "w_cross_o", "w_out", "ffn_norm_w", "w_up", "ffn_conv_w", "ffn_conv_b", "w_down"]


def kernel(**inputs):
    import numpy as _np
    import concourse.bacc as _bacc
    from concourse import mybir as _mybir
    from concourse.bass_utils import run_bass_kernel_spmd as _run

    arrays = {name: _np.ascontiguousarray(inputs[name]) for name in _INS}
    arrays["identity"] = _np.eye(P, dtype=_np.float32)
    arrays["mirror"] = _np.ascontiguousarray(_np.eye(P, dtype=_np.float32)[::-1])
    arrays["bias_onehot"] = bias_constants()
    nc = _bacc.Bacc("TRN2", target_bir_lowering=False, num_devices=1)
    args = {}
    for name, a in arrays.items():
        args[name] = nc.dram_tensor("in_" + name, a.shape, _mybir.dt.from_np(a.dtype), kind="ExternalInput").ap()
    result = nc.dram_tensor("out_0", (1, S, D), _mybir.dt.float32, kind="ExternalOutput").ap()
    build(nc, out=result, **args)
    r = _run(nc, [{"in_" + name: a for name, a in arrays.items()}], core_ids=[0])
    return r.results[0]["out_0"]
```

```python
import math
from contextlib import ExitStack

import numpy as np

import concourse.bass as bass
from concourse import mybir

F32 = mybir.dt.float32
F32R = mybir.dt.float32r
ALU = mybir.AluOpType
ACT = mybir.ActivationFunctionType
AX = mybir.AxisListType

P = 128
S = 1024
D = 1024
NT = S // P
KT = D // P
CW = 512
HD = 128
NH = 4
NG = 3
DIL = (1, 4, 16)
STEPS = 128
SPACING = (1, 4, 8)
CONV_W = 31
CONV_CH = 512
FT = CONV_CH // P
N_MEM = 256
MT = N_MEM // P
D_FF = 2816
NU = D_FF // P
N_BUCKETS = 32
MAX_DISTANCE = 2048
RMS_EPS = 1e-6
LN_EPS = 1e-5
MASKED = -1e30
RING = 8
LINE = 384

V_ATTN_NORM = 0
V_MEM_NORM = V_ATTN_NORM + KT
V_FFN_NORM = V_MEM_NORM + KT
V_GATE_B = V_FFN_NORM + KT
V_QNORM = V_GATE_B + 3 * KT
V_KNORM = V_QNORM + NG
V_XQ = V_KNORM + NG
V_XK = V_XQ + 1
V_DW_B = V_XK + 1
V_LN_W = V_DW_B + FT
V_LN_B = V_LN_W + FT
ROWS_A = V_LN_B + FT
V_FB = ROWS_A
V_FW = V_FB + 2 * NU
V_DW = V_FW + 3 * 2 * NU
NV = V_DW + FT * CONV_W
assert ROWS_A + 2 * NU <= P and NV <= CW
V_QS = NV
NVECS = NV + NG + 1

SLOTS_GROUP = 3 * RING
BASE_MEM = 0
BASE_ATT = BASE_MEM + 2 * RING
BASE_CROSS = BASE_ATT + NG * SLOTS_GROUP
BASE_GLU = BASE_CROSS + RING
SLOTS_BRANCH = 3 * RING
BASE_BRANCH = BASE_GLU + 2 * RING
BASE_WOUT = BASE_BRANCH + 3 * SLOTS_BRANCH
BASE_UP = BASE_WOUT + 2 * RING
N_UP = NU // 2
BASE_DOWN = BASE_UP + N_UP * RING

COL_Q, COL_K, COL_V = 0, NG * CW, 2 * NG * CW
COL_VAL = 3 * NG * CW
COL_GLU = COL_VAL + CONV_CH
COL_XQ = COL_GLU + CONV_CH
COL_GATE = COL_XQ + CW


def bias_constants():
    onehot = np.zeros((N_BUCKETS + 1, NG * LINE), np.float32)
    exact = N_BUCKETS // 2
    for g in range(NG):
        for i in range(LINE):
            apart = 2 * STEPS - 1 - i
            d = apart * SPACING[g]
            if d < 0 or d > STEPS * DIL[g] or d % DIL[g]:
                row = N_BUCKETS
            else:
                large = exact + int(np.float32(math.log(max(d, 1) / exact) / math.log(MAX_DISTANCE / exact)
                                               * (N_BUCKETS - exact)))
                row = d if d < exact else min(large, N_BUCKETS - 1)
            onehot[row, g * LINE + i] = 1.0
    return onehot


def build(nc, x, mem, rel_bias_table, attn_norm_w, w_in, b_gate, q_norm_w, k_norm_w, w_attn_o, conv_dw_w,
          conv_dw_b, conv_ln_w, conv_ln_b, w_conv_o, mem_norm_w, w_mem_kv, xq_norm_w, xk_norm_w,
          w_cross_o, w_out, ffn_norm_w, w_up, ffn_conv_w, ffn_conv_b, w_down, identity, mirror,
          bias_onehot, out):
    x, out, mem = x[0], out[0], mem[0]
    w_in, w_mem_kv, w_out, w_up, w_down = w_in[0], w_mem_kv[0], w_out[0], w_up[0], w_down[0]
    w_branch_o = [w_cross_o[0], w_conv_o[0], w_attn_o[0]]

    ctx = ExitStack()
    with ctx:
        bottom = (nc.sbuf_base + 63) // 64 * 64

        def at(name, offset, shape, dt=F32):
            return nc.alloc_sbuf_tensor_at(name, [P] + shape, dt, offset=bottom + offset)

        slot_bytes = CW * 4
        stage = at("stage", 0, [RING, CW])
        whi = at("whi", RING * slot_bytes, [RING, CW], F32R)
        wlo = at("wlo", 2 * RING * slot_bytes, [RING, CW], F32R)
        ACTS = 3 * RING * slot_bytes
        act_hi = at("act_hi", ACTS, [KT, S], F32R)
        act_lo = at("act_lo", ACTS + KT * S * 4, [KT, S], F32R)
        SMALL = ACTS + 2 * KT * S * 4
        ident = at("ident", SMALL, [P])
        mirror_sb = at("mirror_sb", SMALL + 512, [P])
        vecs = at("vecs", SMALL + 1024, [NVECS])
        STATS = SMALL + 1024 + (NVECS * 4 + 63) // 64 * 64
        sumsq = at("sumsq", STATS, [NT])
        meansq = at("meansq", STATS + 32, [NT])
        rstd = at("rstd", STATS + 64, [2, NT])
        minus_half = at("minus_half", STATS + 128, [NT])
        softstat = at("softstat", STATS + 160, [4, 2, NH])
        recip_l = at("recip_l", STATS + 288, [2, NH])
        moments = at("moments", STATS + 320, [2, 8])
        combine_s = at("combine_s", STATS + 384, [6, NG, NH])
        row_sumsq = at("row_sumsq", STATS + 672, [NT + MT])
        row_meansq = at("row_meansq", STATS + 736, [NT + MT])
        row_scale = at("row_scale", STATS + 800, [NT + MT])
        FREE = STATS + 672 + 3 * 64

        psum = ctx.enter_context(nc.psum_tensor("psum", [P, 8, CW], F32))

        def banks(b, n=2):
            return psum[:, b:b + n, :].rearrange("p b c -> p (b c)")

        bias_lines = nc.dram_tensor("bias_lines", (NG, NH, LINE), F32).ap()
        group_out = [nc.dram_tensor(f"group_out{g}", (S, NH * HD + 2 * NH), F32).ap() for g in range(NG)]
        h_dram = nc.dram_tensor("h_scratch", (S, D), F32).ap()

        def sem(name):
            return ctx.enter_context(nc.semaphore(name))

        w_loaded = [sem(f"w_loaded{p}") for p in range(RING)]
        w_hi = sem("w_hi")
        w_lo = [sem("w_lo_even"), sem("w_lo_odd")]
        w_freed = sem("w_freed")

        def load_slot(sp, turn, pos, src, cols=None):
            if not (isinstance(turn, int) and turn == 0):
                sp.wait_ge(w_lo[pos % 2], 4 * (turn - 1) + pos // 2 + 1)
            dst = stage[:, pos, :]
            if cols:
                dst = dst.rearrange("p (h c) -> p h c", h=cols)
            sp.dma_start(dst, src).then_inc(w_loaded[pos], 16)

        def split_hi(act, turn, pos):
            act.wait_ge(w_loaded[pos], 16 * (turn + 1))
            if not (isinstance(turn, int) and turn == 0):
                act.wait_ge(w_freed, RING * (turn - 1) + pos + 1)
            nc.scalar.copy(whi[:, pos, :], stage[:, pos, :]).then_inc(w_hi, 1)

        def split_lo(eng, ops, turn, pos):
            eng.wait_ge(w_hi, RING * turn + pos + 1)
            ops.tensor_tensor(wlo[:, pos, :], stage[:, pos, :], whi[:, pos, :].bitcast(F32),
                              ALU.subtract).then_inc(w_lo[pos % 2], 1)

        def wait_slot(pe, turn, pos):
            pe.wait_ge(w_lo[pos % 2], 4 * turn + pos // 2 + 1)

        def splits_act(act, turn, first=0, end=RING):
            for pos in range(first, end):
                split_hi(act, turn, pos)

        def splits_dve(dve, turn, first=0, end=RING):
            for pos in range(first, end):
                if pos % 2:
                    split_lo(dve, nc.vector, turn, pos)

        def splits_pool(pool, turn, first=0, end=RING):
            for pos in range(first, end):
                if pos % 2 == 0:
                    split_lo(pool, nc.gpsimd, turn, pos)

        def piece(w, k, col):
            return w[k * P:(k + 1) * P, col:col + CW]

        sources = []
        for col in (0, CW):
            sources.append([piece(w_mem_kv, k, col) for k in range(KT)])
        for g in range(NG):
            for col in (COL_K, COL_V, COL_Q):
                sources.append([piece(w_in, k, col + g * CW) for k in range(KT)])
        for col in (COL_XQ, COL_GLU, COL_VAL):
            sources.append([piece(w_in, k, col) for k in range(KT)])
        for b, gate in enumerate((2, 1, 0)):
            pieces = []
            for j in range(2):
                pieces += [piece(w_in, k, COL_GATE + gate * D + j * CW) for k in range(KT)]
                pieces += [piece(w_branch_o[b], k, j * CW) for k in range(FT)]
            sources += [pieces[i * RING:(i + 1) * RING] for i in range(3)]
        for j in range(2):
            sources.append([piece(w_out, k, j * CW) for k in range(KT)])
        up_halves = w_up.rearrange("k (h c) -> k h c", h=2)
        sources.append([up_halves[k * P:(k + 1) * P, :, 0:CW // 2] for k in range(KT)])

        def load_turns(sp, first, last):
            for turn in range(first, last):
                for pos in range(RING):
                    load_slot(sp, turn, pos, sources[turn][pos], 2 if turn == BASE_UP // RING else None)

        def three(pe, dst, lhs, rhs, first, last):
            nc.tensor.matmul(dst, lhs[1], rhs[0], start=first, stop=False, skip_group_check=True)
            nc.tensor.matmul(dst, lhs[0], rhs[1], start=False, stop=False, skip_group_check=True)
            return nc.tensor.matmul(dst, lhs[0], rhs[0], start=False, stop=last, skip_group_check=True)

        gemm_done = sem("gemm_done")
        gemm_freed = sem("gemm_freed")

        def token_gemm(pe, index, turn, lhs, first, last, between=None):
            if index >= 2:
                pe.wait_ge(gemm_freed, index - 1)
            for k in range(KT):
                if first:
                    wait_slot(pe, turn, k)
                mm = three(pe, psum[:, index % 2, :], lhs(k), (whi[:, k, :], wlo[:, k, :]), k == 0, k == KT - 1)
                if last:
                    mm.then_inc(w_freed, 1)
                elif k == KT - 1:
                    mm.then_inc(gemm_done, 1)
                if between:
                    between(k)
            if last:
                pe.wait_ge(w_freed, RING * (turn + 1))
                pe.sem_inc(gemm_done, 1)

        def act_tile(tokens):
            return lambda k: (act_hi[:, k, tokens], act_lo[:, k, tokens])

        def group_tile(g, t):
            def pick(a, k):
                if g == 0:
                    return a[:, k, t * P:(t + 1) * P]
                if g == 1:
                    r, b = t // 2, t % 2
                    return a[:, k, r + b * 4 * P:r + (b + 1) * 4 * P - 3:4]
                return a[:, k, t:t + 8 * P - 7:8]
            return lambda k: (pick(act_hi, k), pick(act_lo, k))

        row_ss = sem("row_ss")
        row_ms = sem("row_ms")
        row_rstd = sem("row_rstd")
        row_scaled = sem("row_scaled")
        row_tr = sem("row_tr")
        row_hi = sem("row_hi")
        row_lo = sem("row_lo")

        class Rows:
            def __init__(self, before, rows, junk, tiles, batch, wcol, hi, lo, stat=0, banks=(4, 5, 6, 7)):
                self.rows, self.junk, self.tiles, self.batch, self.wcol = rows, junk, tiles, batch, wcol
                self.hi, self.lo, self.stat, self.banks = hi, lo, stat, banks
                self.tile0 = before.tile0 + before.tiles if before else 0
                self.batch0 = before.batch0 + before.tiles // before.batch if before else 0
                self.bank0 = before.bank0 + before.tiles // before.batch * KT if before else 0

        def rows_act_squares(act, r, which, ready):
            for t in which:
                ready(act, t)
                if r.tile0 + t >= 1:
                    act.wait_ge(row_ss, r.tile0 + t)
                nc.scalar.activation(r.junk[:], r.rows[:, t, :], ACT.Square,
                                     accum_out=row_sumsq[:, r.stat + t:r.stat + t + 1]).then_inc(row_ss, 1)

        def rows_pool(pool, r, b):
            s = slice(r.stat + b * r.batch, r.stat + (b + 1) * r.batch)
            pool.wait_ge(row_ss, r.tile0 + (b + 1) * r.batch)
            nc.gpsimd.tensor_scalar(row_meansq[:, s], row_sumsq[:, s], 1.0 / D, RMS_EPS, ALU.mult,
                                    ALU.add).then_inc(row_ms, 1)
            pool.wait_ge(row_ms, r.batch0 + b + 1)
            nc.gpsimd.tensor_tensor(row_scale[:, s], row_meansq[:, s], minus_half[:, 0:r.batch],
                                    ALU.pow).then_inc(row_rstd, 1)

        def rows_dve_scale(dve, r, b):
            dve.wait_ge(row_rstd, r.batch0 + b + 1)
            for t in range(b * r.batch, (b + 1) * r.batch):
                nc.vector.tensor_scalar(r.rows[:, t, :], r.rows[:, t, :], row_scale[:, r.stat + t:r.stat + t + 1],
                                        None, ALU.mult).then_inc(row_scaled, 1)

        def rows_pe_bank(pe, r, b, k):
            n = r.bank0 + b * KT + k
            if n >= 4:
                pe.wait_ge(row_lo, n - 3)
            for i in range(r.batch):
                mm = nc.tensor.transpose(psum[:, r.banks[n % 4], i * P:(i + 1) * P],
                                         r.rows[:, b * r.batch + i, k * P:(k + 1) * P], ident[:])
            mm.then_inc(row_tr, 1)

        def rows_pe(pe, r, b):
            pe.wait_ge(row_scaled, r.tile0 + (b + 1) * r.batch)
            for k in range(KT):
                rows_pe_bank(pe, r, b, k)

        def rows_parts(r, b, which):
            for k in which:
                n = r.bank0 + b * KT + k
                w = vecs[:, r.wcol + k:r.wcol + k + 1]
                cols = slice(b * r.batch * P, (b + 1) * r.batch * P)
                yield n, w, psum[:, r.banks[n % 4], 0:r.batch * P], r.hi[:, k, cols], r.lo[:, k, cols]

        def rows_act_hi(act, r, b, which=range(KT)):
            for n, w, src, hi, _ in rows_parts(r, b, which):
                act.wait_ge(row_tr, n + 1)
                nc.scalar.activation(hi, src, ACT.Copy, scale=w).then_inc(row_hi, 1)

        def rows_dve_lo(dve, r, b, which=range(KT)):
            for n, w, src, hi, lo in rows_parts(r, b, which):
                dve.wait_ge(row_hi, n + 1)
                nc.vector.scalar_tensor_tensor(lo, src, w, hi.bitcast(F32), ALU.mult,
                                               ALU.subtract).then_inc(row_lo, 1)

        x_junk = at("x_junk", FREE, [D])
        mem_rows = at("mem_rows", FREE + 4096, [MT, D])
        dw_rows = at("dw_rows", FREE + 12288, [CONV_CH])
        rows_a = at("rows_a", FREE + 14336, [P])
        rows_b = at("rows_b", FREE + 14848, [P])
        rows_c = at("rows_c", FREE + 15360, [P])
        table_aug = at("table_aug", FREE + 15872, [NG * NH])
        x_rows = at("x_rows", FREE + 16384, [NT, D])
        onehot_sb = at("onehot_sb", FREE + 49152, [NG * LINE])
        lines_sb = at("lines_sb", FREE + 49152 + NG * LINE * 4, [NG, LINE])
        mem_hi = at("mem_hi", FREE + 58368, [KT, N_MEM], F32R)
        mem_lo = at("mem_lo", FREE + 66560, [KT, N_MEM], F32R)
        mem_qn = at("mem_qn", FREE + 8192, [CW])
        mem_sq = at("mem_sq", FREE + 10240, [CW])
        MEM_KV = [("mk_hi", [NH, N_MEM]), ("mk_lo", [NH, N_MEM]), ("mv_hi", [MT, CW]), ("mv_lo", [MT, CW])]
        new_kv = [at("new_" + name, FREE + 74752 + i * 4096, shape, F32R) for i, (name, shape) in enumerate(MEM_KV)]
        kv_dram = [nc.dram_tensor(name, [P] + shape, F32).ap() for name, shape in MEM_KV]

        mr = Rows(None, mem_rows, x_junk, MT, MT, V_MEM_NORM, mem_hi, mem_lo, NT)
        xr = Rows(mr, x_rows, x_junk, NT, NT // 2, V_ATTN_NORM, act_hi, act_lo)
        mem_loaded = sem("mem_loaded")
        x_loaded = [sem(f"x_loaded{b}") for b in range(2)]
        params_loaded = sem("params_loaded")
        ident_loaded = sem("ident_loaded")
        masked_set = sem("masked_set")
        half_set = sem("half_set")
        params_tr = sem("params_tr")
        vecs_ready = sem("vecs_ready")
        lines_mm = sem("lines_mm")
        lines_copied = sem("lines_copied")
        lines_stored = sem("lines_stored")
        kv_stored = sem("kv_stored")
        fw = ffn_conv_w[0].rearrange("w (f p) -> (w f) p", p=P)
        param_loads = []
        row = 0
        for v, n in ((attn_norm_w, KT), (mem_norm_w, KT), (ffn_norm_w, KT), (b_gate, 3 * KT)):
            param_loads.append((v[0].rearrange("(r p) -> r p", p=P), rows_a[row:row + n, :]))
            row += n
        param_loads.append((q_norm_w[0], rows_a[row:row + NG, :]))
        param_loads.append((k_norm_w[0], rows_a[row + NG:row + 2 * NG, :]))
        row += 2 * NG
        param_loads.append((xq_norm_w, rows_a[row:row + 1, :]))
        param_loads.append((xk_norm_w, rows_a[row + 1:row + 2, :]))
        row += 2
        for v, n in ((conv_dw_b, FT), (conv_ln_w, FT), (conv_ln_b, FT), (ffn_conv_b, 2 * NU)):
            param_loads.append((v[0].rearrange("(r p) -> r p", p=P), rows_a[row:row + n, :]))
            row += n
        assert row == V_FW
        param_loads.append((fw[0:4 * NU, :], rows_b[0:4 * NU, :]))
        param_loads.append((fw[4 * NU:6 * NU, :], rows_c[0:2 * NU, :]))
        param_loads.append((conv_dw_w[0], dw_rows[0:CONV_W, :]))
        param_loads.append((rel_bias_table, table_aug[0:N_BUCKETS, :]))
        param_loads.append((bias_onehot, onehot_sb[0:N_BUCKETS + 1, :]))
        param_loads.append((mirror, mirror_sb[:]))
        PARAMS_SYNC = 9

        hn_sq = sem("hn_sq")
        hn_ss = sem("hn_ss")
        hn_ms = sem("hn_ms")
        hn_rstd = sem("hn_rstd")
        hn_tr = sem("hn_tr")
        hn_hi = sem("hn_hi")
        hn_lo = sem("hn_lo")
        s_done = sem("s_done")
        s_read = sem("s_read")
        m_done = sem("m_done")
        p_done = sem("p_done")
        p_scaled = sem("p_scaled")
        l_recip = sem("l_recip")
        tp_done = sem("tp_done")
        pt_hi_done = sem("pt_hi_done")
        pt_lo_done = sem("pt_lo_done")
        o_done = sem("o_done")
        o_read = sem("o_read")
        o_stored = [sem("o_stored_even"), sem("o_stored_odd")]
        bias_loaded = sem("bias_loaded")
        bias_flipped = sem("bias_flipped")
        bias_ready = sem("bias_ready")
        v_hi_done = sem("v_hi_done")
        kv_loaded = sem("kv_loaded")
        b_hi = sem("b_hi")
        b_lo = sem("b_lo")

        def norm_act_square(act, n, index, sq):
            act.wait_ge(gemm_done, index + 1)
            if n >= 1:
                act.wait_ge(hn_ss, n)
            nc.scalar.activation(sq[:], psum[:, index % 2, :], ACT.Square).then_inc(hn_sq, 1)

        def norm_dve_sum(dve, n, sq):
            dve.wait_ge(hn_sq, n + 1)
            nc.vector.tensor_reduce(sumsq[:, 0:NH], sq[:].rearrange("p (h d) -> p h d", h=NH), AX.X,
                                    ALU.add).then_inc(hn_ss, 1)

        def norm_pool(pool, n):
            pool.wait_ge(hn_ss, n + 1)
            nc.gpsimd.tensor_scalar(meansq[:, 0:NH], sumsq[:, 0:NH], 1.0 / HD, RMS_EPS, ALU.mult,
                                    ALU.add).then_inc(hn_ms, 1)
            pool.wait_ge(hn_ms, n + 1)
            nc.gpsimd.tensor_tensor(rstd[:, n % 2, 0:NH], meansq[:, 0:NH], minus_half[:, 0:NH],
                                    ALU.pow).then_inc(hn_rstd, 1)

        def norm_dve_scale(dve, n, index, qn):
            dve.wait_ge(hn_rstd, n + 1)
            if n >= 1:
                dve.wait_ge(hn_tr, n)
            nc.vector.tensor_tensor(qn[:].rearrange("p (h d) -> p h d", h=NH),
                                    psum[:, index % 2, :].rearrange("p (h d) -> p h d", h=NH),
                                    rstd[:, n % 2, 0:NH].unsqueeze(2).to_broadcast([P, NH, HD]),
                                    ALU.mult).then_inc(gemm_freed, 1)

        def norm_pe(pe, n, index, qn):
            pe.wait_ge(gemm_freed, index + 1)
            if n >= 1:
                pe.wait_ge(hn_lo, n)
            for h in range(NH):
                tr = nc.tensor.transpose(psum[:, 2, h * HD:(h + 1) * HD], qn[:, h * HD:(h + 1) * HD], ident[:])
            tr.then_inc(hn_tr, 1)

        bank2_heads = psum[:, 2, :].rearrange("p (h t) -> p h t", h=NH)

        def norm_act_hi(act, n, wcol, hi, free=None):
            act.wait_ge(hn_tr, n + 1)
            if free:
                act.wait_ge(*free)
            nc.scalar.activation(hi, bank2_heads, ACT.Copy, scale=vecs[:, wcol:wcol + 1]).then_inc(hn_hi, 1)

        def norm_dve_lo(dve, n, wcol, hi, lo):
            dve.wait_ge(hn_hi, n + 1)
            nc.vector.scalar_tensor_tensor(lo, bank2_heads, vecs[:, wcol:wcol + 1], hi.bitcast(F32), ALU.mult,
                                           ALU.subtract).then_inc(hn_lo, 1)

        def values_hi(act, n, index, hi):
            act.wait_ge(gemm_done, index + 1)
            nc.scalar.copy(hi, psum[:, index % 2, :]).then_inc(v_hi_done, 1)

        def values_lo(dve, n, index, hi, lo):
            dve.wait_ge(v_hi_done, n + 1)
            nc.vector.tensor_tensor(lo, psum[:, index % 2, :], hi.bitcast(F32), ALU.subtract).then_inc(gemm_freed, 1)

        mem_tiles = [lambda k, t=t: (mem_hi[:, k, t * P:(t + 1) * P], mem_lo[:, k, t * P:(t + 1) * P])
                     for t in range(MT)]

        def key_cols(a, t):
            return a[:, :, t * P:(t + 1) * P]

        with nc.Block() as block:
            @block.sync
            def _(sp):
                sp.dma_start(mem_rows[:], mem.rearrange("(t p) d -> p t d", p=P)).then_inc(mem_loaded, 16)
                sp.dma_start(ident[:], identity).then_inc(ident_loaded, 16)
                for src, dst in param_loads[:PARAMS_SYNC]:
                    sp.dma_start(dst, src).then_inc(params_loaded, 16)
                load_turns(sp, 0, 1)
                for b in range(2):
                    half = slice(b * NT // 2, (b + 1) * NT // 2)
                    sp.dma_start(x_rows[:, half, :], x.rearrange("(t p) d -> p t d", p=P)[:, half, :]
                                 ).then_inc(x_loaded[b], 16)
                load_turns(sp, 1, 2)
                sp.wait_ge(lines_copied, NG)
                sp.dma_start(bias_lines.rearrange("g h i -> h g i"), lines_sb[0:NH, :, :]).then_inc(lines_stored, 16)
                load_turns(sp, 2, 3)

            @block.scalar
            def _(act):
                for src, dst in param_loads[PARAMS_SYNC:]:
                    act.dma_start(dst, src).then_inc(params_loaded, 16)
                rows_act_squares(act, mr, range(MT), lambda e, t: e.wait_ge(mem_loaded, 16))
                act.wait_ge(vecs_ready, 1)
                rows_act_hi(act, mr, 0)
                splits_act(act, 0)
                rows_act_squares(act, xr, range(NT // 2), lambda e, t: e.wait_ge(x_loaded[0], 16))
                norm_act_square(act, 0, 0, mem_sq)
                splits_act(act, 1)
                norm_act_square(act, 1, 1, mem_sq)
                rows_act_hi(act, xr, 0)
                norm_act_hi(act, 0, V_XK, key_cols(new_kv[0], 0))
                values_hi(act, 0, MT, new_kv[2][:, 0, :])
                rows_act_squares(act, xr, range(NT // 2, NT), lambda e, t: e.wait_ge(x_loaded[1], 16))
                norm_act_hi(act, 1, V_XK, key_cols(new_kv[0], 1))
                splits_act(act, 2)
                values_hi(act, 1, MT + 1, new_kv[2][:, 1, :])

            @block.gpsimd
            def _(pool):
                pool.wait_ge(half_set, 1)
                rows_pool(pool, mr, 0)
                splits_pool(pool, 0)
                rows_pool(pool, xr, 0)
                norm_pool(pool, 0)
                splits_pool(pool, 1)
                norm_pool(pool, 1)
                rows_pool(pool, xr, 1)
                splits_pool(pool, 2)

            @block.vector
            def _(dve):
                nc.vector.memset(minus_half[:], -0.5).then_inc(half_set, 1)
                nc.vector.memset(table_aug[N_BUCKETS:N_BUCKETS + 1, :], MASKED).then_inc(masked_set, 1)
                dve.wait_ge(params_tr, 1)
                nc.vector.tensor_copy(vecs[:, 0:NV], psum[:, 0, 0:NV]).then_inc(vecs_ready, 1)
                dve.wait_ge(vecs_ready, 1)
                nc.vector.tensor_scalar(vecs[:, V_QS:V_QS + NG], vecs[:, V_QNORM:V_QNORM + NG], HD ** -0.5, None,
                                        ALU.mult).then_inc(vecs_ready, 1)
                nc.vector.tensor_scalar(vecs[:, V_QS + NG:V_QS + NG + 1], vecs[:, V_XQ:V_XQ + 1], HD ** -0.5, None,
                                        ALU.mult).then_inc(vecs_ready, 1)
                for g in range(NG):
                    dve.wait_ge(lines_mm, g + 1)
                    nc.vector.tensor_copy(lines_sb[0:NH, g, :], psum[0:NH, 1 + g, 0:LINE]).then_inc(lines_copied, 1)
                rows_dve_scale(dve, mr, 0)
                rows_dve_lo(dve, mr, 0)
                splits_dve(dve, 0)
                rows_dve_scale(dve, xr, 0)
                norm_dve_sum(dve, 0, mem_sq)
                norm_dve_scale(dve, 0, 0, mem_qn)
                splits_dve(dve, 1)
                norm_dve_sum(dve, 1, mem_sq)
                rows_dve_lo(dve, xr, 0)
                norm_dve_lo(dve, 0, V_XK, key_cols(new_kv[0], 0), key_cols(new_kv[1], 0))
                norm_dve_scale(dve, 1, 1, mem_qn)
                values_lo(dve, 0, MT, new_kv[2][:, 0, :], new_kv[3][:, 0, :])
                norm_dve_lo(dve, 1, V_XK, key_cols(new_kv[0], 1), key_cols(new_kv[1], 1))
                rows_dve_scale(dve, xr, 1)
                splits_dve(dve, 2)
                values_lo(dve, 1, MT + 1, new_kv[2][:, 1, :], new_kv[3][:, 1, :])

            @block.tensor
            def _(pe):
                pe.wait_ge(ident_loaded, 16)
                pe.wait_ge(params_loaded, 16 * len(param_loads))
                nc.tensor.transpose(psum[:, 0, 0:V_FW], rows_a[0:V_FW, :], ident[0:V_FW, 0:V_FW])
                nc.tensor.transpose(psum[:, 0, V_FW:V_FW + 4 * NU], rows_b[0:4 * NU, :], ident[0:4 * NU, 0:4 * NU])
                nc.tensor.transpose(psum[:, 0, V_FW + 4 * NU:V_DW], rows_c[0:2 * NU, :], ident[0:2 * NU, 0:2 * NU])
                for f in range(FT):
                    tr = nc.tensor.transpose(psum[:, 0, V_DW + f * CONV_W:V_DW + (f + 1) * CONV_W],
                                             dw_rows[0:CONV_W, f * P:(f + 1) * P], ident[0:CONV_W, 0:CONV_W])
                tr.then_inc(params_tr, 1)
                pe.wait_ge(masked_set, 1)
                for g in range(NG):
                    nc.tensor.matmul(psum[0:NH, 1 + g, 0:LINE], table_aug[0:N_BUCKETS + 1, g * NH:(g + 1) * NH],
                                     onehot_sb[0:N_BUCKETS + 1, g * LINE:(g + 1) * LINE],
                                     start=True, stop=True).then_inc(lines_mm, 1)
                rows_pe(pe, mr, 0)
                pe.wait_ge(vecs_ready, 1)
                pe.wait_ge(lines_copied, NG)
                pe.wait_ge(row_lo, mr.bank0 + KT)
                for t in range(MT):
                    token_gemm(pe, t, 0, mem_tiles[t], t == 0, t == MT - 1)
                pe.wait_ge(row_scaled, xr.tile0 + NT // 2)
                token_gemm(pe, MT, 1, mem_tiles[0], True, False, lambda k: rows_pe_bank(pe, xr, 0, k))
                norm_pe(pe, 0, 0, mem_qn)
                token_gemm(pe, MT + 1, 1, mem_tiles[1], False, True,
                           lambda k: norm_pe(pe, 1, 1, mem_qn) if k == KT // 2 else None)

        off = FREE
        kT = [at("k_hi", off, [NH, S], F32R), at("k_lo", off + 16384, [NH, S], F32R)]
        vT = [at("v_hi", off + 32768, [NT, CW], F32R), at("v_lo", off + 49152, [NT, CW], F32R)]
        bact = [at("bact_hi", FREE, [FT, S], F32R), at("bact_lo", FREE + 16384, [FT, S], F32R)]
        mkT = [at("mk_hi", FREE + 32768, [NH, N_MEM], F32R), at("mk_lo", FREE + 36864, [NH, N_MEM], F32R)]
        mv = [at("mv_hi", FREE + 49152, [MT, CW], F32R), at("mv_lo", FREE + 53248, [MT, CW], F32R)]
        VALUE_TILES_OVER = 2 * N_MEM * NH // CW
        off += 65536
        sq = at("sq", off, [CW])
        qn = at("qn", off + 2048, [CW])
        qT = [at("q_hi", off + 4096, [NH, P], F32R), at("q_lo", off + 6144, [NH, P], F32R)]
        sc = at("sc", off + 8192, [NH, 2 * P])
        hankel = at("hankel", off + 8192, [NH, 2 * P])
        pt = [at("pt_hi", off + 12288, [2 * NH * P], F32R), at("pt_lo", off + 16384, [2 * NH * P], F32R)]
        bias = at("bias", off + 20480, [NH, 2 * P])
        ob = at("ob", off + 24576, [2, CW])
        merged = at("merged", FREE + 32768, [KT, S])

        class Tile:
            def __init__(self, kind, g, t, i):
                self.kind, self.g, self.t = kind, g, t
                self.index = 2 * MT + i
                self.turn = BASE_ATT // RING + i // NT
                self.n = MT + 2 * NT * g + (NT if kind == "Q" else 0) + t
                self.v = MT + NT * g + t
                self.a = NT * g + t
                self.prev = kind == "Q" and (t > 0 if g == 0 else t % 2 == 1 if g == 1 else False)
                self.width = 2 * P if self.prev or kind == "X" else P
                self.qcol = V_QS + g
                self.lhs = act_tile(slice(t * P, (t + 1) * P)) if kind == "X" else group_tile(g, t)
                self.last = t == NT - 1

        tiles = []
        for g in range(NG):
            for kind in "KVQ":
                tiles += [Tile(kind, g, t, len(tiles) + t) for t in range(NT)]
        tiles += [Tile("X", NG, t, len(tiles) + t) for t in range(NT)]
        N_TILES = len(tiles)
        assert tiles[NT - 1].index == 2 * MT + NT - 1
        A_ALL = (NG + 1) * NT

        def tile_at(i, kinds):
            return tiles[i] if 0 <= i < N_TILES and tiles[i].kind in kinds else None

        def rows_of(tl):
            g, t = tl.g, tl.t
            if g == 0:
                return group_out[g][t * P:(t + 1) * P, :]
            if g == 1:
                return group_out[g].rearrange("(b p r) c -> r b p c", r=4, p=P)[t // 2, t % 2]
            return group_out[g].rearrange("(p r) c -> r p c", r=8)[t]

        per_tile = 2 * 16
        heads_scores = banks(3).rearrange("p (h c) -> p h c", h=NH)

        def bact_tile(part, t):
            return bact[part][:, :, t * P:(t + 1) * P]

        def bank_channels(b):
            return psum[:, b, :].rearrange("p (f t) -> p f t", f=FT)

        gate_done = sem("gate_done")
        sig_done = sem("sig_done")
        val_done = sem("val_done")
        prod_done = sem("prod_done")
        sum_done = sem("sum_done")

        def feature_half(pe, bank, slots, acts, f, half, first, last, done, between=None):
            for k, s in enumerate(slots):
                turn, pos = s // RING, s % RING
                if first:
                    wait_slot(pe, turn, pos)
                mm = three(pe, psum[:, bank + half, :],
                           (whi[:, pos, f * P:(f + 1) * P], wlo[:, pos, f * P:(f + 1) * P]),
                           (acts[0][:, k, half * CW:(half + 1) * CW], acts[1][:, k, half * CW:(half + 1) * CW]),
                           k == 0, k == len(slots) - 1)
                if last:
                    mm.then_inc(w_freed, 1)
                elif half == 1 and k == len(slots) - 1:
                    mm.then_inc(done, 1)
                if between:
                    between(k)
            if last:
                pe.wait_ge(w_freed, slots[-1] + 1)
                pe.sem_inc(done, 1)

        act_pair = (act_hi, act_lo)

        def gate_features(pe, before, slots, step=None, start=0):
            for f in range(start, 4):
                n = before + f
                if n >= 2:
                    pe.wait_ge(sig_done, n - 1)
                for half in range(2):
                    feature_half(pe, n % 2 * 2, slots, act_pair, f, half, f == 0 and half == 0,
                                 f == 3 and half == 1, gate_done,
                                 step and (lambda k, base=(2 * f + half) * KT: step(base + k)))

        def value_features(pe, before, slots, acts):
            for f in range(4):
                n = before + f
                if n >= 2:
                    pe.wait_ge(prod_done, n - 1)
                for half in range(2):
                    feature_half(pe, 4 + n % 2 * 2, slots, acts, f, half, f == 0 and half == 0,
                                 f == 3 and half == 1, val_done)

        PAD = CONV_W - 1
        u = at("u", FREE + 65536, [FT, S + 32])
        acc = at("acc", FREE + 65536 + FT * (S + 32) * 4, [S])
        pad_set = sem("pad_set")
        conv_done = sem("conv_done")
        turn_glu = BASE_GLU // RING
        glu_slots = range(BASE_GLU, BASE_GLU + RING)

        def conv_weight(f, tap):
            return vecs[:, V_DW + f * CONV_W + tap:V_DW + f * CONV_W + tap + 1]

        SHARED = 20
        acc_shared = at("acc_shared", FREE + 65536 + FT * (S + 32) * 4 + 4096, [S])
        shared_product = at("shared_product", FREE + 65536 + FT * (S + 32) * 4 + 8192, [S])
        shared_mult = sem("shared_mult")
        shared_added = sem("shared_added")
        F_SHARED = FT - 1

        def shared_act(act, ns):
            for n in ns:
                tap = CONV_W - 1 - n
                if n == 0:
                    act.wait_ge(pad_set, 1)
                    act.wait_ge(prod_done, FT)
                else:
                    act.wait_ge(shared_added, n)
                col = V_DW_B + F_SHARED
                nc.scalar.activation((shared_product if n else acc_shared)[:], u[:, F_SHARED, tap:tap + S],
                                     ACT.Identity, bias=0.0 if n else vecs[:, col:col + 1],
                                     scale=conv_weight(F_SHARED, tap)).then_inc(shared_mult, 1)

        def shared_pool(pool, ns):
            for n in ns:
                pool.wait_ge(shared_mult, n + 1)
                if n == 0:
                    pool.sem_inc(shared_added, 1)
                else:
                    pool.wait_ge(shared_added, n)
                    nc.gpsimd.tensor_tensor(acc_shared[:], acc_shared[:], shared_product[:],
                                            ALU.add).then_inc(shared_added, 1)

        conv_list = [(f, tap) for f in range(FT)
                     for tap in reversed(range(CONV_W - (SHARED if f == F_SHARED else 0)))]
        N_CONV = len(conv_list)

        def conv_step(dve, n):
            f, tap = conv_list[n]
            w = conv_weight(f, tap)
            if n >= 1:
                dve.wait_ge(conv_done, n)
            src = u[:, f, tap:tap + S]
            if tap == CONV_W - 1:
                dve.wait_ge(pad_set, 1)
                dve.wait_ge(prod_done, f + 1)
                step = nc.vector.tensor_scalar(acc[:], src, w, vecs[:, V_DW_B + f:V_DW_B + f + 1], ALU.mult, ALU.add)
            else:
                before = acc
                if f == F_SHARED and tap == CONV_W - 1 - SHARED:
                    dve.wait_ge(shared_added, SHARED)
                    before = acc_shared
                step = nc.vector.scalar_tensor_tensor(u[:, f, 0:S] if tap == 0 else acc[:], src, w, before[:],
                                                      ALU.mult, ALU.add)
            step.then_inc(conv_done, 1)

        conv_steps = iter(range(N_CONV))

        def conv(dve, count):
            for _, n in zip(range(count), conv_steps):
                conv_step(dve, n)

        def attention_stage():
            def sync(sp):
                sp.wait_ge(hn_lo, MT)
                sp.wait_ge(gemm_freed, 2 * MT)
                for src, dst in zip(new_kv, kv_dram):
                    sp.dma_start(dst, src[:].bitcast(F32)).then_inc(kv_stored, 16)
                for g in range(NG):
                    turn_k = BASE_ATT // RING + 3 * g
                    load_turns(sp, turn_k + 1, turn_k + 2)
                    if g >= 1:
                        sp.wait_ge(tp_done, NT * g)
                    else:
                        sp.wait_ge(lines_stored, 16)
                        sp.wait_ge(kv_stored, 16 * 4)
                    lines = bass.AP(bias_lines.tensor, g * NH * LINE, [[1, P], [LINE, NH], [1, 2 * P]])
                    sp.dma_start(hankel[:], lines).then_inc(bias_loaded, 16)
                    load_turns(sp, turn_k + 2, turn_k + 4)
                sp.wait_ge(o_done, NT * (NG - 1) + VALUE_TILES_OVER)
                for src, dst in zip(kv_dram, mkT + mv):
                    sp.dma_start(dst[:].bitcast(F32), src).then_inc(kv_loaded, 16)
                load_turns(sp, turn_glu, turn_glu + 3)

            def tensor(pe):
                for i in range(N_TILES + 4):
                    if i < N_TILES:
                        tl = tiles[i]
                        if i == NT // 2:
                            pe.wait_ge(row_lo, xr.bank0 + 2 * KT)
                        between = None
                        if 1 <= i <= 2:
                            pe.wait_ge(row_scaled, xr.tile0 + NT)
                            between = lambda k: rows_pe_bank(pe, xr, 1, (i - 1) * 4 + k // 2) if k % 2 else None
                        token_gemm(pe, tl.index, tl.turn, tl.lhs, tl.t == 0, tl.last, between)
                        if tl.kind == "V" and tl.t == 0:
                            pe.wait_ge(bias_loaded, 16 * (tl.g + 1))
                            if tl.g >= 1:
                                pe.wait_ge(s_read, NT * tl.g)
                            for j in range(2):
                                mm = nc.tensor.matmul(psum[:, 3 + j, :], mirror_sb[:],
                                                      hankel[:, 2 * j:2 * j + 2, :].rearrange("p h c -> p (h c)"),
                                                      start=True, stop=True)
                            mm.then_inc(bias_flipped, 1)
                    else:
                        j = i - N_TILES
                        if j == 2:
                            pe.wait_ge(hn_lo, tiles[-1].n + 1)
                        if j == 3:
                            pe.wait_ge(p_done, A_ALL)
                        feature_half(pe, j // 2 * 2, glu_slots, act_pair, j // 2, j % 2, j == 0, False, gate_done)
                    tl = tile_at(i - 1, "KQX")
                    if tl:
                        norm_pe(pe, tl.n, tl.index, qn)
                    tl = tile_at(i - 2, "QX")
                    if tl:
                        pe.wait_ge(hn_lo, tl.n + 1)
                        if tl.kind == "Q":
                            if tl.a >= 1:
                                pe.wait_ge(s_read, tl.a)
                            if tl.t == 0:
                                pe.wait_ge(bias_ready, tl.g + 1)
                            c0 = (tl.t - tl.prev) * P
                            keys = [k[:, :, c0:c0 + tl.width] for k in kT]
                        else:
                            if tl.t == 0:
                                pe.wait_ge(s_read, tl.a)
                                pe.wait_ge(kv_loaded, 16 * 4)
                            else:
                                pe.wait_ge(p_done, tl.a)
                            keys = [k[:] for k in mkT]
                        for h in range(NH):
                            mm = three(pe, banks(3)[:, h * 256:h * 256 + tl.width], (qT[0][:, h, :], qT[1][:, h, :]),
                                       (keys[0][:, h, :], keys[1][:, h, :]), True, True)
                        mm.then_inc(s_done, 1)
                    tl = tile_at(i - 3, "QX")
                    if tl:
                        if tl.kind == "Q":
                            pe.wait_ge(p_done, tl.a + 1)
                        else:
                            pe.wait_ge(p_scaled, tl.t + 1)
                        if tl.a >= 1:
                            pe.wait_ge(pt_lo_done, tl.a)
                        for h in range(NH):
                            for kt in range(tl.width // P):
                                c = (h * tl.width // P + kt) * P
                                tr = nc.tensor.transpose(banks(5)[:, c:c + P], sc[:, h, kt * P:(kt + 1) * P], ident[:])
                        tr.then_inc(tp_done, 1)
                    tl = tile_at(i - 4, "QX")
                    if tl:
                        pe.wait_ge(pt_lo_done, tl.a + 1)
                        if tl.kind == "Q" or tl.t == 0:
                            if tl.a >= 1:
                                pe.wait_ge(o_read, tl.a)
                        else:
                            pe.wait_ge(b_lo, tl.t)
                        for h in range(NH):
                            for j in range(tl.width // P):
                                c = (h * tl.width // P + j) * P
                                probs = [part[:, c:c + P] for part in pt]
                                if tl.kind == "Q":
                                    vals = [part[:, tl.t - tl.prev + j, h * HD:(h + 1) * HD] for part in vT]
                                    lhs, rhs = probs, vals
                                else:
                                    vals = [part[:, j, h * HD:(h + 1) * HD] for part in mv]
                                    lhs, rhs = vals, probs
                                mm = three(pe, psum[:, 7, h * HD:(h + 1) * HD], lhs, rhs, j == 0,
                                           j == tl.width // P - 1)
                        mm.then_inc(o_done, 1)
                gate_features(pe, 0, glu_slots, start=2)
                pe.wait_ge(b_lo, NT)
                pe.wait_ge(pt_lo_done, A_ALL)
                value_features(pe, 0, range(BASE_GLU + RING, BASE_GLU + 2 * RING), act_pair)

            def glu_sigmoid(act, f):
                act.wait_ge(gate_done, f + 1)
                nc.scalar.activation(merged[:, f, :], banks(f % 2 * 2), ACT.Sigmoid).then_inc(sig_done, 1)

            def scalar(act):
                for i in range(N_TILES + 5):
                    tl = tile_at(i, "KVQX")
                    if tl:
                        if 1 <= i <= 2:
                            rows_act_hi(act, xr, 1, range(4 * i - 4, 4 * i))
                        if tl.last:
                            splits_act(act, tl.turn + 1, 0, RING - 1)
                        if tl.kind == "V":
                            if tl.t == 0 and tl.g:
                                act.wait_ge(o_done, tl.a)
                            values_hi(act, tl.v, tl.index, vT[0][:, tl.t, :])
                        else:
                            norm_act_square(act, tl.n, tl.index, sq)
                        if tl.last:
                            splits_act(act, tl.turn + 1, RING - 1)
                    tl = tile_at(i - 1, "K")
                    if tl:
                        free = (s_done, NT * tl.g if tl.t else NT * (tl.g - 1) + 2) if tl.g else None
                        norm_act_hi(act, tl.n, V_KNORM + tl.g, key_cols(kT[0], tl.t), free)
                    tl = tile_at(i - 1, "QX")
                    if tl:
                        norm_act_hi(act, tl.n, tl.qcol, qT[0][:], (s_done, tl.a) if tl.a else None)
                    tl = tile_at(i - 2, "QX")
                    if tl:
                        act.wait_ge(m_done, tl.a + 1)
                        src = sc
                        if tl.kind == "X":
                            act.wait_ge(tp_done, tl.a)
                            src = heads_scores
                        for h in range(NH):
                            e = nc.scalar.activation(sc[:, h, 0:tl.width], src[:, h, 0:tl.width], ACT.Exp,
                                                     bias=softstat[:, tl.a % 4, 1, h:h + 1],
                                                     accum_out=softstat[:, tl.a % 4, 0, h:h + 1])
                        e.then_inc(p_done, 1)
                    tl = tile_at(i - 3, "QX")
                    if tl:
                        act.wait_ge(tp_done, tl.a + 1)
                        if tl.a >= 1:
                            act.wait_ge(o_done, tl.a)
                        c = NH * tl.width
                        nc.scalar.copy(pt[0][:, 0:c], banks(5)[:, 0:c]).then_inc(pt_hi_done, 1)
                    tl = tile_at(i - 5, "Q")
                    if tl:
                        act.wait_ge(o_read, tl.a + 1)
                        dst = rows_of(tl)
                        act.dma_start(dst[:, 0:CW], ob[:, tl.t % 2, :]).then_inc(o_stored[tl.t % 2], 16)
                        act.dma_start(dst[:, CW:], softstat[:, tl.a % 4, :, :].rearrange(
                            "p a h -> p (a h)")).then_inc(o_stored[tl.t % 2], 16)
                    tl = tile_at(i - 4, "Q")
                    if tl:
                        act.wait_ge(o_done, tl.a + 1)
                        if tl.a >= 2:
                            act.wait_ge(o_stored[tl.a % 2], per_tile * (tl.a // 2))
                        nc.scalar.copy(ob[:, tl.t % 2, :], psum[:, 7, :]).then_inc(o_read, 1)
                    tl = tile_at(i - 4, "X")
                    if tl:
                        act.wait_ge(o_done, tl.a + 1)
                        nc.scalar.copy(bact_tile(0, tl.t), bank_channels(7)).then_inc(b_hi, 1)
                    if i == N_TILES + 2:
                        act.wait_ge(s_done, A_ALL)
                        glu_sigmoid(act, 0)
                glu_sigmoid(act, 1)
                for j in range(2):
                    act.wait_ge(o_stored[j], per_tile * NG * NT // 2)
                glu_sigmoid(act, 2)
                splits_act(act, turn_glu + 1)
                glu_sigmoid(act, 3)
                splits_act(act, turn_glu + 2)

            def gpsimd(pool):
                for tl in tiles:
                    if tl.last:
                        splits_pool(pool, tl.turn + 1)
                    if tl.kind != "V":
                        norm_pool(pool, tl.n)
                splits_pool(pool, turn_glu + 1)
                splits_pool(pool, turn_glu + 2)

            def vector(dve):
                for i in range(N_TILES + 4):
                    tl = tile_at(i, "KVQX")
                    if tl:
                        if 1 <= i <= 2:
                            rows_dve_lo(dve, xr, 1, range(4 * i - 4, 4 * i))
                        if tl.last:
                            splits_dve(dve, tl.turn + 1, 0, RING - 1)
                        if tl.kind == "V":
                            values_lo(dve, tl.v, tl.index, vT[0][:, tl.t, :], vT[1][:, tl.t, :])
                        else:
                            norm_dve_sum(dve, tl.n, sq)
                        if tl.last:
                            splits_dve(dve, tl.turn + 1, RING - 1)
                        if tl.kind == "V" and tl.t == 1:
                            dve.wait_ge(bias_flipped, tl.g + 1)
                            nc.vector.tensor_copy(bias[:].rearrange("p h c -> p (h c)"),
                                                  banks(3)).then_inc(bias_ready, 1)
                    tl = tile_at(i - 1, "K")
                    if tl:
                        norm_dve_lo(dve, tl.n, V_KNORM + tl.g, key_cols(kT[0], tl.t), key_cols(kT[1], tl.t))
                    tl = tile_at(i - 1, "QX")
                    if tl:
                        norm_dve_lo(dve, tl.n, tl.qcol, qT[0][:], qT[1][:])
                    tl = tile_at(i - 2, "QX")
                    if tl:
                        dve.wait_ge(s_done, tl.a + 1)
                        src = heads_scores
                        if tl.a >= 4 and tl.a - 4 < NG * NT:
                            dve.wait_ge(o_stored[tl.a % 2], per_tile * ((tl.a - 4) // 2 + 1))
                        if tl.kind == "Q":
                            if tl.a >= 1:
                                dve.wait_ge(tp_done, tl.a)
                            if tl.t == 0:
                                dve.wait_ge(bias_ready, tl.g + 1)
                            src = sc[:, :, 0:tl.width]
                            nc.vector.tensor_tensor(src, heads_scores[:, :, 0:tl.width], bias[:, :, 2 * P - tl.width:],
                                                    ALU.add).then_inc(s_read, 1)
                            dve.wait_ge(s_read, tl.a + 1)
                        nc.vector.tensor_reduce(softstat[:, tl.a % 4, 1, :], src, AX.X, ALU.max,
                                                negate=True).then_inc(m_done, 1)
                    tl = tile_at(i, "KQX")
                    if tl:
                        norm_dve_scale(dve, tl.n, tl.index, qn)
                    tl = tile_at(i - 3, "QX")
                    if tl:
                        c = NH * tl.width
                        dve.wait_ge(pt_hi_done, tl.a + 1)
                        nc.vector.tensor_tensor(pt[1][:, 0:c], banks(5)[:, 0:c], pt[0][:, 0:c].bitcast(F32),
                                                ALU.subtract).then_inc(pt_lo_done, 1)
                    tl = tile_at(i - 2, "X")
                    if tl:
                        dve.wait_ge(p_done, tl.a + 1)
                        nc.vector.reciprocal(recip_l[:, tl.a % 2, :], softstat[:, tl.a % 4, 0, :]).then_inc(l_recip, 1)
                        dve.wait_ge(l_recip, tl.t + 1)
                        nc.vector.tensor_tensor(sc[:], sc[:],
                                                recip_l[:, tl.a % 2, :].unsqueeze(2).to_broadcast([P, NH, N_MEM]),
                                                ALU.mult).then_inc(p_scaled, 1)
                    tl = tile_at(i - 4, "X")
                    if tl:
                        dve.wait_ge(b_hi, tl.t + 1)
                        nc.vector.tensor_tensor(bact_tile(1, tl.t), bank_channels(7), bact_tile(0, tl.t).bitcast(F32),
                                                ALU.subtract).then_inc(b_lo, 1)
                nc.vector.memset(u[:, :, 0:PAD], 0.0).then_inc(pad_set, 1)
                splits_dve(dve, turn_glu + 1)
                for f in range(4):
                    if f == 3:
                        splits_dve(dve, turn_glu + 2)
                    dve.wait_ge(sig_done, f + 1)
                    dve.wait_ge(val_done, f + 1)
                    nc.vector.tensor_tensor(u[:, f, PAD:PAD + S], banks(4 + f % 2 * 2), merged[:, f, :],
                                            ALU.mult).then_inc(prod_done, 1)
                    if f < 3:
                        conv(dve, 8)

            return sync, tensor, scalar, gpsimd, vector

        gbuf = at("gbuf", FREE + 65536, [4, S])
        off = FREE + 65536 + FT * (S + 32) * 4
        nrm = at("nrm", off, [CW])
        swz = at("swz", off + 2048, [FT, P])
        sws = at("sws", off + 4096, [FT, P])
        grp = at("grp", FREE + 65536 + 16384, [2, NG, CW])
        gstat = at("gstat", FREE + 65536 + 3 * S * 4, [NG, NT, 2 * NH])
        c_low, c_total, c_recip = (at(name, FREE + 65536 + 3 * S * 4 + 768 + i * 128, [NT, NH])
                                   for i, name in enumerate(("c_low", "c_total", "c_recip")))
        c_shift, c_exp, c_le, c_f = (at(name, FREE + 65536 + 3 * S * 4 + 1152 + i * 384, [NG, NT, NH])
                                     for i, name in enumerate(("c_shift", "c_exp", "c_le", "c_f")))

        ln_tr = sem("ln_tr")
        ln_stats = sem("ln_stats")
        ln_aggr = sem("ln_aggr")
        ln_eps = sem("ln_eps")
        ln_rstd = sem("ln_rstd")
        ln_normed = sem("ln_normed")
        ln_back = sem("ln_back")
        sw_z = sem("sw_z")
        sw_sig = sem("sw_sig")
        sw_done = sem("sw_done")
        grp_loaded = [sem("grp_loaded_even"), sem("grp_loaded_odd")]
        gstat_loaded = sem("gstat_loaded")
        cmb_min = sem("cmb_min")
        cmb_first = sem("cmb_first")
        cmb_exp = sem("cmb_exp")
        cmb_step = sem("cmb_step")
        cmb_done = sem("cmb_done")
        cmb_tr = sem("cmb_tr")

        def channels_norm_pe(pe, s):
            if s % 6 == 0 and s // 6 < NT:
                q = s // 6
                if q == 0:
                    pe.wait_ge(conv_done, N_CONV)
                    pe.wait_ge(prod_done, 4 + KT)
                else:
                    pe.wait_ge(ln_normed, q - 1)
                for f in range(FT):
                    tr = nc.tensor.transpose(psum[:, 4 + q % 2, f * P:(f + 1) * P], u[:, f, q * P:(q + 1) * P], ident[:])
                tr.then_inc(ln_tr, 1)
            if s % 6 == 3 and 0 <= s // 6 - 1 < NT:
                t = s // 6 - 1
                pe.wait_ge(ln_normed, t + 1)
                if t >= 2:
                    pe.wait_ge(sw_sig, t - 1)
                for f in range(FT):
                    tr = nc.tensor.transpose(psum[:, 6 + t % 2, f * P:(f + 1) * P], nrm[:, f * P:(f + 1) * P], ident[:])
                tr.then_inc(ln_back, 1)

        def channels_norm_dve(dve, q):
            if q < NT:
                m = moments[:, q % 2, :]
                dve.wait_ge(ln_tr, q + 1)
                nc.vector.bn_stats(combine_s[:, 0:1, :, 0:2], psum[:, 4 + q % 2, :]).then_inc(ln_stats, 1)
                dve.wait_ge(ln_stats, q + 1)
                nc.vector.bn_aggr(m[:, 0:2], combine_s[:, 0:1, :, 0:2]).then_inc(ln_aggr, 1)
            if q >= 2:
                t = q - 2
                dve.wait_ge(sw_sig, t + 1)
                nc.vector.tensor_tensor(swz[:], swz[:], sws[:], ALU.mult).then_inc(sw_done, 1)
                dve.wait_ge(b_hi, NT + t + 1)
                nc.vector.tensor_tensor(bact_tile(1, t), swz[:], bact_tile(0, t).bitcast(F32),
                                        ALU.subtract).then_inc(b_lo, 1)
            if q < NT:
                dve.wait_ge(ln_rstd, q + 1)
                if q >= 1:
                    dve.wait_ge(ln_back, q)
                nc.vector.tensor_scalar(nrm[:], psum[:, 4 + q % 2, :], m[:, 0:1], m[:, 3:4], ALU.subtract,
                                        ALU.mult).then_inc(ln_normed, 1)

        def channels_norm_pool(pool, q):
            if q < NT:
                m = moments[:, q % 2, :]
                pool.wait_ge(ln_aggr, q + 1)
                nc.gpsimd.tensor_scalar(m[:, 2:3], m[:, 1:2], 1.0, LN_EPS, ALU.mult, ALU.add).then_inc(ln_eps, 1)
                pool.wait_ge(ln_eps, q + 1)
                nc.gpsimd.tensor_tensor(m[:, 3:4], m[:, 2:3], minus_half[:, 0:1], ALU.pow).then_inc(ln_rstd, 1)

        def channels_norm_act(act, q):
            if q >= 1 and q <= NT:
                t = q - 1
                act.wait_ge(ln_back, t + 1)
                if t >= 1:
                    act.wait_ge(b_lo, NT + t)
                for f in range(FT):
                    w, b = (vecs[:, v + f:v + f + 1] for v in (V_LN_W, V_LN_B))
                    src = psum[:, 6 + t % 2, f * P:(f + 1) * P]
                    z = nc.scalar.activation(swz[:, f, :], src, ACT.Identity, bias=b, scale=w)
                    s = nc.scalar.activation(sws[:, f, :], src, ACT.Sigmoid, bias=b, scale=w)
                s.then_inc(sw_sig, 1)
                act.wait_ge(sw_done, t + 1)
                nc.scalar.copy(bact_tile(0, t), swz[:]).then_inc(b_hi, 1)

        def groups_mean_sync(sp):
            for j in range(2):
                sp.wait_ge(o_stored[j], per_tile * NG * NT // 2)
            sp.wait_ge(sum_done, KT)
            for g in range(NG):
                sp.dma_start(gstat[:, g], group_out[g].rearrange("(t p) c -> p t c", p=P)[:, :, CW:]
                             ).then_inc(gstat_loaded, 16)
            for t in range(NT):
                if t >= 2:
                    sp.wait_ge(cmb_tr, t - 1)
                for g in range(NG):
                    sp.dma_start(grp[:, t % 2, g, :], group_out[g][t * P:(t + 1) * P, 0:CW]
                                 ).then_inc(grp_loaded[t % 2], 16)

        def group_weights_dve(dve):
            def chained(ins, n):
                ins.then_inc(cmb_step, 1)
                dve.wait_ge(cmb_step, n)

            def each(a):
                return a[:].unsqueeze(1).to_broadcast([P, NG, NT, NH])
            dve.wait_ge(gstat_loaded, 16 * NG)
            sums, neg = gstat[:, :, :, 0:NH], gstat[:, :, :, NH:]
            chained(nc.vector.tensor_tensor(c_low[:], neg[:, 0], neg[:, 1], ALU.min), 1)
            chained(nc.vector.tensor_tensor(c_low[:], c_low[:], neg[:, 2], ALU.min), 2)
            for g in range(NG):
                last = nc.vector.tensor_tensor(c_shift[:, g], c_low[:], neg[:, g], ALU.subtract)
            last.then_inc(cmb_min, 1)
            dve.wait_ge(cmb_exp, 1)
            for g in range(NG):
                last = nc.vector.tensor_tensor(c_le[:, g], c_exp[:, g], sums[:, g], ALU.mult)
            chained(last, 3)
            chained(nc.vector.tensor_tensor(c_total[:], c_le[:, 0], c_le[:, 1], ALU.add), 4)
            chained(nc.vector.tensor_tensor(c_total[:], c_total[:], c_le[:, 2], ALU.add), 5)
            chained(nc.vector.reciprocal(c_recip[:], c_total[:]), 6)
            for g in range(NG):
                last = nc.vector.tensor_tensor(c_f[:, g], c_exp[:, g], c_recip[:], ALU.mult)
            last.then_inc(cmb_weights, 1)

        def groups_mean_dve(dve, q):
            if q == 0:
                group_weights_dve(dve)
                dve.wait_ge(cmb_weights, 1)
            if q < NT:
                dve.wait_ge(cmb_first, q + 1)
                mean = grp[:, q % 2, 0, :]
                for g in (1, 2):
                    if g == 2:
                        dve.wait_ge(cmb_part, q + 1)
                    for h in range(NH):
                        cols = slice(h * HD, (h + 1) * HD)
                        last = nc.vector.scalar_tensor_tensor(mean[:, cols], grp[:, q % 2, g, cols],
                                                              c_f[:, g, q, h:h + 1], mean[:, cols], ALU.mult, ALU.add)
                    last.then_inc(cmb_part if g == 1 else cmb_done, 1)
            if 1 <= q <= NT:
                t = q - 1
                dve.wait_ge(b_hi, 2 * NT + t + 1)
                nc.vector.tensor_tensor(bact_tile(1, t), bank_channels(4 + t % 2), bact_tile(0, t).bitcast(F32),
                                        ALU.subtract).then_inc(b_lo, 1)

        def groups_mean_act(act, q):
            if q == 0:
                act.wait_ge(cmb_min, 1)
                nc.scalar.activation(c_exp[:], c_shift[:], ACT.Exp).then_inc(cmb_exp, 1)
                act.wait_ge(cmb_weights, 1)
            if q < NT:
                act.wait_ge(grp_loaded[q % 2], 16 * NG * (q // 2 + 1))
                for h in range(NH):
                    cols = grp[:, q % 2, 0, h * HD:(h + 1) * HD]
                    last = nc.scalar.activation(cols, cols, ACT.Copy, scale=c_f[:, 0, q, h:h + 1])
                last.then_inc(cmb_first, 1)
            if 1 <= q <= NT:
                t = q - 1
                act.wait_ge(cmb_tr, t + 1)
                nc.scalar.copy(bact_tile(0, t), bank_channels(4 + t % 2)).then_inc(b_hi, 1)

        def groups_mean_pe(pe, s):
            if s >= 16 and (s - 16) % 5 == 0 and (s - 16) // 5 < NT:
                t = (s - 16) // 5
                pe.wait_ge(cmb_done, t + 1)
                if t >= 2:
                    pe.wait_ge(b_lo, 2 * NT + t - 1)
                else:
                    pe.wait_ge(prod_done, 4 + 2 * KT)
                for h in range(NH):
                    tr = nc.tensor.transpose(psum[:, 4 + t % 2, h * P:(h + 1) * P],
                                             grp[:, t % 2, 0, h * P:(h + 1) * P], ident[:])
                tr.then_inc(cmb_tr, 1)

        cmb_part = sem("cmb_part")
        cmb_weights = sem("cmb_weights")
        PREP_STEPS = NT + 2
        SIGMOID_AFTER = (2, 5, 7)
        NOTHING = (lambda e, q: None,) * 4
        prepare = [NOTHING, (channels_norm_pe, channels_norm_act, channels_norm_dve, channels_norm_pool),
                   (groups_mean_pe, groups_mean_act, groups_mean_dve, lambda e, q: None)]

        m_hi = sem("m_hi")
        m_lo = sem("m_lo")

        def merged_hi(act, ks):
            for k in ks:
                act.wait_ge(gate_done, 4 + 3 * KT)
                act.wait_ge(sum_done, KT + k + 1)
                nc.scalar.copy(act_hi[:, k, :], merged[:, k, :]).then_inc(m_hi, 1)

        def merged_lo(dve, ks):
            for k in ks:
                dve.wait_ge(m_hi, k + 1)
                nc.vector.tensor_tensor(act_lo[:, k, :], merged[:, k, :], act_hi[:, k, :].bitcast(F32),
                                        ALU.subtract).then_inc(m_lo, 1)

        def branch_stage(b, gate):
            first = BASE_BRANCH + b * SLOTS_BRANCH
            turn = first // RING
            gates = [range(first, first + 8), range(first + 12, first + 20)]
            outs = [range(first + 8, first + 12), range(first + 20, first + 24)]
            before = 4 + b * KT

            def quarters(a):
                return a.rearrange("p (a c) -> p a c", c=S // 4)

            def sig_at(f):
                if b == 0:
                    return quarters(merged[:, f, :])
                if b == 1:
                    return u[:, :, f % 4 * 2 * P:(f % 4 * 2 + 2) * P]
                return quarters(gbuf[:, f % 4, :])
            prep_pe, prep_act, prep_dve, prep_pool = prepare[b]

            def pair(n, base=0):
                return banks(base + n % 2 * 2)

            def split_range(eng, ops, s0, s1):
                for s in range(s0, s1):
                    t, pos = (first + s) // RING, (first + s) % RING
                    if ops is None:
                        split_hi(eng, t, pos)
                    elif (pos % 2 == 0) == (ops is nc.gpsimd):
                        split_lo(eng, ops, t, pos)

            def sync(sp):
                if b == 2:
                    groups_mean_sync(sp)
                load_turns(sp, turn + 1, turn + 4)

            def tensor(pe):
                gate_features(pe, before, gates[0], lambda s: prep_pe(pe, s))
                pe.wait_ge(b_lo, NT * (b + 1))
                value_features(pe, before, outs[0], bact)
                gate_features(pe, before + 4, gates[1])
                value_features(pe, before + 4, outs[1], bact)

            def gate_sigmoid(act, f):
                n = before + f
                act.wait_ge(gate_done, n + 1)
                if b == 0 and f < 4:
                    act.wait_ge(prod_done, f + 1)
                if b == 2 and f < 4:
                    act.wait_ge(sum_done, KT)
                    if f == 3:
                        act.wait_ge(cmb_done, NT)
                if b >= 1 and f >= 4:
                    act.wait_ge(prod_done, n - 3)
                    act.wait_ge(sum_done, (b - 1) * KT + f - 3)
                if b == 1 and f < 4:
                    act.wait_ge(ln_tr, 2 * f + 2)
                col = V_GATE_B + gate * KT + f
                nc.scalar.activation(sig_at(f), quarters(pair(n)), ACT.Sigmoid, bias=vecs[:, col:col + 1]).then_inc(sig_done, 1)

            def scalar(act):
                for q in range(PREP_STEPS):
                    prep_act(act, q)
                    if b == 0 and q < NT:
                        shared_act(act, [q])
                    if q in SIGMOID_AFTER:
                        gate_sigmoid(act, SIGMOID_AFTER.index(q))
                split_range(act, None, 8, 16)
                gate_sigmoid(act, 3)
                if b == 0:
                    shared_act(act, range(8, 12))
                split_range(act, None, 16, 20)
                for f in range(4, KT):
                    if b == 0:
                        shared_act(act, range(3 * f, min(3 * f + 3, SHARED)))
                    if f == KT - 1:
                        split_range(act, None, 20, 28)
                    gate_sigmoid(act, f)
                if b == 2:
                    merged_hi(act, range(KT - 1))
                split_range(act, None, 28, 32)
                if b == 2:
                    merged_hi(act, [KT - 1])

            def gpsimd(pool):
                for q in range(NT):
                    prep_pool(pool, q)
                    if b == 0:
                        shared_pool(pool, [q])
                split_range(pool, nc.gpsimd, 8, 16)
                if b == 0:
                    shared_pool(pool, range(8, 12))
                split_range(pool, nc.gpsimd, 16, 20)
                if b == 0:
                    shared_pool(pool, range(12, SHARED))
                split_range(pool, nc.gpsimd, 20, 32)

            def branch_product(dve, f):
                n = before + f
                dve.wait_ge(sig_done, n + 1)
                dve.wait_ge(val_done, n + 1)
                nc.vector.tensor_tensor(sig_at(f), quarters(pair(n, 4)), sig_at(f), ALU.mult).then_inc(prod_done, 1)
                if b >= 1:
                    dve.wait_ge(prod_done, n + 1)
                    nc.vector.tensor_tensor(quarters(merged[:, f, :]), quarters(merged[:, f, :]), sig_at(f),
                                            ALU.add).then_inc(sum_done, 1)

            def vector(dve):
                for q in range(PREP_STEPS):
                    prep_dve(dve, q)
                    if b == 0 and q < NT:
                        conv(dve, 4 if q < NT - 1 else 2)
                split_range(dve, nc.vector, 8, 16)
                for f in range(0, 4):
                    if f == 3:
                        split_range(dve, nc.vector, 16, 20)
                    branch_product(dve, f)
                    if b == 0:
                        conv(dve, 3)
                if b == 0:
                    conv(dve, 31)
                split_range(dve, nc.vector, 20, 28)
                for f in range(4, KT):
                    if f == KT - 1:
                        if b == 0:
                            conv(dve, N_CONV)
                        if b == 2:
                            merged_lo(dve, [KT - 2])
                        split_range(dve, nc.vector, 28, 32)
                    branch_product(dve, f)
                    if b == 0 and f < KT - 1:
                        conv(dve, 1)
                    if b == 2:
                        merged_lo(dve, range(2 * f - 8, 2 * f - 6) if f < KT - 1 else [KT - 1])

            return sync, tensor, scalar, gpsimd, vector

        h_rows = at("h_rows", FREE, [NT, D])
        h_junk = at("h_junk", FREE + 65536, [D])
        H_BATCH = 2
        h_batches = range(NT // H_BATCH)
        res_loaded = [[sem(f"res_loaded{j}{b}") for b in h_batches] for j in range(2)]
        h_stored = [sem(f"h_stored{b}") for b in h_batches]
        turn_o = BASE_WOUT // RING
        io = 2 * MT + N_TILES
        hr = Rows(xr, h_rows, h_junk, NT, H_BATCH, V_FFN_NORM, act_hi, act_lo, banks=(2, 3, 6, 7))
        T_UP = BASE_UP // RING
        T_DOWN = BASE_DOWN // RING

        def w_out_stage():
            def sync(sp):
                sp.wait_ge(val_done, 4 + 3 * KT)
                for j in range(2):
                    for b in h_batches:
                        rows, cols = slice(b * H_BATCH, (b + 1) * H_BATCH), slice(j * CW, (j + 1) * CW)
                        sp.dma_start(h_rows[:, rows, cols], x.rearrange("(t p) d -> p t d", p=P)[:, rows, cols]
                                     ).then_inc(res_loaded[j][b], 16)
                load_turns(sp, turn_o + 1, turn_o + 3)

            def tensor(pe):
                pe.wait_ge(sig_done, 4 + 3 * KT)
                for j in range(2):
                    for t in range(NT):
                        tile = act_tile(slice(t * P, (t + 1) * P))
                        between = None
                        if j == 0 and t == 0:
                            def lhs(k, tile=tile):
                                pe.wait_ge(m_lo, k + 1)
                                return tile(k)
                        else:
                            lhs = tile
                        if j == 1 and t in (4, 6):
                            b = t // 2 - 2
                            pe.wait_ge(row_scaled, hr.tile0 + (b + 1) * H_BATCH)
                            between = lambda k: rows_pe_bank(pe, hr, b, k)
                        token_gemm(pe, io + j * NT + t, turn_o + j, lhs, t == 0, t == NT - 1, between)

            def scalar(act):
                splits_act(act, turn_o + 1)
                for t in range(NT):
                    if t in (4, 6):
                        rows_act_hi(act, hr, t // 2 - 2)
                    if t == NT - 1:
                        splits_act(act, turn_o + 2)
                    act.wait_ge(gemm_freed, io + NT + t + 1)
                    act.dma_start(h_dram[t * P:(t + 1) * P, :], h_rows[:, t, :]).then_inc(h_stored[t // H_BATCH], 16)
                    rows_act_squares(act, hr, [t], lambda e, t: None)
                for b in (2, 3):
                    rows_act_hi(act, hr, b)

            def gpsimd(pool):
                splits_pool(pool, turn_o + 1)
                for b in range(3):
                    rows_pool(pool, hr, b)
                splits_pool(pool, turn_o + 2)
                rows_pool(pool, hr, 3)

            def vector(dve):
                def scale(b):
                    dve.wait_ge(h_stored[b], 16 * H_BATCH)
                    rows_dve_scale(dve, hr, b)

                for j in range(2):
                    for t in range(NT):
                        if j == 1 and t == 4:
                            scale(0)
                            rows_dve_lo(dve, hr, 0)
                        if j == 1 and t == 6:
                            scale(1)
                            rows_dve_lo(dve, hr, 1)
                        if t == NT - 1:
                            if j == 1:
                                scale(2)
                            splits_dve(dve, turn_o + 1 + j)
                        n = io + j * NT + t
                        cols = slice(j * CW, (j + 1) * CW)
                        dve.wait_ge(gemm_done, n + 1)
                        if t % H_BATCH == 0:
                            dve.wait_ge(res_loaded[j][t // H_BATCH], 16)
                        nc.vector.tensor_tensor(h_rows[:, t, cols], psum[:, n % 2, :], h_rows[:, t, cols],
                                                ALU.add).then_inc(gemm_freed, 1)
                rows_dve_lo(dve, hr, 2, range(6))
                scale(3)
                rows_dve_lo(dve, hr, 2, range(6, KT))
                rows_dve_lo(dve, hr, 3)

            return sync, tensor, scalar, gpsimd, vector

        gated = at("gated", FREE, [NU, S])
        value = at("value", FREE + NU * S * 4, [S])
        wait_met = sem("wait_met")
        up_done = sem("up_done")
        pairs_free = sem("pairs_free")
        base_done = sem("base_done")
        tap_done = sem("tap_done")
        silu_done = sem("silu_done")
        value_free = sem("value_free")

        def up_param(base, kind, U):
            col = base + kind * NU + U
            return vecs[:, bass.ds(col, 1)]

        def up_dst(kind, U):
            return gated[:, U, :] if kind else value[:]

        def met(act):
            act.sem_inc(wait_met, 1)

        def up_base(act, kind, U, i):
            act.wait_ge(up_done, 2 * U + (1 if kind else 2))
            if not kind:
                act.wait_ge(value_free, U + 1)
            met(act)
            nc.scalar.activation(up_dst(kind, U), banks((0 if kind else 4) + 2 * i), ACT.Identity,
                                 bias=up_param(V_FB, kind, U), scale=up_param(V_FW + 4 * NU, kind, U)
                                 ).then_inc(base_done, 1)

        def up_silu(act, U):
            act.wait_ge(pairs_free, 4 + 2 * U + 1)
            met(act)
            nc.scalar.activation(gated[:, U, :], gated[:, U, :], ACT.Silu).then_inc(silu_done, 1)

        def up_taps(dve, kind, U, i):
            src, dst = banks((0 if kind else 4) + 2 * i), up_dst(kind, U)
            dve.wait_ge(base_done, 2 * U + (1 if kind else 2))
            nc.vector.scalar_tensor_tensor(dst[:, 1:], src[:, 0:S - 1], up_param(V_FW + 2 * NU, kind, U), dst[:, 1:],
                                           ALU.mult, ALU.add).then_inc(tap_done, 1)
            dve.wait_ge(tap_done, 2 * U + (1 if kind else 2))
            nc.vector.scalar_tensor_tensor(dst[:, 2:], src[:, 0:S - 2], up_param(V_FW, kind, U), dst[:, 2:],
                                           ALU.mult, ALU.add).then_inc(pairs_free, 1)

        def up_product(dve, U):
            dve.wait_ge(silu_done, U + 1)
            dve.wait_ge(pairs_free, 4 + 2 * U + 2)
            nc.vector.tensor_tensor(gated[:, U, :], gated[:, U, :], value[:], ALU.mult).then_inc(value_free, 1)

        def up_chunk_act(act, c, between):
            for i in range(2):
                U = 2 * c + i
                up_base(act, 1, U, i)
                if i == 1:
                    between(act)
                up_base(act, 0, U, i)
                up_silu(act, U)

        def up_chunk_dve(dve, c, between, before_product=None):
            for i in range(2):
                U = 2 * c + i
                up_taps(dve, 1, U, i)
                if i == 1:
                    between(dve)
                up_taps(dve, 0, U, i)
                if i == 1 and before_product:
                    before_product(dve)
                up_product(dve, U)

        def down_piece(k, n):
            return w_down[bass.ds(k * P, P), n * CW:(n + 1) * CW]

        gs = [[at("gs_hi0", 2 * slot_bytes, [S], F32R), at("gs_hi1", 4 * slot_bytes, [S], F32R)],
              [at("gs_lo0", 6 * slot_bytes, [S], F32R), at("gs_lo1", ACTS, [S], F32R)]]
        h_res = at("h_res", ACTS + S * 4, [NT, D])
        gs_hi_done = sem("gs_hi_done")
        gs_lo_done = sem("gs_lo_done")
        hres_loaded = sem("hres_loaded")
        down_done = sem("down_done")
        out_ready = sem("out_ready")
        out_stored = sem("out_stored")
        LO0, FREED0 = 4 * T_DOWN, BASE_DOWN

        def down_split_hi(act, half_m, pos, k, with_weight):
            if with_weight:
                act.wait_ge(w_freed, 2 * half_m + (pos - 1 + FREED0))
                met(act)
            nc.scalar.copy(gs[0][pos][:], gated[:, k, :]).then_inc(gs_hi_done, 1)
            if with_weight:
                act.wait_ge(w_loaded[pos], 16 * half_m + 16 * (T_DOWN + 1))
                nc.scalar.copy(whi[:, pos, :], stage[:, pos, :]).then_inc(w_hi, 1)

        def down_lo_gated(dve, half_m, pos, k):
            dve.wait_ge(gs_hi_done, 2 * half_m + (pos + 1))
            nc.vector.tensor_tensor(gs[1][pos][:], gated[:, k, :], gs[0][pos][:].bitcast(F32),
                                    ALU.subtract).then_inc(gs_lo_done, 1)

        def down_lo_weight(eng, ops, half_m, pos):
            eng.wait_ge(w_hi, 2 * half_m + (FREED0 + pos + 1))
            ops.tensor_tensor(wlo[:, pos, :], stage[:, pos, :], whi[:, pos, :].bitcast(F32),
                              ALU.subtract).then_inc(w_lo[pos], 1)

        def up_stage():
            def sync(sp):
                with sp.Fori(0, N_UP - 1) as c:
                    for pos in range(RING):
                        load_slot(sp, c + (T_UP + 1), pos,
                                  up_halves[pos * P:(pos + 1) * P, :, bass.ds((c + 1) * (CW // 2), CW // 2)], 2)
                for pos in range(2):
                    load_slot(sp, T_DOWN, pos, w_down[pos * P:(pos + 1) * P, 0:CW])

            def up_half(pe, c, i, kind, half, between=None):
                last = i == 1 and kind == 0 and half == 1
                for k in range(KT):
                    if i == 0 and kind == 1 and half == 0:
                        wait_slot(pe, c + T_UP, k)
                    cols = slice((2 * kind + i) * P, (2 * kind + i + 1) * P)
                    mm = three(pe, psum[:, (0 if kind else 4) + 2 * i + half, :],
                               (whi[:, k, cols], wlo[:, k, cols]),
                               (act_hi[:, k, half * CW:(half + 1) * CW],
                                act_lo[:, k, half * CW:(half + 1) * CW]), k == 0, k == KT - 1)
                    if last:
                        mm.then_inc(w_freed, 1)
                    elif half == 1 and k == KT - 1:
                        mm.then_inc(up_done, 1)
                    if between:
                        between(k)
                if last:
                    pe.wait_ge(w_freed, RING * c + (BASE_UP + RING))
                    pe.sem_inc(up_done, 1)

            def tensor(pe):
                pe.wait_ge(row_lo, hr.bank0 + 2 * KT)
                pe.wait_ge(gemm_freed, io + 2 * NT - 1)
                for b, kind in ((2, 1), (3, 0)):
                    pe.wait_ge(row_scaled, hr.tile0 + (b + 1) * H_BATCH)
                    up_half(pe, 0, 0, kind, 0, lambda k: rows_pe_bank(pe, hr, b, k))
                pe.wait_ge(row_lo, hr.bank0 + len(h_batches) * KT)
                pe.wait_ge(gemm_freed, io + 2 * NT)
                for kind in (1, 0):
                    up_half(pe, 0, 0, kind, 1)
                for kind in (1, 0):
                    for half in range(2):
                        up_half(pe, 0, 1, kind, half)
                with pe.Fori(1, N_UP) as c:
                    for i in range(2):
                        for kind in (1, 0):
                            pe.wait_ge(pairs_free, 4 * c + (2 * i + 2 - kind))
                            for half in range(2):
                                up_half(pe, c, i, kind, half)

            def scalar(act):
                with act.Fori(0, N_UP - 1) as c:
                    up_chunk_act(act, c, lambda e: splits_act(e, c + (T_UP + 1)))

                def first_pieces(act):
                    for parity in range(2):
                        act.wait_ge(w_lo[parity], LO0)
                    for pos in range(2):
                        down_split_hi(act, 0, pos, pos, False)
                    splits_act(act, T_DOWN, 0, 2)
                up_chunk_act(act, N_UP - 1, first_pieces)

            def gpsimd(pool):
                with pool.Fori(0, N_UP - 1) as c:
                    splits_pool(pool, c + (T_UP + 1))
                splits_pool(pool, T_DOWN, 0, 2)

            def vector(dve):
                dve.sem_inc(pairs_free, 4)
                dve.sem_inc(value_free, 1)
                with dve.Fori(0, N_UP - 1) as c:
                    up_chunk_dve(dve, c, lambda e: splits_dve(e, c + (T_UP + 1)))

                def first_piece(dve):
                    down_lo_gated(dve, 0, 0, 0)
                    splits_dve(dve, T_DOWN, 0, 2)
                up_chunk_dve(dve, N_UP - 1, first_piece, lambda e: down_lo_gated(e, 0, 1, 1))

            return sync, tensor, scalar, gpsimd, vector

        def down_stage():
            def sync(sp):
                def load_pieces(kk, n):
                    for pos in range(2):
                        sp.wait_ge(w_lo[pos], kk + (LO0 + NU // 2 * n))
                        sp.dma_start(stage[:, pos, :], down_piece(2 * kk + pos, n)).then_inc(w_loaded[pos], 16)

                def load_residual(t):
                    sp.dma_start(h_res[:, t, :], h_dram[t * P:(t + 1) * P, :]).then_inc(hres_loaded, 16)

                def store_columns(n):
                    for t in range(NT):
                        sp.wait_ge(out_ready, NT * n + t + 1)
                        sp.dma_start(out[t * P:(t + 1) * P, n * CW:(n + 1) * CW],
                                     h_res[:, t, n * CW:(n + 1) * CW]).then_inc(out_stored, 16)

                load_pieces(1, 0)
                sp.wait_ge(up_done, 2 * NU)
                for b in h_batches:
                    sp.wait_ge(h_stored[b], 16 * H_BATCH)
                for t in range(NT):
                    load_residual(t)
                    load_pieces(t + 2, 0)
                with sp.Fori(NT + 2, NU // 2) as kk:
                    load_pieces(kk, 0)
                for pos in range(2):
                    sp.wait_ge(w_lo[pos], LO0 + NU // 2)
                    sp.dma_start(stage[:, pos, :], w_down[pos * P:(pos + 1) * P, CW:2 * CW]).then_inc(w_loaded[pos], 16)
                load_pieces(1, 1)
                store_columns(0)
                with sp.Fori(2, NU // 2) as kk:
                    load_pieces(kk, 1)
                store_columns(1)
                sp.wait_ge(out_stored, 2 * 16 * NT)

            def tensor(pe):
                def piece_products(half_m, pos, start, stop, n):
                    wait_count = half_m + (LO0 + 1)
                    pe.wait_ge(w_lo[pos], wait_count)
                    pe.wait_ge(gs_lo_done, 2 * half_m + (pos + 1))
                    for t in range(NT):
                        if start and n == 0 and t % 2 == 0:
                            pe.wait_ge(pairs_free, 2 * NU + (1, 3, 2, 4)[t // 2])
                        if start and n == 1:
                            pe.wait_ge(out_ready, t + 1)
                        tok = slice(t * P, (t + 1) * P)
                        mm = three(pe, psum[:, t, :], (gs[0][pos][:, tok], gs[1][pos][:, tok]),
                                   (whi[:, pos, :], wlo[:, pos, :]), start, stop)
                        if stop:
                            mm.then_inc(down_done, 1)
                    if stop:
                        pe.wait_ge(down_done, NT * (n + 1))
                        pe.sem_inc(w_freed, 1)
                    else:
                        mm.then_inc(w_freed, 1)

                for n in range(2):
                    half0 = n * NU // 2
                    piece_products(half0, 0, True, False, n)
                    piece_products(half0, 1, False, False, n)
                    with pe.Fori(1, NU // 2 - 1) as kk:
                        for pos in range(2):
                            piece_products(kk + half0, pos, False, False, n)
                    piece_products(half0 + NU // 2 - 1, 0, False, False, n)
                    piece_products(half0 + NU // 2 - 1, 1, False, True, n)

            def scalar(act):
                act.wait_ge(value_free, NU + 1)
                with act.Fori(1, NU // 2) as kk:
                    for pos in range(2):
                        down_split_hi(act, kk, pos, 2 * kk + pos, True)
                with act.Fori(0, NU // 2) as kk:
                    for pos in range(2):
                        down_split_hi(act, kk + NU // 2, pos, 2 * kk + pos, True)

            def gpsimd(pool):
                with pool.Fori(1, NU) as half_m:
                    down_lo_weight(pool, nc.gpsimd, half_m, 0)

            def vector(dve):
                def finish_columns(n):
                    dve.wait_ge(hres_loaded, 16 * NT)
                    for t in range(NT):
                        dve.wait_ge(down_done, NT * n + t + 1)
                        cols = h_res[:, t, n * CW:(n + 1) * CW]
                        nc.vector.tensor_tensor(cols, psum[:, t, :], cols, ALU.add).then_inc(out_ready, 1)

                with dve.Fori(1, NU // 2) as kk:
                    down_lo_gated(dve, kk, 0, 2 * kk)
                    down_lo_gated(dve, kk, 1, 2 * kk + 1)
                    down_lo_weight(dve, nc.vector, kk, 1)
                half0 = NU // 2
                down_lo_gated(dve, half0, 0, 0)
                finish_columns(0)
                down_lo_gated(dve, half0, 1, 1)
                down_lo_weight(dve, nc.vector, half0, 1)
                with dve.Fori(1, NU // 2) as kk:
                    down_lo_gated(dve, kk + half0, 0, 2 * kk)
                    down_lo_gated(dve, kk + half0, 1, 2 * kk + 1)
                    down_lo_weight(dve, nc.vector, kk + half0, 1)
                finish_columns(1)

            return sync, tensor, scalar, gpsimd, vector

        stages = [attention_stage()] + [branch_stage(b, gate) for b, gate in enumerate((2, 1, 0))]
        stages += [w_out_stage(), up_stage(), down_stage()]

        with nc.Block() as block:
            @block.sync
            def _(sp):
                for sync, _, _, _, _ in stages:
                    sync(sp)

            @block.tensor
            def _(pe):
                for _, tensor, _, _, _ in stages:
                    tensor(pe)

            @block.scalar
            def _(act):
                for _, _, scalar, _, _ in stages:
                    scalar(act)

            @block.gpsimd
            def _(pool):
                for _, _, _, gpsimd, _ in stages:
                    gpsimd(pool)

            @block.vector
            def _(dve):
                for _, _, _, _, vector in stages:
                    vector(dve)


_INS = ["x", "mem", "rel_bias_table", "attn_norm_w", "w_in", "b_gate", "q_norm_w", "k_norm_w", "w_attn_o",
        "conv_dw_w", "conv_dw_b", "conv_ln_w", "conv_ln_b", "w_conv_o", "mem_norm_w", "w_mem_kv", "xq_norm_w",
        "xk_norm_w", "w_cross_o", "w_out", "ffn_norm_w", "w_up", "ffn_conv_w", "ffn_conv_b", "w_down"]


def kernel(**inputs):
    import numpy as _np
    import concourse.bacc as _bacc
    from concourse import mybir as _mybir
    from concourse.bass_utils import run_bass_kernel_spmd as _run

    arrays = {name: _np.ascontiguousarray(inputs[name]) for name in _INS}
    arrays["identity"] = _np.eye(P, dtype=_np.float32)
    arrays["mirror"] = _np.ascontiguousarray(_np.eye(P, dtype=_np.float32)[::-1])
    arrays["bias_onehot"] = bias_constants()
    nc = _bacc.Bacc("TRN2", target_bir_lowering=False, num_devices=1)
    args = {}
    for name, a in arrays.items():
        args[name] = nc.dram_tensor("in_" + name, a.shape, _mybir.dt.from_np(a.dtype), kind="ExternalInput").ap()
    result = nc.dram_tensor("out_0", (1, S, D), _mybir.dt.float32, kind="ExternalOutput").ap()
    build(nc, out=result, **args)
    r = _run(nc, [{"in_" + name: a for name, a in arrays.items()}], core_ids=[0])
    return r.results[0]["out_0"]
```

```python
import math
from contextlib import ExitStack

import numpy as np

import concourse.bass as bass
from concourse import mybir

F32 = mybir.dt.float32
F32R = mybir.dt.float32r
ALU = mybir.AluOpType
ACT = mybir.ActivationFunctionType
AX = mybir.AxisListType

P = 128
S = 1024
D = 1024
NT = S // P
KT = D // P
CW = 512
HD = 128
NH = 4
NG = 3
DIL = (1, 4, 16)
STEPS = 128
SPACING = (1, 4, 8)
CONV_W = 31
CONV_CH = 512
FT = CONV_CH // P
N_MEM = 256
MT = N_MEM // P
D_FF = 2816
NU = D_FF // P
N_BUCKETS = 32
MAX_DISTANCE = 2048
RMS_EPS = 1e-6
LN_EPS = 1e-5
MASKED = -1e30
RING = 8
LINE = 384

V_ATTN_NORM = 0
V_MEM_NORM = V_ATTN_NORM + KT
V_FFN_NORM = V_MEM_NORM + KT
V_GATE_B = V_FFN_NORM + KT
V_QNORM = V_GATE_B + 3 * KT
V_KNORM = V_QNORM + NG
V_XQ = V_KNORM + NG
V_XK = V_XQ + 1
V_DW_B = V_XK + 1
V_LN_W = V_DW_B + FT
V_LN_B = V_LN_W + FT
ROWS_A = V_LN_B + FT
V_FB = ROWS_A
V_FW = V_FB + 2 * NU
V_DW = V_FW + 3 * 2 * NU
NV = V_DW + FT * CONV_W
assert ROWS_A + 2 * NU <= P and NV <= CW
V_QS = NV
NVECS = NV + NG + 1

SLOTS_GROUP = 3 * RING
BASE_MEM = 0
BASE_ATT = BASE_MEM + 2 * RING
BASE_CROSS = BASE_ATT + NG * SLOTS_GROUP
BASE_GLU = BASE_CROSS + RING
SLOTS_BRANCH = 3 * RING
BASE_BRANCH = BASE_GLU + 2 * RING
BASE_WOUT = BASE_BRANCH + 3 * SLOTS_BRANCH
BASE_UP = BASE_WOUT + 2 * RING
N_UP = NU // 2
BASE_DOWN = BASE_UP + N_UP * RING

COL_Q, COL_K, COL_V = 0, NG * CW, 2 * NG * CW
COL_VAL = 3 * NG * CW
COL_GLU = COL_VAL + CONV_CH
COL_XQ = COL_GLU + CONV_CH
COL_GATE = COL_XQ + CW


def bias_constants():
    onehot = np.zeros((N_BUCKETS + 1, NG * LINE), np.float32)
    exact = N_BUCKETS // 2
    for g in range(NG):
        for i in range(LINE):
            apart = 2 * STEPS - 1 - i
            d = apart * SPACING[g]
            if d < 0 or d > STEPS * DIL[g] or d % DIL[g]:
                row = N_BUCKETS
            else:
                large = exact + int(np.float32(math.log(max(d, 1) / exact) / math.log(MAX_DISTANCE / exact)
                                               * (N_BUCKETS - exact)))
                row = d if d < exact else min(large, N_BUCKETS - 1)
            onehot[row, g * LINE + i] = 1.0
    return onehot


def build(nc, x, mem, rel_bias_table, attn_norm_w, w_in, b_gate, q_norm_w, k_norm_w, w_attn_o, conv_dw_w,
          conv_dw_b, conv_ln_w, conv_ln_b, w_conv_o, mem_norm_w, w_mem_kv, xq_norm_w, xk_norm_w,
          w_cross_o, w_out, ffn_norm_w, w_up, ffn_conv_w, ffn_conv_b, w_down, identity, mirror,
          bias_onehot, out):
    x, out, mem = x[0], out[0], mem[0]
    w_in, w_mem_kv, w_out, w_up, w_down = w_in[0], w_mem_kv[0], w_out[0], w_up[0], w_down[0]
    w_branch_o = [w_cross_o[0], w_conv_o[0], w_attn_o[0]]

    ctx = ExitStack()
    with ctx:
        bottom = (nc.sbuf_base + 63) // 64 * 64

        def at(name, offset, shape, dt=F32):
            return nc.alloc_sbuf_tensor_at(name, [P] + shape, dt, offset=bottom + offset)

        slot_bytes = CW * 4
        stage = at("stage", 0, [RING, CW])
        whi = at("whi", RING * slot_bytes, [RING, CW], F32R)
        wlo = at("wlo", 2 * RING * slot_bytes, [RING, CW], F32R)
        ACTS = 3 * RING * slot_bytes
        act_hi = at("act_hi", ACTS, [KT, S], F32R)
        act_lo = at("act_lo", ACTS + KT * S * 4, [KT, S], F32R)
        SMALL = ACTS + 2 * KT * S * 4
        ident = at("ident", SMALL, [P])
        mirror_sb = at("mirror_sb", SMALL + 512, [P])
        vecs = at("vecs", SMALL + 1024, [NVECS])
        STATS = SMALL + 1024 + (NVECS * 4 + 63) // 64 * 64
        sumsq = at("sumsq", STATS, [NT])
        meansq = at("meansq", STATS + 32, [NT])
        rstd = at("rstd", STATS + 64, [2, NT])
        minus_half = at("minus_half", STATS + 128, [NT])
        softstat = at("softstat", STATS + 160, [4, 2, NH])
        recip_l = at("recip_l", STATS + 288, [2, NH])
        moments = at("moments", STATS + 320, [2, 8])
        combine_s = at("combine_s", STATS + 384, [6, NG, NH])
        row_sumsq = at("row_sumsq", STATS + 672, [NT + MT])
        row_meansq = at("row_meansq", STATS + 736, [NT + MT])
        row_scale = at("row_scale", STATS + 800, [NT + MT])
        FREE = STATS + 672 + 3 * 64

        psum = ctx.enter_context(nc.psum_tensor("psum", [P, 8, CW], F32))

        def banks(b, n=2):
            return psum[:, b:b + n, :].rearrange("p b c -> p (b c)")

        bias_lines = nc.dram_tensor("bias_lines", (NG, NH, LINE), F32).ap()
        group_out = [nc.dram_tensor(f"group_out{g}", (S, NH * HD + 2 * NH), F32).ap() for g in range(NG)]
        h_dram = nc.dram_tensor("h_scratch", (S, D), F32).ap()

        def sem(name):
            return ctx.enter_context(nc.semaphore(name))

        w_loaded = [sem(f"w_loaded{p}") for p in range(RING)]
        w_hi = sem("w_hi")
        w_lo = [sem("w_lo_even"), sem("w_lo_odd")]
        w_freed = sem("w_freed")

        def load_slot(sp, turn, pos, src, cols=None):
            if not (isinstance(turn, int) and turn == 0):
                sp.wait_ge(w_lo[pos % 2], 4 * (turn - 1) + pos // 2 + 1)
            dst = stage[:, pos, :]
            if cols:
                dst = dst.rearrange("p (h c) -> p h c", h=cols)
            sp.dma_start(dst, src).then_inc(w_loaded[pos], 16)

        def split_hi(act, turn, pos):
            act.wait_ge(w_loaded[pos], 16 * (turn + 1))
            if not (isinstance(turn, int) and turn == 0):
                act.wait_ge(w_freed, RING * (turn - 1) + pos + 1)
            nc.scalar.copy(whi[:, pos, :], stage[:, pos, :]).then_inc(w_hi, 1)

        def split_lo(eng, ops, turn, pos):
            eng.wait_ge(w_hi, RING * turn + pos + 1)
            ops.tensor_tensor(wlo[:, pos, :], stage[:, pos, :], whi[:, pos, :].bitcast(F32),
                              ALU.subtract).then_inc(w_lo[pos % 2], 1)

        def wait_slot(pe, turn, pos):
            pe.wait_ge(w_lo[pos % 2], 4 * turn + pos // 2 + 1)

        def splits_act(act, turn, first=0, end=RING):
            for pos in range(first, end):
                split_hi(act, turn, pos)

        def splits_dve(dve, turn, first=0, end=RING):
            for pos in range(first, end):
                if pos % 2:
                    split_lo(dve, nc.vector, turn, pos)

        def splits_pool(pool, turn, first=0, end=RING):
            for pos in range(first, end):
                if pos % 2 == 0:
                    split_lo(pool, nc.gpsimd, turn, pos)

        def piece(w, k, col):
            return w[k * P:(k + 1) * P, col:col + CW]

        sources = []
        for col in (0, CW):
            sources.append([piece(w_mem_kv, k, col) for k in range(KT)])
        for g in range(NG):
            for col in (COL_K, COL_V, COL_Q):
                sources.append([piece(w_in, k, col + g * CW) for k in range(KT)])
        for col in (COL_XQ, COL_GLU, COL_VAL):
            sources.append([piece(w_in, k, col) for k in range(KT)])
        for b, gate in enumerate((2, 1, 0)):
            pieces = []
            for j in range(2):
                pieces += [piece(w_in, k, COL_GATE + gate * D + j * CW) for k in range(KT)]
                pieces += [piece(w_branch_o[b], k, j * CW) for k in range(FT)]
            sources += [pieces[i * RING:(i + 1) * RING] for i in range(3)]
        for j in range(2):
            sources.append([piece(w_out, k, j * CW) for k in range(KT)])
        up_halves = w_up.rearrange("k (h c) -> k h c", h=2)
        sources.append([up_halves[k * P:(k + 1) * P, :, 0:CW // 2] for k in range(KT)])

        def load_turns(sp, first, last):
            for turn in range(first, last):
                for pos in range(RING):
                    load_slot(sp, turn, pos, sources[turn][pos], 2 if turn == BASE_UP // RING else None)

        def three(pe, dst, lhs, rhs, first, last):
            nc.tensor.matmul(dst, lhs[1], rhs[0], start=first, stop=False, skip_group_check=True)
            nc.tensor.matmul(dst, lhs[0], rhs[1], start=False, stop=False, skip_group_check=True)
            return nc.tensor.matmul(dst, lhs[0], rhs[0], start=False, stop=last, skip_group_check=True)

        gemm_done = sem("gemm_done")
        gemm_freed = sem("gemm_freed")

        def token_gemm(pe, index, turn, lhs, first, last, between=None):
            if index >= 2:
                pe.wait_ge(gemm_freed, index - 1)
            for k in range(KT):
                if first:
                    wait_slot(pe, turn, k)
                mm = three(pe, psum[:, index % 2, :], lhs(k), (whi[:, k, :], wlo[:, k, :]), k == 0, k == KT - 1)
                if last:
                    mm.then_inc(w_freed, 1)
                elif k == KT - 1:
                    mm.then_inc(gemm_done, 1)
                if between:
                    between(k)

        def wait_gemm(eng, index):
            if index < 2 * MT:
                chunk, last = index // MT, index % MT == MT - 1
            else:
                chunk, last = 2 + (index - 2 * MT) // NT, (index - 2 * MT) % NT == NT - 1
            turn = chunk if chunk < BASE_GLU // RING else chunk + (BASE_WOUT - BASE_GLU) // RING
            if last:
                eng.wait_ge(w_freed, RING * (turn + 1))
            else:
                eng.wait_ge(gemm_done, index + 1 - chunk)

        def act_tile(tokens):
            return lambda k: (act_hi[:, k, tokens], act_lo[:, k, tokens])

        def group_tile(g, t):
            def pick(a, k):
                if g == 0:
                    return a[:, k, t * P:(t + 1) * P]
                if g == 1:
                    r, b = t // 2, t % 2
                    return a[:, k, r + b * 4 * P:r + (b + 1) * 4 * P - 3:4]
                return a[:, k, t:t + 8 * P - 7:8]
            return lambda k: (pick(act_hi, k), pick(act_lo, k))

        row_ss = sem("row_ss")
        row_ms = sem("row_ms")
        row_rstd = sem("row_rstd")
        row_scaled = sem("row_scaled")
        row_tr = sem("row_tr")
        row_hi = sem("row_hi")
        row_lo = sem("row_lo")

        class Rows:
            def __init__(self, before, rows, junk, tiles, batch, wcol, hi, lo, stat=0, banks=lambda b: (4, 5, 6, 7)):
                self.rows, self.junk, self.tiles, self.batch, self.wcol = rows, junk, tiles, batch, wcol
                self.hi, self.lo, self.stat, self.banks = hi, lo, stat, banks
                self.tile0 = before.tile0 + before.tiles if before else 0
                self.batch0 = before.batch0 + before.tiles // before.batch if before else 0
                self.bank0 = before.bank0 + before.tiles // before.batch * KT if before else 0

            def bank(self, b, k):
                return self.banks(b)[k % 4]

        def rows_act_squares(act, r, which, ready):
            for t in which:
                ready(act, t)
                if r.tile0 + t >= 1:
                    act.wait_ge(row_ss, r.tile0 + t)
                nc.scalar.activation(r.junk[:], r.rows[:, t, :], ACT.Square,
                                     accum_out=row_sumsq[:, r.stat + t:r.stat + t + 1]).then_inc(row_ss, 1)

        def rows_pool(pool, r, b):
            s = slice(r.stat + b * r.batch, r.stat + (b + 1) * r.batch)
            pool.wait_ge(row_ss, r.tile0 + (b + 1) * r.batch)
            nc.gpsimd.tensor_scalar(row_meansq[:, s], row_sumsq[:, s], 1.0 / D, RMS_EPS, ALU.mult,
                                    ALU.add).then_inc(row_ms, 1)
            pool.wait_ge(row_ms, r.batch0 + b + 1)
            nc.gpsimd.tensor_tensor(row_scale[:, s], row_meansq[:, s], minus_half[:, 0:r.batch],
                                    ALU.pow).then_inc(row_rstd, 1)

        def rows_dve_scale(dve, r, b):
            dve.wait_ge(row_rstd, r.batch0 + b + 1)
            for t in range(b * r.batch, (b + 1) * r.batch):
                nc.vector.tensor_scalar(r.rows[:, t, :], r.rows[:, t, :], row_scale[:, r.stat + t:r.stat + t + 1],
                                        None, ALU.mult).then_inc(row_scaled, 1)

        def rows_pe_bank(pe, r, b, k):
            n = r.bank0 + b * KT + k
            if n >= 4:
                pe.wait_ge(row_lo, n - 3)
            if r.bank(b, k) < 2:
                pe.wait_ge(gemm_freed, io + 2 * NT)
            for i in range(r.batch):
                mm = nc.tensor.transpose(psum[:, r.bank(b, k), i * P:(i + 1) * P],
                                         r.rows[:, b * r.batch + i, k * P:(k + 1) * P], ident[:])
            mm.then_inc(row_tr, 1)

        def rows_parts(r, b, which):
            for k in which:
                n = r.bank0 + b * KT + k
                w = vecs[:, r.wcol + k:r.wcol + k + 1]
                cols = slice(b * r.batch * P, (b + 1) * r.batch * P)
                yield n, w, psum[:, r.bank(b, k), 0:r.batch * P], r.hi[:, k, cols], r.lo[:, k, cols]

        def rows_act_hi(act, r, b, which=range(KT)):
            for n, w, src, hi, _ in rows_parts(r, b, which):
                act.wait_ge(row_tr, n + 1)
                nc.scalar.activation(hi, src, ACT.Copy, scale=w).then_inc(row_hi, 1)

        def rows_dve_lo(dve, r, b, which=range(KT)):
            for n, w, src, hi, lo in rows_parts(r, b, which):
                dve.wait_ge(row_hi, n + 1)
                nc.vector.scalar_tensor_tensor(lo, src, w, hi.bitcast(F32), ALU.mult,
                                               ALU.subtract).then_inc(row_lo, 1)

        x_junk = at("x_junk", FREE, [D])
        mem_rows = at("mem_rows", FREE + 4096, [MT, D])
        dw_rows = at("dw_rows", FREE + 12288, [CONV_CH])
        rows_a = at("rows_a", FREE + 14336, [P])
        rows_b = at("rows_b", FREE + 14848, [P])
        rows_c = at("rows_c", FREE + 15360, [P])
        table_aug = at("table_aug", FREE + 15872, [NG * NH])
        x_rows = at("x_rows", FREE + 16384, [NT, D])
        onehot_sb = at("onehot_sb", FREE + 49152, [NG * LINE])
        lines_sb = at("lines_sb", FREE + 49152 + NG * LINE * 4, [NG, LINE])
        mem_hi = at("mem_hi", FREE + 58368, [KT, N_MEM], F32R)
        mem_lo = at("mem_lo", FREE + 66560, [KT, N_MEM], F32R)
        mem_qn = at("mem_qn", FREE + 8192, [CW])
        mem_sq = at("mem_sq", FREE + 10240, [CW])
        MEM_KV = [("mk_hi", [NH, N_MEM]), ("mk_lo", [NH, N_MEM]), ("mv_hi", [MT, CW]), ("mv_lo", [MT, CW])]
        new_kv = [at("new_" + name, FREE + 74752 + i * 4096, shape, F32R) for i, (name, shape) in enumerate(MEM_KV)]
        kv_dram = [nc.dram_tensor(name, [P] + shape, F32).ap() for name, shape in MEM_KV]

        mr = Rows(None, mem_rows, x_junk, MT, MT, V_MEM_NORM, mem_hi, mem_lo, NT)
        xr = Rows(mr, x_rows, x_junk, NT, NT // 2, V_ATTN_NORM, act_hi, act_lo)
        mem_loaded = sem("mem_loaded")
        x_loaded = [sem(f"x_loaded{b}") for b in range(2)]
        params_loaded = sem("params_loaded")
        bias_params_loaded = sem("bias_params_loaded")
        ident_loaded = sem("ident_loaded")
        masked_set = sem("masked_set")
        half_set = sem("half_set")
        params_tr = sem("params_tr")
        vecs_ready = sem("vecs_ready")
        lines_mm = sem("lines_mm")
        lines_copied = sem("lines_copied")
        lines_stored = sem("lines_stored")
        kv_stored = sem("kv_stored")
        fw = ffn_conv_w[0].rearrange("w (f p) -> (w f) p", p=P)
        param_loads = []
        row = 0
        for v, n in ((attn_norm_w, KT), (mem_norm_w, KT), (ffn_norm_w, KT), (b_gate, 3 * KT)):
            param_loads.append((v[0].rearrange("(r p) -> r p", p=P), rows_a[row:row + n, :]))
            row += n
        param_loads.append((q_norm_w[0], rows_a[row:row + NG, :]))
        param_loads.append((k_norm_w[0], rows_a[row + NG:row + 2 * NG, :]))
        row += 2 * NG
        param_loads.append((xq_norm_w, rows_a[row:row + 1, :]))
        param_loads.append((xk_norm_w, rows_a[row + 1:row + 2, :]))
        row += 2
        for v, n in ((conv_dw_b, FT), (conv_ln_w, FT), (conv_ln_b, FT), (ffn_conv_b, 2 * NU)):
            param_loads.append((v[0].rearrange("(r p) -> r p", p=P), rows_a[row:row + n, :]))
            row += n
        assert row == V_FW
        param_loads.append((fw[0:4 * NU, :], rows_b[0:4 * NU, :]))
        param_loads.append((fw[4 * NU:6 * NU, :], rows_c[0:2 * NU, :]))
        param_loads.append((conv_dw_w[0], dw_rows[0:CONV_W, :]))
        bias_param_loads = [(rel_bias_table, table_aug[0:N_BUCKETS, :]), (bias_onehot, onehot_sb[0:N_BUCKETS + 1, :]),
                            (mirror, mirror_sb[:])]

        hn_sq = sem("hn_sq")
        hn_ss = sem("hn_ss")
        hn_ms = sem("hn_ms")
        hn_rstd = sem("hn_rstd")
        hn_tr = sem("hn_tr")
        hn_hi = sem("hn_hi")
        hn_lo = sem("hn_lo")
        s_done = sem("s_done")
        s_read = sem("s_read")
        m_done = sem("m_done")
        p_done = sem("p_done")
        p_scaled = sem("p_scaled")
        l_recip = sem("l_recip")
        tp_done = sem("tp_done")
        pt_hi_done = sem("pt_hi_done")
        pt_lo_done = sem("pt_lo_done")
        o_done = sem("o_done")
        o_read = sem("o_read")
        o_stored = [sem("o_stored_even"), sem("o_stored_odd")]
        bias_loaded = sem("bias_loaded")
        bias_flipped = sem("bias_flipped")
        bias_ready = sem("bias_ready")
        v_hi_done = sem("v_hi_done")
        kv_loaded = sem("kv_loaded")
        b_hi = sem("b_hi")
        b_lo = sem("b_lo")

        def norm_act_square(act, n, index, sq):
            wait_gemm(act, index)
            if n >= 1:
                act.wait_ge(hn_ss, n)
            nc.scalar.activation(sq[:], psum[:, index % 2, :], ACT.Square).then_inc(hn_sq, 1)

        def norm_dve_sum(dve, n, sq):
            dve.wait_ge(hn_sq, n + 1)
            nc.vector.tensor_reduce(sumsq[:, 0:NH], sq[:].rearrange("p (h d) -> p h d", h=NH), AX.X,
                                    ALU.add).then_inc(hn_ss, 1)

        def norm_pool(pool, n):
            pool.wait_ge(hn_ss, n + 1)
            nc.gpsimd.tensor_scalar(meansq[:, 0:NH], sumsq[:, 0:NH], 1.0 / HD, RMS_EPS, ALU.mult,
                                    ALU.add).then_inc(hn_ms, 1)
            pool.wait_ge(hn_ms, n + 1)
            nc.gpsimd.tensor_tensor(rstd[:, n % 2, 0:NH], meansq[:, 0:NH], minus_half[:, 0:NH],
                                    ALU.pow).then_inc(hn_rstd, 1)

        def norm_dve_scale(dve, n, index, qn):
            dve.wait_ge(hn_rstd, n + 1)
            if n >= 1:
                dve.wait_ge(hn_tr, n)
            nc.vector.tensor_tensor(qn[:].rearrange("p (h d) -> p h d", h=NH),
                                    psum[:, index % 2, :].rearrange("p (h d) -> p h d", h=NH),
                                    rstd[:, n % 2, 0:NH].unsqueeze(2).to_broadcast([P, NH, HD]),
                                    ALU.mult).then_inc(gemm_freed, 1)

        def norm_pe(pe, n, index, qn):
            pe.wait_ge(gemm_freed, index + 1)
            if n >= 1:
                pe.wait_ge(hn_lo, n)
            for h in range(NH):
                tr = nc.tensor.transpose(psum[:, 2, h * HD:(h + 1) * HD], qn[:, h * HD:(h + 1) * HD], ident[:])
            tr.then_inc(hn_tr, 1)

        bank2_heads = psum[:, 2, :].rearrange("p (h t) -> p h t", h=NH)

        def norm_act_hi(act, n, wcol, hi, free=None):
            act.wait_ge(hn_tr, n + 1)
            if free:
                act.wait_ge(*free)
            nc.scalar.activation(hi, bank2_heads, ACT.Copy, scale=vecs[:, wcol:wcol + 1]).then_inc(hn_hi, 1)

        def norm_dve_lo(dve, n, wcol, hi, lo):
            dve.wait_ge(hn_hi, n + 1)
            nc.vector.scalar_tensor_tensor(lo, bank2_heads, vecs[:, wcol:wcol + 1], hi.bitcast(F32), ALU.mult,
                                           ALU.subtract).then_inc(hn_lo, 1)

        def values_hi(act, n, index, hi):
            wait_gemm(act, index)
            nc.scalar.copy(hi, psum[:, index % 2, :]).then_inc(v_hi_done, 1)

        def values_lo(dve, n, index, hi, lo):
            dve.wait_ge(v_hi_done, n + 1)
            nc.vector.tensor_tensor(lo, psum[:, index % 2, :], hi.bitcast(F32), ALU.subtract).then_inc(gemm_freed, 1)

        mem_tiles = [lambda k, t=t: (mem_hi[:, k, t * P:(t + 1) * P], mem_lo[:, k, t * P:(t + 1) * P])
                     for t in range(MT)]

        def key_cols(a, t):
            return a[:, :, t * P:(t + 1) * P]

        def memory_stage():
            def sync(sp):
                sp.dma_start(mem_rows[:], mem.rearrange("(t p) d -> p t d", p=P)).then_inc(mem_loaded, 16)
                sp.dma_start(ident[:], identity).then_inc(ident_loaded, 16)
                for src, dst in param_loads:
                    sp.dma_start(dst, src).then_inc(params_loaded, 16)
                load_turns(sp, 0, 1)
                for src, dst in bias_param_loads:
                    sp.dma_start(dst, src).then_inc(bias_params_loaded, 16)
                for b in range(2):
                    half = slice(b * NT // 2, (b + 1) * NT // 2)
                    sp.dma_start(x_rows[:, half, :], x.rearrange("(t p) d -> p t d", p=P)[:, half, :]
                                 ).then_inc(x_loaded[b], 16)
                load_turns(sp, 1, 2)
                load_turns(sp, 2, 3)
                sp.wait_ge(lines_copied, NG)
                sp.dma_start(bias_lines.rearrange("g h i -> h g i"), lines_sb[0:NH, :, :]).then_inc(lines_stored, 16)

            def scalar(act):
                rows_act_squares(act, mr, range(MT), lambda e, t: e.wait_ge(mem_loaded, 16))
                act.wait_ge(vecs_ready, 1)
                for k in range(KT):
                    rows_act_hi(act, mr, 0, [k])
                    split_hi(act, 0, k)
                rows_act_squares(act, xr, range(NT // 2), lambda e, t: e.wait_ge(x_loaded[0], 16))
                norm_act_square(act, 0, 0, mem_sq)
                splits_act(act, 1)
                norm_act_square(act, 1, 1, mem_sq)
                norm_act_hi(act, 0, V_XK, key_cols(new_kv[0], 0))
                for k in range(KT):
                    if k == 4:
                        values_hi(act, 0, MT, new_kv[2][:, 0, :])
                    rows_act_hi(act, xr, 0, [k])
                    if k in (1, 3, 4, 5):
                        rows_act_squares(act, xr, [NT // 2 + (1, 3, 4, 5).index(k)],
                                         lambda e, t: e.wait_ge(x_loaded[1], 16))
                norm_act_hi(act, 1, V_XK, key_cols(new_kv[0], 1))
                splits_act(act, 2)
                values_hi(act, 1, MT + 1, new_kv[2][:, 1, :])

            def gpsimd(pool):
                pool.wait_ge(half_set, 1)
                rows_pool(pool, mr, 0)
                splits_pool(pool, 0)
                rows_pool(pool, xr, 0)
                norm_pool(pool, 0)
                splits_pool(pool, 1)
                norm_pool(pool, 1)
                rows_pool(pool, xr, 1)
                splits_pool(pool, 2)

            def vector(dve):
                nc.vector.memset(minus_half[:], -0.5).then_inc(half_set, 1)
                nc.vector.memset(table_aug[N_BUCKETS:N_BUCKETS + 1, :], MASKED).then_inc(masked_set, 1)
                rows_dve_scale(dve, mr, 0)
                dve.wait_ge(params_tr, 1)
                nc.vector.tensor_copy(vecs[:, 0:NV], psum[:, 0, 0:NV]).then_inc(vecs_ready, 1)
                dve.wait_ge(vecs_ready, 1)
                nc.vector.tensor_scalar(vecs[:, V_QS:V_QS + NG], vecs[:, V_QNORM:V_QNORM + NG], HD ** -0.5, None,
                                        ALU.mult).then_inc(vecs_ready, 1)
                nc.vector.tensor_scalar(vecs[:, V_QS + NG:V_QS + NG + 1], vecs[:, V_XQ:V_XQ + 1], HD ** -0.5, None,
                                        ALU.mult).then_inc(vecs_ready, 1)
                for k in range(KT):
                    rows_dve_lo(dve, mr, 0, [k])
                    splits_dve(dve, 0, k, k + 1)

                def copy_line(g):
                    dve.wait_ge(lines_mm, g + 1)
                    nc.vector.tensor_copy(lines_sb[0:NH, g, :], psum[0:NH, 3, 0:LINE]).then_inc(lines_copied, 1)
                norm_dve_sum(dve, 0, mem_sq)
                rows_dve_scale(dve, xr, 0)
                norm_dve_scale(dve, 0, 0, mem_qn)
                copy_line(0)
                splits_dve(dve, 1)
                norm_dve_sum(dve, 1, mem_sq)
                norm_dve_lo(dve, 0, V_XK, key_cols(new_kv[0], 0), key_cols(new_kv[1], 0))
                norm_dve_scale(dve, 1, 1, mem_qn)
                rows_dve_lo(dve, xr, 0, range(4))
                values_lo(dve, 0, MT, new_kv[2][:, 0, :], new_kv[3][:, 0, :])
                copy_line(1)
                rows_dve_lo(dve, xr, 0, range(4, KT))
                norm_dve_lo(dve, 1, V_XK, key_cols(new_kv[0], 1), key_cols(new_kv[1], 1))
                splits_dve(dve, 2)
                values_lo(dve, 1, MT + 1, new_kv[2][:, 1, :], new_kv[3][:, 1, :])
                copy_line(2)
                rows_dve_scale(dve, xr, 1)

            def tensor(pe):
                pe.wait_ge(ident_loaded, 16)
                pe.wait_ge(row_scaled, MT)
                for k in range(4):
                    rows_pe_bank(pe, mr, 0, k)
                pe.wait_ge(params_loaded, 16 * len(param_loads))
                nc.tensor.transpose(psum[:, 0, 0:V_FW], rows_a[0:V_FW, :], ident[0:V_FW, 0:V_FW])
                nc.tensor.transpose(psum[:, 0, V_FW:V_FW + 4 * NU], rows_b[0:4 * NU, :], ident[0:4 * NU, 0:4 * NU])
                nc.tensor.transpose(psum[:, 0, V_FW + 4 * NU:V_DW], rows_c[0:2 * NU, :], ident[0:2 * NU, 0:2 * NU])
                for f in range(FT):
                    tr = nc.tensor.transpose(psum[:, 0, V_DW + f * CONV_W:V_DW + (f + 1) * CONV_W],
                                             dw_rows[0:CONV_W, f * P:(f + 1) * P], ident[0:CONV_W, 0:CONV_W])
                tr.then_inc(params_tr, 1)
                def bias_line(g):
                    if g == 0:
                        pe.wait_ge(masked_set, 1)
                        pe.wait_ge(bias_params_loaded, 16 * len(bias_param_loads))
                    else:
                        pe.wait_ge(lines_copied, g)
                    nc.tensor.matmul(psum[0:NH, 3, 0:LINE], table_aug[0:N_BUCKETS + 1, g * NH:(g + 1) * NH],
                                     onehot_sb[0:N_BUCKETS + 1, g * LINE:(g + 1) * LINE],
                                     start=True, stop=True).then_inc(lines_mm, 1)

                def mem_when_cut(k):
                    pe.wait_ge(row_lo, mr.bank0 + k + 1)
                    return mem_tiles[0](k)
                pe.wait_ge(vecs_ready, 1)
                token_gemm(pe, 0, 0, mem_when_cut, True, False,
                           lambda k: rows_pe_bank(pe, mr, 0, k + 4) if k < 4 else None)
                bias_line(0)
                token_gemm(pe, 1, 0, mem_tiles[1], False, True)
                def between_values(t, k):
                    if k == (1, 5)[t]:
                        norm_pe(pe, t, t, mem_qn)
                    if (k >= 4) == (t == 0):
                        pe.wait_ge(row_scaled, xr.tile0 + NT // 2)
                        rows_pe_bank(pe, xr, 0, (k + 4) % KT)
                token_gemm(pe, MT, 1, mem_tiles[0], True, False, lambda k: between_values(0, k))
                bias_line(1)
                token_gemm(pe, MT + 1, 1, mem_tiles[1], False, True, lambda k: between_values(1, k))
                bias_line(2)

            return sync, tensor, scalar, gpsimd, vector

        off = FREE
        kT = [at("k_hi", off, [NH, S], F32R), at("k_lo", off + 16384, [NH, S], F32R)]
        vT = [at("v_hi", off + 32768, [NT, CW], F32R), at("v_lo", off + 49152, [NT, CW], F32R)]
        bact = [at("bact_hi", FREE, [FT, S], F32R), at("bact_lo", FREE + 16384, [FT, S], F32R)]
        mkT = [at("mk_hi", FREE + 32768, [NH, N_MEM], F32R), at("mk_lo", FREE + 36864, [NH, N_MEM], F32R)]
        mv = [at("mv_hi", FREE + 49152, [MT, CW], F32R), at("mv_lo", FREE + 53248, [MT, CW], F32R)]
        VALUE_TILES_OVER = 2 * N_MEM * NH // CW
        off += 65536
        sq = at("sq", off, [CW])
        qn = at("qn", off + 2048, [CW])
        qT = [at("q_hi", off + 4096, [NH, P], F32R), at("q_lo", off + 6144, [NH, P], F32R)]
        sc = at("sc", off + 8192, [NH, 2 * P])
        hankel = at("hankel", off + 8192, [NH, 2 * P])
        pt = [at("pt_hi", off + 12288, [2 * NH * P], F32R), at("pt_lo", off + 16384, [2 * NH * P], F32R)]
        bias = at("bias", off + 20480, [NH, 2 * P])
        ob = at("ob", off + 24576, [2, CW])
        merged = at("merged", FREE + 32768, [KT, S])

        class Tile:
            def __init__(self, kind, g, t, i):
                self.kind, self.g, self.t = kind, g, t
                self.index = 2 * MT + i
                self.turn = BASE_ATT // RING + i // NT
                self.n = MT + 2 * NT * g + (NT if kind == "Q" else 0) + t
                self.v = MT + NT * g + t
                self.a = NT * g + t
                self.prev = kind == "Q" and (t > 0 if g == 0 else t % 2 == 1 if g == 1 else False)
                self.width = 2 * P if self.prev or kind == "X" else P
                self.qcol = V_QS + g
                self.lhs = act_tile(slice(t * P, (t + 1) * P)) if kind == "X" else group_tile(g, t)
                self.last = t == NT - 1

        tiles = []
        for g in range(NG):
            for kind in "KVQ":
                tiles += [Tile(kind, g, t, len(tiles) + t) for t in range(NT)]
        tiles += [Tile("X", NG, t, len(tiles) + t) for t in range(NT)]
        N_TILES = len(tiles)
        assert tiles[NT - 1].index == 2 * MT + NT - 1
        A_ALL = (NG + 1) * NT

        def tile_at(i, kinds):
            return tiles[i] if 0 <= i < N_TILES and tiles[i].kind in kinds else None

        def rows_of(tl):
            g, t = tl.g, tl.t
            if g == 0:
                return group_out[g][t * P:(t + 1) * P, :]
            if g == 1:
                return group_out[g].rearrange("(b p r) c -> r b p c", r=4, p=P)[t // 2, t % 2]
            return group_out[g].rearrange("(p r) c -> r p c", r=8)[t]

        per_tile = 2 * 16
        heads_scores = banks(3).rearrange("p (h c) -> p h c", h=NH)

        def bact_tile(part, t):
            return bact[part][:, :, t * P:(t + 1) * P]

        def bank_channels(b):
            return psum[:, b, :].rearrange("p (f t) -> p f t", f=FT)

        gate_done = sem("gate_done")
        sig_done = sem("sig_done")
        val_done = sem("val_done")
        prod_done = sem("prod_done")
        sum_done = sem("sum_done")

        def feature_half(pe, bank, slots, acts, f, half, first, last, done, between=None):
            for k, s in enumerate(slots):
                turn, pos = s // RING, s % RING
                if first:
                    wait_slot(pe, turn, pos)
                mm = three(pe, psum[:, bank + half, :],
                           (whi[:, pos, f * P:(f + 1) * P], wlo[:, pos, f * P:(f + 1) * P]),
                           (acts[0][:, k, half * CW:(half + 1) * CW], acts[1][:, k, half * CW:(half + 1) * CW]),
                           k == 0, k == len(slots) - 1)
                if last:
                    mm.then_inc(w_freed, 1)
                elif half == 1 and k == len(slots) - 1:
                    mm.then_inc(done, 1)
                if between:
                    between(k)

        def wait_feature(eng, done, n):
            chunk, gate = n // 4, done is gate_done
            if n % 4 < 3:
                eng.wait_ge(done, n + 1 - chunk)
            elif chunk == 0:
                eng.wait_ge(w_freed, BASE_GLU + (1 if gate else 2) * RING)
            else:
                b, j = (chunk - 1) // 2, (chunk - 1) % 2
                eng.wait_ge(w_freed, BASE_BRANCH + b * SLOTS_BRANCH + j * 12 + (8 if gate else 12))

        act_pair = (act_hi, act_lo)

        def gate_features(pe, before, slots, step=None, start=0):
            for f in range(start, 4):
                n = before + f
                if n >= 2:
                    pe.wait_ge(sig_done, n - 1)
                for half in range(2):
                    feature_half(pe, n % 2 * 2, slots, act_pair, f, half, f == 0 and half == 0,
                                 f == 3 and half == 1, gate_done,
                                 step and (lambda k, base=(2 * f + half) * KT: step(base + k)))

        def value_features(pe, before, slots, acts):
            for f in range(4):
                n = before + f
                if n >= 2:
                    pe.wait_ge(prod_done, n - 1)
                for half in range(2):
                    feature_half(pe, 4 + n % 2 * 2, slots, acts, f, half, f == 0 and half == 0,
                                 f == 3 and half == 1, val_done)

        PAD = CONV_W - 1
        u = at("u", FREE + 65536, [FT, S + 32])
        acc = at("acc", FREE + 65536 + FT * (S + 32) * 4, [S])
        pad_set = sem("pad_set")
        conv_done = sem("conv_done")
        turn_glu = BASE_GLU // RING
        glu_slots = range(BASE_GLU, BASE_GLU + RING)

        def conv_weight(f, tap):
            return vecs[:, V_DW + f * CONV_W + tap:V_DW + f * CONV_W + tap + 1]

        SHARED = 30
        acc_shared = at("acc_shared", FREE + 65536 + FT * (S + 32) * 4 + 4096, [S])
        shared_product = [at("shared_product", FREE + 65536 + FT * (S + 32) * 4 + 8192, [S])[:],
                          merged[:, KT - 2, :]]
        shared_mult = sem("shared_mult")
        shared_added = sem("shared_added")
        F_SHARED = FT - 1
        SHARED_COUNTS = [2, 1, 2, 1, 2, 1, 2, 2] + [5] + [4, 4, 4, 0]
        assert sum(SHARED_COUNTS) == SHARED
        SHARED_AT = [range(sum(SHARED_COUNTS[:i]), sum(SHARED_COUNTS[:i + 1])) for i in range(len(SHARED_COUNTS))]

        def shared_act(act, ns):
            for n in ns:
                tap = CONV_W - 1 - n
                if n == 0:
                    act.wait_ge(pad_set, 1)
                    act.wait_ge(prod_done, FT)
                elif n >= 2:
                    act.wait_ge(shared_added, n - 1)
                col = V_DW_B + F_SHARED
                nc.scalar.activation(shared_product[n % 2] if n else acc_shared[:], u[:, F_SHARED, tap:tap + S],
                                     ACT.Identity, bias=0.0 if n else vecs[:, col:col + 1],
                                     scale=conv_weight(F_SHARED, tap)).then_inc(shared_mult, 1)

        def shared_pool(pool, ns):
            for n in ns:
                pool.wait_ge(shared_mult, n + 1)
                if n == 0:
                    pool.sem_inc(shared_added, 1)
                else:
                    pool.wait_ge(shared_added, n)
                    nc.gpsimd.tensor_tensor(acc_shared[:], acc_shared[:], shared_product[n % 2],
                                            ALU.add).then_inc(shared_added, 1)

        conv_taps = [[(f, tap) for tap in reversed(range(CONV_W - (SHARED if f == F_SHARED else 0)))]
                     for f in range(FT)]

        def in_turn(a, b):
            return [step for pair in zip(a, b) for step in pair]
        HEAD = 7
        REST = CONV_W - HEAD
        N_LAST = CONV_W - SHARED
        conv_list = (conv_taps[0][:HEAD] + in_turn(conv_taps[0][HEAD:], conv_taps[1][:REST])
                     + in_turn(conv_taps[1][REST:], conv_taps[2][:HEAD]) + conv_taps[2][HEAD:CONV_W - N_LAST]
                     + in_turn(conv_taps[2][CONV_W - N_LAST:], conv_taps[F_SHARED]))
        N_CONV = len(conv_list)
        assert sorted(conv_list) == sorted(sum(conv_taps, []))
        conv_sum = [acc[:], merged[:, KT - 1, :], acc[:], acc_shared[:]]
        CONV_1_DONE = conv_list.index((1, 0)) + 1

        def conv_step(dve, n):
            f, tap = conv_list[n]
            w, total, src = conv_weight(f, tap), conv_sum[f], u[:, f, tap:tap + S]
            if tap < CONV_W - 1 and (f, tap + 1) in conv_list:
                dve.wait_ge(conv_done, conv_list.index((f, tap + 1)) + 1)
            if tap == CONV_W - 1:
                dve.wait_ge(pad_set, 1)
                dve.wait_ge(prod_done, f + 1)
                if f == 2:
                    dve.wait_ge(conv_done, conv_list.index((0, 0)) + 1)
                step = nc.vector.tensor_scalar(total, src, w, vecs[:, V_DW_B + f:V_DW_B + f + 1], ALU.mult, ALU.add)
            else:
                if f == F_SHARED and tap == CONV_W - 1 - SHARED:
                    dve.wait_ge(shared_added, SHARED)
                step = nc.vector.scalar_tensor_tensor(u[:, f, 0:S] if tap == 0 else total, src, w, total,
                                                      ALU.mult, ALU.add)
            step.then_inc(conv_done, 1)

        conv_steps = iter(range(N_CONV))

        def conv(dve, count):
            for _, n in zip(range(count), conv_steps):
                conv_step(dve, n)

        def attention_stage():
            def sync(sp):
                sp.wait_ge(hn_lo, MT)
                sp.wait_ge(gemm_freed, 2 * MT)
                for src, dst in zip(new_kv, kv_dram):
                    sp.dma_start(dst, src[:].bitcast(F32)).then_inc(kv_stored, 16)
                for g in range(NG):
                    turn_k = BASE_ATT // RING + 3 * g
                    load_turns(sp, turn_k + 1, turn_k + 2)
                    if g >= 1:
                        sp.wait_ge(tp_done, NT * g)
                    else:
                        sp.wait_ge(lines_stored, 16)
                        sp.wait_ge(kv_stored, 16 * 4)
                    lines = bass.AP(bias_lines.tensor, g * NH * LINE, [[1, P], [LINE, NH], [1, 2 * P]])
                    sp.dma_start(hankel[:], lines).then_inc(bias_loaded, 16)
                    load_turns(sp, turn_k + 2, turn_k + 4)
                sp.wait_ge(o_done, NT * (NG - 1) + VALUE_TILES_OVER)
                for src, dst in zip(kv_dram, mkT + mv):
                    sp.dma_start(dst[:].bitcast(F32), src).then_inc(kv_loaded, 16)
                load_turns(sp, turn_glu, turn_glu + 3)

            def tensor(pe):
                for i in range(N_TILES + 4):
                    if i < N_TILES:
                        tl = tiles[i]
                        if i == NT // 2:
                            pe.wait_ge(row_lo, xr.bank0 + 2 * KT)
                        between = None
                        if 2 <= i <= 3:
                            pe.wait_ge(row_scaled, xr.tile0 + NT)
                            between = lambda k: None if k % 2 else rows_pe_bank(pe, xr, 1, (i - 2) * 4 + k // 2)
                        token_gemm(pe, tl.index, tl.turn, tl.lhs, tl.t == 0, tl.last, between)
                        if tl.kind == "V" and tl.t == 0:
                            pe.wait_ge(bias_loaded, 16 * (tl.g + 1))
                            if tl.g >= 1:
                                pe.wait_ge(s_read, NT * tl.g)
                            for j in range(2):
                                mm = nc.tensor.matmul(psum[:, 3 + j, :], mirror_sb[:],
                                                      hankel[:, 2 * j:2 * j + 2, :].rearrange("p h c -> p (h c)"),
                                                      start=True, stop=True)
                            mm.then_inc(bias_flipped, 1)
                    else:
                        j = i - N_TILES
                        if j == 2:
                            pe.wait_ge(hn_lo, tiles[-1].n + 1)
                        if j == 3:
                            pe.wait_ge(p_done, A_ALL)
                        feature_half(pe, j // 2 * 2, glu_slots, act_pair, j // 2, j % 2, j == 0, False, gate_done)
                    tl = tile_at(i - 1, "KQX")
                    if tl:
                        norm_pe(pe, tl.n, tl.index, qn)
                    tl = tile_at(i - 2, "QX")
                    if tl:
                        pe.wait_ge(hn_lo, tl.n + 1)
                        if tl.kind == "Q":
                            if tl.a >= 1:
                                pe.wait_ge(s_read, tl.a)
                            if tl.t == 0:
                                pe.wait_ge(bias_ready, tl.g + 1)
                            c0 = (tl.t - tl.prev) * P
                            keys = [k[:, :, c0:c0 + tl.width] for k in kT]
                        else:
                            if tl.t == 0:
                                pe.wait_ge(s_read, tl.a)
                                pe.wait_ge(kv_loaded, 16 * 4)
                            else:
                                pe.wait_ge(p_done, tl.a)
                            keys = [k[:] for k in mkT]
                        for h in range(NH):
                            mm = three(pe, banks(3)[:, h * 256:h * 256 + tl.width], (qT[0][:, h, :], qT[1][:, h, :]),
                                       (keys[0][:, h, :], keys[1][:, h, :]), True, True)
                        mm.then_inc(s_done, 1)
                    tl = tile_at(i - 3, "QX")
                    if tl:
                        if tl.kind == "Q":
                            pe.wait_ge(p_done, tl.a + 1)
                        else:
                            pe.wait_ge(p_scaled, tl.t + 1)
                        if tl.a >= 1:
                            pe.wait_ge(pt_lo_done, tl.a)
                        for h in range(NH):
                            for kt in range(tl.width // P):
                                c = (h * tl.width // P + kt) * P
                                tr = nc.tensor.transpose(banks(5)[:, c:c + P], sc[:, h, kt * P:(kt + 1) * P], ident[:])
                        tr.then_inc(tp_done, 1)
                    tl = tile_at(i - 4, "QX")
                    if tl:
                        pe.wait_ge(pt_lo_done, tl.a + 1)
                        if tl.kind == "Q" or tl.t == 0:
                            if tl.a >= 1:
                                pe.wait_ge(o_read, tl.a)
                        else:
                            pe.wait_ge(b_lo, tl.t)
                        for h in range(NH):
                            for j in range(tl.width // P):
                                c = (h * tl.width // P + j) * P
                                probs = [part[:, c:c + P] for part in pt]
                                if tl.kind == "Q":
                                    vals = [part[:, tl.t - tl.prev + j, h * HD:(h + 1) * HD] for part in vT]
                                    lhs, rhs = probs, vals
                                else:
                                    vals = [part[:, j, h * HD:(h + 1) * HD] for part in mv]
                                    lhs, rhs = vals, probs
                                mm = three(pe, psum[:, 7, h * HD:(h + 1) * HD], lhs, rhs, j == 0,
                                           j == tl.width // P - 1)
                        mm.then_inc(o_done, 1)
                gate_features(pe, 0, glu_slots, start=2)
                pe.wait_ge(b_lo, NT)
                pe.wait_ge(pt_lo_done, A_ALL)
                value_features(pe, 0, range(BASE_GLU + RING, BASE_GLU + 2 * RING), act_pair)

            def glu_sigmoid(act, f):
                wait_feature(act, gate_done, f)
                nc.scalar.activation(merged[:, f, :], banks(f % 2 * 2), ACT.Sigmoid).then_inc(sig_done, 1)

            def scalar(act):
                for i in range(N_TILES + 5):
                    tl = tile_at(i, "KVQX")
                    if tl:
                        if 2 <= i <= 3:
                            rows_act_hi(act, xr, 1, range(4 * i - 8, 4 * i - 4))
                        if tl.last:
                            splits_act(act, tl.turn + 1, 0, RING - 1)
                        if tl.kind == "V":
                            if tl.t == 0 and tl.g:
                                act.wait_ge(o_done, tl.a)
                            values_hi(act, tl.v, tl.index, vT[0][:, tl.t, :])
                        else:
                            norm_act_square(act, tl.n, tl.index, sq)
                        if tl.last:
                            splits_act(act, tl.turn + 1, RING - 1)
                    tl = tile_at(i - 1, "K")
                    if tl:
                        free = (s_done, NT * tl.g if tl.t else NT * (tl.g - 1) + 2) if tl.g else None
                        norm_act_hi(act, tl.n, V_KNORM + tl.g, key_cols(kT[0], tl.t), free)
                    tl = tile_at(i - 1, "QX")
                    if tl:
                        norm_act_hi(act, tl.n, tl.qcol, qT[0][:], (s_done, tl.a) if tl.a else None)
                    tl = tile_at(i - 2, "QX")
                    if tl:
                        act.wait_ge(m_done, tl.a + 1)
                        src = sc
                        if tl.kind == "X":
                            act.wait_ge(tp_done, tl.a)
                            src = heads_scores
                        for h in range(NH):
                            e = nc.scalar.activation(sc[:, h, 0:tl.width], src[:, h, 0:tl.width], ACT.Exp,
                                                     bias=softstat[:, tl.a % 4, 1, h:h + 1],
                                                     accum_out=softstat[:, tl.a % 4, 0, h:h + 1])
                        e.then_inc(p_done, 1)
                    tl = tile_at(i - 3, "QX")
                    if tl:
                        act.wait_ge(tp_done, tl.a + 1)
                        if tl.a >= 1:
                            act.wait_ge(o_done, tl.a)
                        c = NH * tl.width
                        nc.scalar.copy(pt[0][:, 0:c], banks(5)[:, 0:c]).then_inc(pt_hi_done, 1)
                    tl = tile_at(i - 5, "Q")
                    if tl:
                        act.wait_ge(o_read, tl.a + 1)
                        dst = rows_of(tl)
                        act.dma_start(dst[:, 0:CW], ob[:, tl.t % 2, :]).then_inc(o_stored[tl.t % 2], 16)
                        act.dma_start(dst[:, CW:], softstat[:, tl.a % 4, :, :].rearrange(
                            "p a h -> p (a h)")).then_inc(o_stored[tl.t % 2], 16)
                    tl = tile_at(i - 4, "Q")
                    if tl:
                        act.wait_ge(o_done, tl.a + 1)
                        if tl.a >= 2:
                            act.wait_ge(o_stored[tl.a % 2], per_tile * (tl.a // 2))
                        nc.scalar.copy(ob[:, tl.t % 2, :], psum[:, 7, :]).then_inc(o_read, 1)
                    tl = tile_at(i - 4, "X")
                    if tl:
                        act.wait_ge(o_done, tl.a + 1)
                        nc.scalar.copy(bact_tile(0, tl.t), bank_channels(7)).then_inc(b_hi, 1)
                    if i == N_TILES + 2:
                        act.wait_ge(s_done, A_ALL)
                        glu_sigmoid(act, 0)
                glu_sigmoid(act, 1)
                for j in range(2):
                    act.wait_ge(o_stored[j], per_tile * NG * NT // 2)
                glu_sigmoid(act, 2)
                splits_act(act, turn_glu + 1)
                glu_sigmoid(act, 3)
                splits_act(act, turn_glu + 2)

            def gpsimd(pool):
                for tl in tiles:
                    if tl.last:
                        splits_pool(pool, tl.turn + 1)
                    if tl.kind != "V":
                        norm_pool(pool, tl.n)
                splits_pool(pool, turn_glu + 1)
                splits_pool(pool, turn_glu + 2)

            def vector(dve):
                for i in range(N_TILES + 4):
                    tl = tile_at(i, "KVQX")
                    if tl:
                        if 2 <= i <= 3:
                            rows_dve_lo(dve, xr, 1, range(4 * i - 8, 4 * i - 4))
                        if tl.last:
                            splits_dve(dve, tl.turn + 1, 0, RING - 1)
                        if tl.kind == "V":
                            values_lo(dve, tl.v, tl.index, vT[0][:, tl.t, :], vT[1][:, tl.t, :])
                        else:
                            norm_dve_sum(dve, tl.n, sq)
                        if tl.last:
                            splits_dve(dve, tl.turn + 1, RING - 1)
                        if tl.kind == "V" and tl.t == 1:
                            dve.wait_ge(bias_flipped, tl.g + 1)
                            nc.vector.tensor_copy(bias[:].rearrange("p h c -> p (h c)"),
                                                  banks(3)).then_inc(bias_ready, 1)
                    tl = tile_at(i - 1, "K")
                    if tl:
                        norm_dve_lo(dve, tl.n, V_KNORM + tl.g, key_cols(kT[0], tl.t), key_cols(kT[1], tl.t))
                    tl = tile_at(i - 1, "QX")
                    if tl:
                        norm_dve_lo(dve, tl.n, tl.qcol, qT[0][:], qT[1][:])
                    tl = tile_at(i - 2, "QX")
                    if tl:
                        dve.wait_ge(s_done, tl.a + 1)
                        src = heads_scores
                        if tl.a >= 4 and tl.a - 4 < NG * NT:
                            dve.wait_ge(o_stored[tl.a % 2], per_tile * ((tl.a - 4) // 2 + 1))
                        if tl.kind == "Q":
                            if tl.a >= 1:
                                dve.wait_ge(tp_done, tl.a)
                            if tl.t == 0:
                                dve.wait_ge(bias_ready, tl.g + 1)
                            src = sc[:, :, 0:tl.width]
                            nc.vector.tensor_tensor(src, heads_scores[:, :, 0:tl.width], bias[:, :, 2 * P - tl.width:],
                                                    ALU.add).then_inc(s_read, 1)
                            dve.wait_ge(s_read, tl.a + 1)
                        nc.vector.tensor_reduce(softstat[:, tl.a % 4, 1, :], src, AX.X, ALU.max,
                                                negate=True).then_inc(m_done, 1)
                    tl = tile_at(i, "KQX")
                    if tl:
                        norm_dve_scale(dve, tl.n, tl.index, qn)
                    tl = tile_at(i - 3, "QX")
                    if tl:
                        c = NH * tl.width
                        dve.wait_ge(pt_hi_done, tl.a + 1)
                        nc.vector.tensor_tensor(pt[1][:, 0:c], banks(5)[:, 0:c], pt[0][:, 0:c].bitcast(F32),
                                                ALU.subtract).then_inc(pt_lo_done, 1)
                    tl = tile_at(i - 2, "X")
                    if tl:
                        dve.wait_ge(p_done, tl.a + 1)
                        nc.vector.reciprocal(recip_l[:, tl.a % 2, :], softstat[:, tl.a % 4, 0, :]).then_inc(l_recip, 1)
                        dve.wait_ge(l_recip, tl.t + 1)
                        nc.vector.tensor_tensor(sc[:], sc[:],
                                                recip_l[:, tl.a % 2, :].unsqueeze(2).to_broadcast([P, NH, N_MEM]),
                                                ALU.mult).then_inc(p_scaled, 1)
                    tl = tile_at(i - 4, "X")
                    if tl:
                        dve.wait_ge(b_hi, tl.t + 1)
                        nc.vector.tensor_tensor(bact_tile(1, tl.t), bank_channels(7), bact_tile(0, tl.t).bitcast(F32),
                                                ALU.subtract).then_inc(b_lo, 1)
                nc.vector.memset(u[:, :, 0:PAD], 0.0).then_inc(pad_set, 1)
                splits_dve(dve, turn_glu + 1)
                for f in range(4):
                    if f == 3:
                        splits_dve(dve, turn_glu + 2, 0, RING - 1)
                    dve.wait_ge(sig_done, f + 1)
                    wait_feature(dve, val_done, f)
                    nc.vector.tensor_tensor(u[:, f, PAD:PAD + S], banks(4 + f % 2 * 2), merged[:, f, :],
                                            ALU.mult).then_inc(prod_done, 1)
                    if f == 3:
                        splits_dve(dve, turn_glu + 2, RING - 1)
                    else:
                        conv(dve, 7)

            return sync, tensor, scalar, gpsimd, vector

        gbuf = at("gbuf", FREE + 65536, [4, S])
        off = FREE + 65536 + FT * (S + 32) * 4
        nrm = at("nrm", off, [CW])
        swz = at("swz", off + 2048, [2, FT, P])
        grp = at("grp", FREE + 65536 + 16384, [2, NG, CW])
        gstat = at("gstat", FREE + 65536 + 3 * S * 4, [NG, NT, 2 * NH])
        c_low, c_total, c_recip = (at(name, FREE + 65536 + 3 * S * 4 + 768 + i * 128, [NT, NH])
                                   for i, name in enumerate(("c_low", "c_total", "c_recip")))
        c_shift, c_exp, c_le, c_f = (at(name, FREE + 65536 + 3 * S * 4 + 1152 + i * 384, [NG, NT, NH])
                                     for i, name in enumerate(("c_shift", "c_exp", "c_le", "c_f")))

        ln_tr = sem("ln_tr")
        ln_stats = sem("ln_stats")
        ln_aggr = sem("ln_aggr")
        ln_eps = sem("ln_eps")
        ln_rstd = sem("ln_rstd")
        ln_normed = sem("ln_normed")
        ln_back = sem("ln_back")
        sw_done = sem("sw_done")
        grp_loaded = [sem("grp_loaded_even"), sem("grp_loaded_odd")]
        gstat_loaded = sem("gstat_loaded")
        cmb_min = sem("cmb_min")
        cmb_first = sem("cmb_first")
        cmb_exp = sem("cmb_exp")
        cmb_step = sem("cmb_step")
        cmb_done = sem("cmb_done")
        cmb_tr = sem("cmb_tr")

        LN_STEPS = [5 + 11 * q // 2 for q in range(NT)]

        def channels_norm_pe(pe, s):
            if s in LN_STEPS:
                q = LN_STEPS.index(s)
                if q == 0:
                    pe.wait_ge(conv_done, N_CONV)
                    pe.wait_ge(prod_done, 4 + KT)
                else:
                    pe.wait_ge(ln_normed, q - 1)
                for f in range(FT):
                    tr = nc.tensor.transpose(psum[:, 4 + q % 2, f * P:(f + 1) * P], u[:, f, q * P:(q + 1) * P], ident[:])
                tr.then_inc(ln_tr, 1)
            if s - 9 in LN_STEPS:
                t = LN_STEPS.index(s - 9)
                pe.wait_ge(ln_normed, t + 1)
                if t >= 2:
                    pe.wait_ge(sw_done, t - 1)
                for f in range(FT):
                    tr = nc.tensor.transpose(psum[:, 6 + t % 2, f * P:(f + 1) * P], nrm[:, f * P:(f + 1) * P], ident[:])
                tr.then_inc(ln_back, 1)

        def channels_norm_dve(dve, q):
            if q < NT:
                m = moments[:, q % 2, :]
                dve.wait_ge(ln_tr, q + 1)
                nc.vector.bn_stats(combine_s[:, 0:1, :, 0:2], psum[:, 4 + q % 2, :]).then_inc(ln_stats, 1)
                dve.wait_ge(ln_stats, q + 1)
                nc.vector.bn_aggr(m[:, 0:2], combine_s[:, 0:1, :, 0:2]).then_inc(ln_aggr, 1)
            if q >= 2:
                t = q - 2
                dve.wait_ge(b_hi, NT + t + 1)
                nc.vector.tensor_tensor(bact_tile(1, t), swz[:, t % 2], bact_tile(0, t).bitcast(F32),
                                        ALU.subtract).then_inc(b_lo, 1)
            if q < NT:
                dve.wait_ge(ln_rstd, q + 1)
                if q >= 1:
                    dve.wait_ge(ln_back, q)
                nc.vector.tensor_scalar(nrm[:], psum[:, 4 + q % 2, :], m[:, 0:1], m[:, 3:4], ALU.subtract,
                                        ALU.mult).then_inc(ln_normed, 1)

        def channels_norm_pool(pool, q):
            if q < NT:
                m = moments[:, q % 2, :]
                pool.wait_ge(ln_aggr, q + 1)
                nc.gpsimd.tensor_scalar(m[:, 2:3], m[:, 1:2], 1.0, LN_EPS, ALU.mult, ALU.add).then_inc(ln_eps, 1)
                pool.wait_ge(ln_eps, q + 1)
                nc.gpsimd.tensor_tensor(m[:, 3:4], m[:, 2:3], minus_half[:, 0:1], ALU.pow).then_inc(ln_rstd, 1)

        def channels_norm_act(act, q):
            if 1 <= q <= NT:
                t = q - 1
                act.wait_ge(ln_back, t + 1)
                if t >= 2:
                    act.wait_ge(b_lo, NT + t - 1)
                for f in range(FT):
                    w, b = (vecs[:, v + f:v + f + 1] for v in (V_LN_W, V_LN_B))
                    z = nc.scalar.activation(swz[:, t % 2, f, :], psum[:, 6 + t % 2, f * P:(f + 1) * P], ACT.Silu,
                                             bias=b, scale=w)
                z.then_inc(sw_done, 1)
                act.wait_ge(sw_done, t + 1)
                nc.scalar.copy(bact_tile(0, t), swz[:, t % 2]).then_inc(b_hi, 1)

        def groups_mean_sync(sp):
            for j in range(2):
                sp.wait_ge(o_stored[j], per_tile * NG * NT // 2)
            sp.wait_ge(sum_done, KT)
            for g in range(NG):
                sp.dma_start(gstat[:, g], group_out[g].rearrange("(t p) c -> p t c", p=P)[:, :, CW:]
                             ).then_inc(gstat_loaded, 16)
            for t in range(NT):
                if t >= 2:
                    sp.wait_ge(cmb_done, t - 1)
                for g in (1, 2, 0):
                    if t >= 2 and g == 0:
                        sp.wait_ge(cmb_tr, t - 1)
                    sp.dma_start(grp[:, t % 2, g, :], group_out[g][t * P:(t + 1) * P, 0:CW]
                                 ).then_inc(grp_loaded[t % 2], 16)

        def group_weights_dve(dve):
            def chained(ins, n):
                ins.then_inc(cmb_step, 1)
                dve.wait_ge(cmb_step, n)

            def each(a):
                return a[:].unsqueeze(1).to_broadcast([P, NG, NT, NH])
            dve.wait_ge(gstat_loaded, 16 * NG)
            sums, neg = gstat[:, :, :, 0:NH], gstat[:, :, :, NH:]
            chained(nc.vector.tensor_tensor(c_low[:], neg[:, 0], neg[:, 1], ALU.min), 1)
            chained(nc.vector.tensor_tensor(c_low[:], c_low[:], neg[:, 2], ALU.min), 2)
            for g in range(NG):
                last = nc.vector.tensor_tensor(c_shift[:, g], c_low[:], neg[:, g], ALU.subtract)
            last.then_inc(cmb_min, 1)
            dve.wait_ge(cmb_exp, 1)
            for g in range(NG):
                last = nc.vector.tensor_tensor(c_le[:, g], c_exp[:, g], sums[:, g], ALU.mult)
            chained(last, 3)
            chained(nc.vector.tensor_tensor(c_total[:], c_le[:, 0], c_le[:, 1], ALU.add), 4)
            chained(nc.vector.tensor_tensor(c_total[:], c_total[:], c_le[:, 2], ALU.add), 5)
            chained(nc.vector.reciprocal(c_recip[:], c_total[:]), 6)
            for g in range(NG):
                last = nc.vector.tensor_tensor(c_f[:, g], c_exp[:, g], c_recip[:], ALU.mult)
            last.then_inc(cmb_weights, 1)

        def groups_mean_dve(dve, q):
            if q == 0:
                group_weights_dve(dve)
                dve.wait_ge(cmb_weights, 1)
            if q < NT:
                dve.wait_ge(cmb_first, q + 1)
                mean = grp[:, q % 2, 0, :]
                for g in (1, 2):
                    if g == 2:
                        dve.wait_ge(cmb_part, q + 1)
                    for h in range(NH):
                        cols = slice(h * HD, (h + 1) * HD)
                        last = nc.vector.scalar_tensor_tensor(mean[:, cols], grp[:, q % 2, g, cols],
                                                              c_f[:, g, q, h:h + 1], mean[:, cols], ALU.mult, ALU.add)
                    last.then_inc(cmb_part if g == 1 else cmb_done, 1)
            if 1 <= q <= NT:
                t = q - 1
                dve.wait_ge(b_hi, 2 * NT + t + 1)
                nc.vector.tensor_tensor(bact_tile(1, t), bank_channels(4 + t % 2), bact_tile(0, t).bitcast(F32),
                                        ALU.subtract).then_inc(b_lo, 1)

        def groups_mean_act(act, q):
            if q == 0:
                act.wait_ge(cmb_min, 1)
                nc.scalar.activation(c_exp[:], c_shift[:], ACT.Exp).then_inc(cmb_exp, 1)
                act.wait_ge(cmb_weights, 1)
            if q < NT:
                act.wait_ge(grp_loaded[q % 2], 16 * NG * (q // 2 + 1))
                for h in range(NH):
                    cols = grp[:, q % 2, 0, h * HD:(h + 1) * HD]
                    last = nc.scalar.activation(cols, cols, ACT.Copy, scale=c_f[:, 0, q, h:h + 1])
                last.then_inc(cmb_first, 1)
            if 1 <= q <= NT:
                t = q - 1
                act.wait_ge(cmb_tr, t + 1)
                nc.scalar.copy(bact_tile(0, t), bank_channels(4 + t % 2)).then_inc(b_hi, 1)

        def groups_mean_pe(pe, s):
            if s >= 20 and (s - 20) % 5 == 0 and (s - 20) // 5 < NT:
                t = (s - 20) // 5
                pe.wait_ge(cmb_done, t + 1)
                if t >= 2:
                    pe.wait_ge(b_lo, 2 * NT + t - 1)
                else:
                    pe.wait_ge(prod_done, 4 + 2 * KT)
                for h in range(NH):
                    tr = nc.tensor.transpose(psum[:, 4 + t % 2, h * P:(h + 1) * P],
                                             grp[:, t % 2, 0, h * P:(h + 1) * P], ident[:])
                tr.then_inc(cmb_tr, 1)

        cmb_part = sem("cmb_part")
        cmb_weights = sem("cmb_weights")
        PREP_STEPS = NT + 2
        SIGMOID_AFTER = (2, 5, 7)
        NOTHING = (lambda e, q: None,) * 4
        prepare = [NOTHING, (channels_norm_pe, channels_norm_act, channels_norm_dve, channels_norm_pool),
                   (groups_mean_pe, groups_mean_act, groups_mean_dve, lambda e, q: None)]

        POOL_SUMS = (4, 5, 6)

        m_hi = sem("m_hi")
        m_lo = sem("m_lo")

        def merged_hi(act, ks):
            for k in ks:
                wait_feature(act, gate_done, 3 + 3 * KT)
                act.wait_ge(sum_done, KT + k + 1)
                nc.scalar.copy(act_hi[:, k, :], merged[:, k, :]).then_inc(m_hi, 1)

        def merged_lo(dve, ks):
            for k in ks:
                dve.wait_ge(m_hi, k + 1)
                nc.vector.tensor_tensor(act_lo[:, k, :], merged[:, k, :], act_hi[:, k, :].bitcast(F32),
                                        ALU.subtract).then_inc(m_lo, 1)

        def branch_stage(b, gate):
            first = BASE_BRANCH + b * SLOTS_BRANCH
            turn = first // RING
            gates = [range(first, first + 8), range(first + 12, first + 20)]
            outs = [range(first + 8, first + 12), range(first + 20, first + 24)]
            before = 4 + b * KT

            def quarters(a):
                return a.rearrange("p (a c) -> p a c", c=S // 4)

            def sig_at(f):
                if b == 0:
                    return quarters(merged[:, f, :])
                if b == 1:
                    return u[:, :, f % 4 * 2 * P:(f % 4 * 2 + 2) * P]
                return quarters(gbuf[:, f % 4, :])
            prep_pe, prep_act, prep_dve, prep_pool = prepare[b]

            def pair(n, base=0):
                return banks(base + n % 2 * 2)

            def split_range(eng, ops, s0, s1):
                for s in range(s0, s1):
                    t, pos = (first + s) // RING, (first + s) % RING
                    if ops is None:
                        split_hi(eng, t, pos)
                    elif (pos % 2 == 0) == (ops is nc.gpsimd):
                        split_lo(eng, ops, t, pos)

            def sync(sp):
                if b == 2:
                    groups_mean_sync(sp)
                load_turns(sp, turn + 1, turn + 4)

            def tensor(pe):
                gate_features(pe, before, gates[0], lambda s: prep_pe(pe, s))
                pe.wait_ge(b_lo, NT * (b + 1))
                value_features(pe, before, outs[0], bact)
                gate_features(pe, before + 4, gates[1])
                value_features(pe, before + 4, outs[1], bact)

            def gate_sigmoid(act, f):
                n = before + f
                wait_feature(act, gate_done, n)
                if b == 0 and f < 4:
                    act.wait_ge(prod_done, f + 1)
                if b == 0 and f == KT - 2:
                    act.wait_ge(shared_added, SHARED)
                if b == 0 and f == KT - 1:
                    act.wait_ge(conv_done, CONV_1_DONE)
                if b == 2 and f < 4:
                    act.wait_ge(sum_done, KT)
                    if f == 3:
                        act.wait_ge(cmb_done, NT)
                if b >= 1 and f >= 4:
                    act.wait_ge(prod_done, n - 3)
                    act.wait_ge(sum_done, (b - 1) * KT + f - 3)
                if b == 1 and f < 4:
                    act.wait_ge(ln_tr, 2 * f + 2)
                col = V_GATE_B + gate * KT + f
                nc.scalar.activation(sig_at(f), quarters(pair(n)), ACT.Sigmoid, bias=vecs[:, col:col + 1]).then_inc(sig_done, 1)

            def scalar(act):
                for q in range(PREP_STEPS):
                    prep_act(act, q)
                    if b == 0 and q < NT:
                        shared_act(act, SHARED_AT[q])
                    if q in SIGMOID_AFTER:
                        gate_sigmoid(act, SIGMOID_AFTER.index(q))
                split_range(act, None, 8, 16)
                gate_sigmoid(act, 3)
                if b == 0:
                    shared_act(act, SHARED_AT[8])
                split_range(act, None, 16, 20)
                for f in range(4, KT):
                    if b == 0:
                        shared_act(act, SHARED_AT[5 + f])
                    if f == KT - 1:
                        split_range(act, None, 20, 28)
                    gate_sigmoid(act, f)
                if b == 2:
                    merged_hi(act, range(KT - 2))
                split_range(act, None, 28, 30)
                if b == 2:
                    merged_hi(act, [KT - 2])
                split_range(act, None, 30, 32)
                if b == 2:
                    merged_hi(act, [KT - 1])

            def gpsimd(pool):
                for q in range(NT):
                    prep_pool(pool, q)
                    if b == 0:
                        shared_pool(pool, SHARED_AT[q])
                split_range(pool, nc.gpsimd, 8, 16)
                if b == 0:
                    shared_pool(pool, SHARED_AT[8])
                split_range(pool, nc.gpsimd, 16, 20)
                if b == 0:
                    for f in range(4, KT):
                        shared_pool(pool, SHARED_AT[5 + f])
                split_range(pool, nc.gpsimd, 20, 28)
                if b == 2:
                    for f in POOL_SUMS:
                        pool.wait_ge(prod_done, before + f + 1)
                        nc.gpsimd.tensor_tensor(merged[:, f, :], merged[:, f, :], gbuf[:, f % 4, :],
                                                ALU.add).then_inc(sum_done, 1)
                split_range(pool, nc.gpsimd, 28, 32)

            def branch_product(dve, f):
                n = before + f
                dve.wait_ge(sig_done, n + 1)
                wait_feature(dve, val_done, n)
                nc.vector.tensor_tensor(sig_at(f), quarters(pair(n, 4)), sig_at(f), ALU.mult).then_inc(prod_done, 1)
                if b >= 1 and not (b == 2 and f in POOL_SUMS):
                    dve.wait_ge(prod_done, n + 1)
                    if b == 2 and f > POOL_SUMS[-1]:
                        dve.wait_ge(sum_done, KT + f)
                    nc.vector.tensor_tensor(quarters(merged[:, f, :]), quarters(merged[:, f, :]), sig_at(f),
                                            ALU.add).then_inc(sum_done, 1)

            def vector(dve):
                for q in range(PREP_STEPS):
                    prep_dve(dve, q)
                    if b == 0 and q < NT:
                        conv(dve, 4 if q < NT - 1 else 2)
                split_range(dve, nc.vector, 8, 16)
                for f in range(0, 4):
                    if f == 3:
                        split_range(dve, nc.vector, 16, 20)
                    branch_product(dve, f)
                    if b == 0:
                        conv(dve, 3)
                if b == 0:
                    conv(dve, 27)
                split_range(dve, nc.vector, 20, 28)
                for f in range(4, KT):
                    if f == KT - 1:
                        if b == 0:
                            conv(dve, N_CONV)
                        split_range(dve, nc.vector, 28, 31)
                    branch_product(dve, f)
                    if f == KT - 1:
                        if b == 2:
                            merged_lo(dve, [KT - 2])
                        split_range(dve, nc.vector, 31, 32)
                    if b == 0 and f < KT - 1:
                        conv(dve, 1)
                    if b == 2:
                        merged_lo(dve, range(2 * f - 8, 2 * f - 6) if f < KT - 1 else [KT - 1])

            return sync, tensor, scalar, gpsimd, vector

        h_rows = at("h_rows", FREE, [NT, D])
        h_junk = at("h_junk", FREE + 65536, [D])
        H_BATCH = 2
        h_batches = range(NT // H_BATCH)
        res_loaded = [[sem(f"res_loaded{j}{b}") for b in h_batches] for j in range(2)]
        h_stored = [sem(f"h_stored{b}") for b in h_batches]
        turn_o = BASE_WOUT // RING
        io = 2 * MT + N_TILES
        hr = Rows(xr, h_rows, h_junk, NT, H_BATCH, V_FFN_NORM, act_hi, act_lo, 
                  banks=lambda b: (2, 3, 6, 7) if b < 2 else (3, 5, 7, 1))
        T_UP = BASE_UP // RING
        T_DOWN = BASE_DOWN // RING

        def w_out_stage():
            def sync(sp):
                wait_feature(sp, val_done, 3 + 3 * KT)
                for j in range(2):
                    for b in h_batches:
                        rows, cols = slice(b * H_BATCH, (b + 1) * H_BATCH), slice(j * CW, (j + 1) * CW)
                        sp.dma_start(h_rows[:, rows, cols], x.rearrange("(t p) d -> p t d", p=P)[:, rows, cols]
                                     ).then_inc(res_loaded[j][b], 16)
                load_turns(sp, turn_o + 1, turn_o + 3)

            def tensor(pe):
                pe.wait_ge(sig_done, 4 + 3 * KT)
                for j in range(2):
                    for t in range(NT):
                        tile = act_tile(slice(t * P, (t + 1) * P))
                        between = None
                        if j == 0 and t == 0:
                            def lhs(k, tile=tile):
                                pe.wait_ge(m_lo, k + 1)
                                return tile(k)
                        else:
                            lhs = tile
                        if j == 1 and t in (5, 6):
                            b = t - 5
                            pe.wait_ge(row_scaled, hr.tile0 + (b + 1) * H_BATCH)
                            between = lambda k: rows_pe_bank(pe, hr, b, k)
                        token_gemm(pe, io + j * NT + t, turn_o + j, lhs, t == 0, t == NT - 1, between)

            def scalar(act):
                splits_act(act, turn_o + 1)
                for t in range(NT):
                    if t in (5, 6):
                        rows_act_hi(act, hr, t - 5)
                    if t == NT - 1:
                        splits_act(act, turn_o + 2)
                    act.wait_ge(gemm_freed, io + NT + t + 1)
                    act.dma_start(h_dram[t * P:(t + 1) * P, :], h_rows[:, t, :]).then_inc(h_stored[t // H_BATCH], 16)
                    if t == NT - 1:
                        rows_act_hi(act, hr, 2)
                    rows_act_squares(act, hr, [t], lambda e, t: None)
                rows_act_hi(act, hr, 3)

            def gpsimd(pool):
                splits_pool(pool, turn_o + 1)
                for b in range(3):
                    rows_pool(pool, hr, b)
                splits_pool(pool, turn_o + 2)
                rows_pool(pool, hr, 3)

            def vector(dve):
                def scale(b):
                    dve.wait_ge(h_stored[b], 16 * H_BATCH)
                    rows_dve_scale(dve, hr, b)

                for j in range(2):
                    for t in range(NT):
                        if j == 1 and t in (5, 6):
                            rows_dve_lo(dve, hr, t - 5)
                        if t == NT - 1:
                            splits_dve(dve, turn_o + 1 + j)
                        n = io + j * NT + t
                        cols = slice(j * CW, (j + 1) * CW)
                        wait_gemm(dve, n)
                        if t % H_BATCH == 0:
                            dve.wait_ge(res_loaded[j][t // H_BATCH], 16)
                        nc.vector.tensor_tensor(h_rows[:, t, cols], psum[:, n % 2, :], h_rows[:, t, cols],
                                                ALU.add).then_inc(gemm_freed, 1)
                        if j == 1 and t in (3, 4, 6):
                            scale((3, 4, 6).index(t))
                rows_dve_lo(dve, hr, 2)
                scale(3)
                rows_dve_lo(dve, hr, 3)

            return sync, tensor, scalar, gpsimd, vector

        gated = at("gated", FREE, [NU, S])
        value = at("value", FREE + NU * S * 4, [S])
        wait_met = sem("wait_met")
        up_done = sem("up_done")
        pairs_free = sem("pairs_free")
        base_done = sem("base_done")
        tap_done = sem("tap_done")
        silu_done = sem("silu_done")
        value_free = sem("value_free")

        def up_param(base, kind, U):
            col = base + kind * NU + U
            return vecs[:, bass.ds(col, 1)]

        def up_dst(kind, U):
            return gated[:, U, :] if kind else value[:]

        def met(act):
            act.sem_inc(wait_met, 1)

        def up_base(act, kind, c, i):
            U = 2 * c + i
            if kind or i == 0:
                act.wait_ge(up_done, 3 * c + (2 * i + 2 - kind))
            else:
                act.wait_ge(w_freed, RING * c + (BASE_UP + RING))
            if not kind:
                act.wait_ge(value_free, U + 1)
            met(act)
            nc.scalar.activation(up_dst(kind, U), banks((0 if kind else 4) + 2 * i), ACT.Identity,
                                 bias=up_param(V_FB, kind, U), scale=up_param(V_FW + 4 * NU, kind, U)
                                 ).then_inc(base_done, 1)

        def up_silu(act, U):
            act.wait_ge(pairs_free, 4 + 2 * U + 1)
            met(act)
            nc.scalar.activation(gated[:, U, :], gated[:, U, :], ACT.Silu).then_inc(silu_done, 1)

        def up_taps(dve, kind, U, i):
            src, dst = banks((0 if kind else 4) + 2 * i), up_dst(kind, U)
            dve.wait_ge(base_done, 2 * U + (1 if kind else 2))
            nc.vector.scalar_tensor_tensor(dst[:, 1:], src[:, 0:S - 1], up_param(V_FW + 2 * NU, kind, U), dst[:, 1:],
                                           ALU.mult, ALU.add).then_inc(tap_done, 1)
            dve.wait_ge(tap_done, 2 * U + (1 if kind else 2))
            nc.vector.scalar_tensor_tensor(dst[:, 2:], src[:, 0:S - 2], up_param(V_FW, kind, U), dst[:, 2:],
                                           ALU.mult, ALU.add).then_inc(pairs_free, 1)

        def up_product(dve, U):
            dve.wait_ge(silu_done, U + 1)
            dve.wait_ge(pairs_free, 4 + 2 * U + 2)
            nc.vector.tensor_tensor(gated[:, U, :], gated[:, U, :], value[:], ALU.mult).then_inc(value_free, 1)

        def up_chunk_act(act, c, between):
            for i in range(2):
                U = 2 * c + i
                up_base(act, 1, c, i)
                if i == 1:
                    between(act)
                up_base(act, 0, c, i)
                up_silu(act, U)

        def up_chunk_dve(dve, c, between, before_product=None):
            for i in range(2):
                U = 2 * c + i
                up_taps(dve, 1, U, i)
                if i == 1:
                    between(dve)
                up_taps(dve, 0, U, i)
                if i == 1 and before_product:
                    before_product(dve)
                up_product(dve, U)

        def down_piece(k, n):
            return w_down[bass.ds(k * P, P), n * CW:(n + 1) * CW]

        gs = [[at("gs_hi0", 2 * slot_bytes, [S], F32R), at("gs_hi1", 4 * slot_bytes, [S], F32R)],
              [at("gs_lo0", 6 * slot_bytes, [S], F32R), at("gs_lo1", ACTS, [S], F32R)]]
        h_res = at("h_res", ACTS + S * 4, [NT, D])
        gs_hi_done = sem("gs_hi_done")
        gs_lo_done = sem("gs_lo_done")
        hres_loaded = sem("hres_loaded")
        down_done = sem("down_done")
        out_ready = sem("out_ready")
        out_stored = sem("out_stored")
        LO0, FREED0 = 4 * T_DOWN, BASE_DOWN

        def down_split_hi(act, half_m, pos, k, with_weight):
            if with_weight:
                act.wait_ge(w_freed, 2 * half_m + (pos - 1 + FREED0))
                met(act)
            nc.scalar.copy(gs[0][pos][:], gated[:, k, :]).then_inc(gs_hi_done, 1)
            if with_weight:
                act.wait_ge(w_loaded[pos], 16 * half_m + 16 * (T_DOWN + 1))
                nc.scalar.copy(whi[:, pos, :], stage[:, pos, :]).then_inc(w_hi, 1)

        def down_lo_gated(dve, half_m, pos, k):
            dve.wait_ge(gs_hi_done, 2 * half_m + (pos + 1))
            nc.vector.tensor_tensor(gs[1][pos][:], gated[:, k, :], gs[0][pos][:].bitcast(F32),
                                    ALU.subtract).then_inc(gs_lo_done, 1)

        def down_lo_weight(eng, ops, half_m, pos):
            eng.wait_ge(w_hi, 2 * half_m + (FREED0 + pos + 1))
            ops.tensor_tensor(wlo[:, pos, :], stage[:, pos, :], whi[:, pos, :].bitcast(F32),
                              ALU.subtract).then_inc(w_lo[pos], 1)

        def up_stage():
            def sync(sp):
                with sp.Fori(0, N_UP - 1) as c:
                    for pos in range(RING):
                        load_slot(sp, c + (T_UP + 1), pos,
                                  up_halves[pos * P:(pos + 1) * P, :, bass.ds((c + 1) * (CW // 2), CW // 2)], 2)
                for pos in range(2):
                    load_slot(sp, T_DOWN, pos, w_down[pos * P:(pos + 1) * P, 0:CW])

            def up_half(pe, c, i, kind, half, between=None):
                last = i == 1 and kind == 0 and half == 1
                for k in range(KT):
                    if i == 0 and kind == 1 and half == 0:
                        wait_slot(pe, c + T_UP, k)
                    cols = slice((2 * kind + i) * P, (2 * kind + i + 1) * P)
                    mm = three(pe, psum[:, (0 if kind else 4) + 2 * i + half, :],
                               (whi[:, k, cols], wlo[:, k, cols]),
                               (act_hi[:, k, half * CW:(half + 1) * CW],
                                act_lo[:, k, half * CW:(half + 1) * CW]), k == 0, k == KT - 1)
                    if last:
                        mm.then_inc(w_freed, 1)
                    elif half == 1 and k == KT - 1:
                        mm.then_inc(up_done, 1)
                    if between:
                        between(k)

            def tensor(pe):
                pe.wait_ge(row_lo, hr.bank0 + 2 * KT)
                pe.wait_ge(gemm_freed, io + 2 * NT - 1)
                for i, kind, b in ((0, 1, 2), (0, 0, None), (1, 1, 3), (1, 0, None)):
                    between = None
                    if b:
                        pe.wait_ge(row_scaled, hr.tile0 + (b + 1) * H_BATCH)
                        between = lambda k: rows_pe_bank(pe, hr, b, k)
                    up_half(pe, 0, i, kind, 0, between)
                pe.wait_ge(row_lo, hr.bank0 + len(h_batches) * KT)
                for i in range(2):
                    for kind in (1, 0):
                        up_half(pe, 0, i, kind, 1)
                with pe.Fori(0, N_UP // 2) as cc:
                    for ci in range(2):
                        c = 2 * cc + (1 + ci)
                        for i in range(2):
                            for kind in (1, 0):
                                pe.wait_ge(pairs_free, 4 * c + (2 * i + 2 - kind))
                                for half in range(2):
                                    up_half(pe, c, i, kind, half)

            def scalar(act):
                with act.Fori(0, N_UP - 1) as c:
                    up_chunk_act(act, c, lambda e: splits_act(e, c + (T_UP + 1)))

                def first_pieces(act):
                    for parity in range(2):
                        act.wait_ge(w_lo[parity], LO0)
                    for pos in range(2):
                        down_split_hi(act, 0, pos, pos, False)
                    splits_act(act, T_DOWN, 0, 2)
                up_chunk_act(act, N_UP - 1, first_pieces)

            def gpsimd(pool):
                with pool.Fori(0, N_UP - 1) as c:
                    splits_pool(pool, c + (T_UP + 1))
                splits_pool(pool, T_DOWN, 0, 2)

            def vector(dve):
                dve.sem_inc(pairs_free, 4)
                dve.sem_inc(value_free, 1)
                with dve.Fori(0, N_UP - 1) as c:
                    up_chunk_dve(dve, c, lambda e: splits_dve(e, c + (T_UP + 1)))

                def first_piece(dve):
                    down_lo_gated(dve, 0, 0, 0)
                    splits_dve(dve, T_DOWN, 0, 2)
                up_chunk_dve(dve, N_UP - 1, first_piece, lambda e: down_lo_gated(e, 0, 1, 1))

            return sync, tensor, scalar, gpsimd, vector

        def down_stage():
            def sync(sp):
                def load_pieces(kk, n):
                    for pos in range(2):
                        sp.wait_ge(w_lo[pos], kk + (LO0 + NU // 2 * n))
                        sp.dma_start(stage[:, pos, :], down_piece(2 * kk + pos, n)).then_inc(w_loaded[pos], 16)

                def load_residual(t):
                    sp.dma_start(h_res[:, t, :], h_dram[t * P:(t + 1) * P, :]).then_inc(hres_loaded, 16)

                def store_columns(n):
                    for t in range(NT):
                        sp.wait_ge(out_ready, NT * n + t + 1)
                        sp.dma_start(out[t * P:(t + 1) * P, n * CW:(n + 1) * CW],
                                     h_res[:, t, n * CW:(n + 1) * CW]).then_inc(out_stored, 16)

                load_pieces(1, 0)
                sp.wait_ge(w_freed, BASE_DOWN)
                for b in h_batches:
                    sp.wait_ge(h_stored[b], 16 * H_BATCH)
                for t in range(NT):
                    load_residual(t)
                    load_pieces(t + 2, 0)
                with sp.Fori(NT + 2, NU // 2) as kk:
                    load_pieces(kk, 0)
                for pos in range(2):
                    sp.wait_ge(w_lo[pos], LO0 + NU // 2)
                    sp.dma_start(stage[:, pos, :], w_down[pos * P:(pos + 1) * P, CW:2 * CW]).then_inc(w_loaded[pos], 16)
                load_pieces(1, 1)
                store_columns(0)
                with sp.Fori(2, NU // 2) as kk:
                    load_pieces(kk, 1)
                store_columns(1)
                sp.wait_ge(out_stored, 2 * 16 * NT)

            def tensor(pe):
                def piece_products(half_m, pos, start, stop, n):
                    wait_count = half_m + (LO0 + 1)
                    pe.wait_ge(w_lo[pos], wait_count)
                    pe.wait_ge(gs_lo_done, 2 * half_m + (pos + 1))
                    for t in range(NT):
                        if start and n == 0 and t % 2 == 0:
                            pe.wait_ge(pairs_free, 2 * NU + (1, 3, 2, 4)[t // 2])
                        if start and n == 1:
                            pe.wait_ge(out_ready, t + 1)
                        tok = slice(t * P, (t + 1) * P)
                        mm = three(pe, psum[:, t, :], (gs[0][pos][:, tok], gs[1][pos][:, tok]),
                                   (whi[:, pos, :], wlo[:, pos, :]), start, stop)
                        if stop and t < NT - 1:
                            mm.then_inc(down_done, 1)
                    mm.then_inc(w_freed, 1)

                for n in range(2):
                    half0 = n * NU // 2
                    piece_products(half0, 0, True, False, n)
                    piece_products(half0, 1, False, False, n)
                    with pe.Fori(1, NU // 2 - 1) as kk:
                        for pos in range(2):
                            piece_products(kk + half0, pos, False, False, n)
                    piece_products(half0 + NU // 2 - 1, 0, False, False, n)
                    piece_products(half0 + NU // 2 - 1, 1, False, True, n)

            def scalar(act):
                act.wait_ge(value_free, NU + 1)
                with act.Fori(1, NU // 2) as kk:
                    for pos in range(2):
                        down_split_hi(act, kk, pos, 2 * kk + pos, True)
                with act.Fori(0, NU // 2) as kk:
                    for pos in range(2):
                        down_split_hi(act, kk + NU // 2, pos, 2 * kk + pos, True)

            def gpsimd(pool):
                with pool.Fori(1, NU) as half_m:
                    down_lo_weight(pool, nc.gpsimd, half_m, 0)

            def vector(dve):
                def finish_columns(n):
                    dve.wait_ge(hres_loaded, 16 * NT)
                    for t in range(NT):
                        if t < NT - 1:
                            dve.wait_ge(down_done, (NT - 1) * n + t + 1)
                        else:
                            dve.wait_ge(w_freed, BASE_DOWN + NU * (n + 1))
                        cols = h_res[:, t, n * CW:(n + 1) * CW]
                        nc.vector.tensor_tensor(cols, psum[:, t, :], cols, ALU.add).then_inc(out_ready, 1)

                with dve.Fori(1, NU // 2) as kk:
                    down_lo_gated(dve, kk, 0, 2 * kk)
                    down_lo_gated(dve, kk, 1, 2 * kk + 1)
                    down_lo_weight(dve, nc.vector, kk, 1)
                half0 = NU // 2
                down_lo_gated(dve, half0, 0, 0)
                finish_columns(0)
                down_lo_gated(dve, half0, 1, 1)
                down_lo_weight(dve, nc.vector, half0, 1)
                with dve.Fori(1, NU // 2) as kk:
                    down_lo_gated(dve, kk + half0, 0, 2 * kk)
                    down_lo_gated(dve, kk + half0, 1, 2 * kk + 1)
                    down_lo_weight(dve, nc.vector, kk + half0, 1)
                finish_columns(1)

            return sync, tensor, scalar, gpsimd, vector

        stages = [memory_stage(), attention_stage()] + [branch_stage(b, gate) for b, gate in enumerate((2, 1, 0))]
        stages += [w_out_stage(), up_stage(), down_stage()]

        with nc.Block() as block:
            @block.sync
            def _(sp):
                for sync, _, _, _, _ in stages:
                    sync(sp)

            @block.tensor
            def _(pe):
                for _, tensor, _, _, _ in stages:
                    tensor(pe)

            @block.scalar
            def _(act):
                for _, _, scalar, _, _ in stages:
                    scalar(act)

            @block.gpsimd
            def _(pool):
                for _, _, _, gpsimd, _ in stages:
                    gpsimd(pool)

            @block.vector
            def _(dve):
                for _, _, _, _, vector in stages:
                    vector(dve)


_INS = ["x", "mem", "rel_bias_table", "attn_norm_w", "w_in", "b_gate", "q_norm_w", "k_norm_w", "w_attn_o",
        "conv_dw_w", "conv_dw_b", "conv_ln_w", "conv_ln_b", "w_conv_o", "mem_norm_w", "w_mem_kv", "xq_norm_w",
        "xk_norm_w", "w_cross_o", "w_out", "ffn_norm_w", "w_up", "ffn_conv_w", "ffn_conv_b", "w_down"]


def kernel(**inputs):
    import numpy as _np
    import concourse.bacc as _bacc
    from concourse import mybir as _mybir
    from concourse.bass_utils import run_bass_kernel_spmd as _run

    arrays = {name: _np.ascontiguousarray(inputs[name]) for name in _INS}
    arrays["identity"] = _np.eye(P, dtype=_np.float32)
    arrays["mirror"] = _np.ascontiguousarray(_np.eye(P, dtype=_np.float32)[::-1])
    arrays["bias_onehot"] = bias_constants()
    nc = _bacc.Bacc("TRN2", target_bir_lowering=False, num_devices=1)
    args = {}
    for name, a in arrays.items():
        args[name] = nc.dram_tensor("in_" + name, a.shape, _mybir.dt.from_np(a.dtype), kind="ExternalInput").ap()
    result = nc.dram_tensor("out_0", (1, S, D), _mybir.dt.float32, kind="ExternalOutput").ap()
    build(nc, out=result, **args)
    r = _run(nc, [{"in_" + name: a for name, a in arrays.items()}], core_ids=[0])
    return r.results[0]["out_0"]
```
